# Optimizing a Trainium2 kernel written in Bass

```python
import jax, jax.numpy as jnp
from jax import lax
import numpy as np
import math

D_MODEL = 2048
BATCH = 1
SEQ = 256
DEPTH = 2

CHUNK = 64
N_MIXERS = 2
N_A = (DEPTH + N_MIXERS - 1) // N_MIXERS
N_B = DEPTH // N_MIXERS
NORM_EPS = 1e-6

SGU_BLOCK = 128
SGU_WIDTH = 2 * D_MODEL
SGU_GROUPS = 16
SGU_GROUP_DIM = SGU_WIDTH // SGU_GROUPS

MLA_HEADS = 16
Q_LORA_RANK = 448
KV_LORA_RANK = 512
QK_NOPE_DIM = 128
QK_ROPE_DIM = 64
V_HEAD_DIM = 128
MLA_WIDTH = MLA_HEADS * V_HEAD_DIM
ROPE_THETA = 10000.0
Q_BLOCK = 128


def rms_norm(x, g):
    xf = x.astype(jnp.float32)
    y = xf * lax.rsqrt(jnp.mean(xf * xf, axis=-1, keepdims=True) + NORM_EPS)
    return (y * g.astype(jnp.float32)).astype(x.dtype)

def layer_norm(x, g):
    xf = x.astype(jnp.float32)
    mu = jnp.mean(xf, axis=-1, keepdims=True)
    var = jnp.mean(jnp.square(xf - mu), axis=-1, keepdims=True)
    return ((xf - mu) * lax.rsqrt(var + NORM_EPS) * g.astype(jnp.float32)).astype(x.dtype)

def apply_rope(x, cos, sin):
    xf = x.astype(jnp.float32)
    x1, x2 = jnp.split(xf, 2, axis=-1)
    return jnp.concatenate([x1 * cos - x2 * sin, x1 * sin + x2 * cos], axis=-1).astype(x.dtype)

def sgu_mixer(h, w_in, norm_g, w_s, b_s, w_out):
    B, S, _ = h.shape
    u, v, z = jnp.split(h @ w_in, 3, axis=-1)
    u = jax.nn.gelu(u, approximate=False)
    v = layer_norm(jax.nn.gelu(v, approximate=False), norm_g)
    t_chunk = jnp.arange(SGU_BLOCK) // CHUNK
    mask = (t_chunk[None, :] <= t_chunk[:, None]).astype(w_s.dtype)
    w = w_s * mask[None]
    vb = v.reshape(B, S // SGU_BLOCK, SGU_BLOCK, SGU_GROUPS, SGU_GROUP_DIM)
    vm = jnp.einsum('gts,bnsgc->bntgc', w, vb) + b_s.T[:, :, None]
    y = u * vm.reshape(B, S, SGU_WIDTH) * jax.nn.silu(z)
    return y @ w_out

def chunk_causal_attention(q_nope, q_rope, k_nope, k_rope, v):
    B, S, H, _ = q_nope.shape
    nqb = S // Q_BLOCK
    scale = (QK_NOPE_DIM + QK_ROPE_DIM) ** -0.5
    k_chunk = jnp.arange(S) // CHUNK

    def to_blocks(t):
        return jnp.moveaxis(t.reshape(B, nqb, Q_BLOCK, *t.shape[2:]), 1, 0)

    def one_block(args):
        idx, qn, qr = args
        s = (jnp.einsum('bqhd,bkhd->bhqk', qn, k_nope)
             + jnp.einsum('bqhd,bkd->bhqk', qr, k_rope)).astype(jnp.float32) * scale
        q_chunk = (idx * Q_BLOCK + jnp.arange(Q_BLOCK)) // CHUNK
        mask = k_chunk[None, :] <= q_chunk[:, None]
        p = jax.nn.softmax(jnp.where(mask, s, -1e30), axis=-1).astype(v.dtype)
        return jnp.einsum('bhqk,bkhd->bqhd', p, v)

    out = lax.map(one_block, (jnp.arange(nqb), to_blocks(q_nope), to_blocks(q_rope)))
    return jnp.moveaxis(out, 0, 1).reshape(B, S, H, V_HEAD_DIM)

def mla_mixer(h, w_in, q_norm_g, kv_norm_g, w_uq, w_ukv, w_out):
    B, S, _ = h.shape
    o1 = Q_LORA_RANK
    o2 = o1 + KV_LORA_RANK
    o3 = o2 + QK_ROPE_DIM
    cq, ckv, k_rope, z = jnp.split(h @ w_in, [o1, o2, o3], axis=-1)
    q = (rms_norm(cq, q_norm_g) @ w_uq).reshape(B, S, MLA_HEADS, QK_NOPE_DIM + QK_ROPE_DIM)
    kv = (rms_norm(ckv, kv_norm_g) @ w_ukv).reshape(B, S, MLA_HEADS, QK_NOPE_DIM + V_HEAD_DIM)
    q_nope, q_rope = q[..., :QK_NOPE_DIM], q[..., QK_NOPE_DIM:]
    k_nope, v = kv[..., :QK_NOPE_DIM], kv[..., QK_NOPE_DIM:]
    pos = jnp.arange(S, dtype=jnp.float32)
    inv_freq = ROPE_THETA ** (-jnp.arange(0, QK_ROPE_DIM, 2, dtype=jnp.float32) / QK_ROPE_DIM)
    ang = pos[:, None] * inv_freq[None, :]
    cos, sin = jnp.cos(ang), jnp.sin(ang)
    q_rope = apply_rope(q_rope, cos[:, None, :], sin[:, None, :])
    k_rope = apply_rope(k_rope, cos, sin)
    o = chunk_causal_attention(q_nope, q_rope, k_nope, k_rope, v)
    y = o.reshape(B, S, MLA_WIDTH) * jax.nn.silu(z)
    return y @ w_out

def first_inputs(seed: int = 0) -> dict:
    key = jax.random.key(seed)
    ks = jax.random.split(key, 17)
    f32 = jnp.float32
    D = D_MODEL

    def nrm(k, shape, s):
        return jax.random.normal(k, shape, f32) * s

    def gain(k, shape):
        return 1.0 + 0.05 * jax.random.normal(k, shape, f32)

    mla_in_cols = Q_LORA_RANK + KV_LORA_RANK + QK_ROPE_DIM + MLA_WIDTH
    return {
        'x': nrm(ks[0], (BATCH, SEQ, D), 1.0),
        'c': nrm(ks[1], (BATCH, D), 1.0),
        'ada_w': nrm(ks[2], (DEPTH, D, 3 * D), 0.5 * D ** -0.5),
        'ada_b': nrm(ks[3], (DEPTH, 3 * D), 0.01),
        'pre_g': gain(ks[4], (DEPTH, D)),
        'post_g': gain(ks[5], (DEPTH, D)),
        'sgu_w_in': nrm(ks[6], (N_A, D, 3 * SGU_WIDTH), D ** -0.5),
        'sgu_norm_g': gain(ks[7], (N_A, SGU_WIDTH)),
        'sgu_w_s': nrm(ks[8], (N_A, SGU_GROUPS, SGU_BLOCK, SGU_BLOCK), SGU_BLOCK ** -0.5),
        'sgu_b_s': gain(ks[9], (N_A, SGU_GROUPS, SGU_BLOCK)),
        'sgu_w_out': nrm(ks[10], (N_A, SGU_WIDTH, D), SGU_WIDTH ** -0.5),
        'mla_w_in': nrm(ks[11], (N_B, D, mla_in_cols), D ** -0.5),
        'mla_q_norm_g': gain(ks[12], (N_B, Q_LORA_RANK)),
        'mla_kv_norm_g': gain(ks[13], (N_B, KV_LORA_RANK)),
        'mla_w_uq': nrm(ks[14], (N_B, Q_LORA_RANK, MLA_HEADS * (QK_NOPE_DIM + QK_ROPE_DIM)), Q_LORA_RANK ** -0.5),
        'mla_w_ukv': nrm(ks[15], (N_B, KV_LORA_RANK, MLA_HEADS * (QK_NOPE_DIM + V_HEAD_DIM)), KV_LORA_RANK ** -0.5),
        'mla_w_out': nrm(ks[16], (N_B, MLA_WIDTH, D), MLA_WIDTH ** -0.5),
    }

def first_block(x, c, ada_w, ada_b, pre_g, post_g, sgu_w_in, sgu_norm_g, sgu_w_s, sgu_b_s, sgu_w_out,
              mla_w_in, mla_q_norm_g, mla_kv_norm_g, mla_w_uq, mla_w_ukv, mla_w_out):
    cond = jax.nn.silu(c)
    for i in range(DEPTH):
        mod = cond @ ada_w[i] + ada_b[i]
        shift, scale, gate = jnp.split(mod, 3, axis=-1)
        h = rms_norm(x, pre_g[i]) * (1 + scale[:, None, :]) + shift[:, None, :]
        j = i // N_MIXERS
        if i % N_MIXERS == 0:
            y = sgu_mixer(h, sgu_w_in[j], sgu_norm_g[j], sgu_w_s[j], sgu_b_s[j], sgu_w_out[j])
        else:
            y = mla_mixer(h, mla_w_in[j], mla_q_norm_g[j], mla_kv_norm_g[j], mla_w_uq[j], mla_w_ukv[j], mla_w_out[j])
        x = x + gate[:, None, :] * rms_norm(y, post_g[i])
    return x


N_MIXERS_2 = 3
HEAD_DIM = 64
ROPE_DIM = HEAD_DIM // 4
ROPE_THETA_2 = 500000.0
NORM_EPS_2 = 1e-5

A_HEADS = D_MODEL // HEAD_DIM
A_KV_HEADS = A_HEADS // 8
A_GROUP = A_HEADS // A_KV_HEADS
A_WIDTH = A_HEADS * HEAD_DIM
A_KV_WIDTH = A_KV_HEADS * HEAD_DIM
A_IN = 2 * A_WIDTH + 2 * A_KV_WIDTH
A_WINDOW = 128
A_QBLOCK = 128

B_HEADS = D_MODEL // HEAD_DIM
B_KV_GROUPS = 4
B_GROUP = B_HEADS // B_KV_GROUPS
B_WIDTH = B_HEADS * HEAD_DIM
B_KV_WIDTH = B_KV_GROUPS * HEAD_DIM
B_N_BRANCH = 3
B_IN = 2 * B_WIDTH + 6 * B_KV_WIDTH + B_N_BRANCH * B_HEADS
CMP_BLOCK = 32
CMP_STRIDE = 16
CMP_HIDDEN = 4 * HEAD_DIM
SLC_BLOCK = 64
SLC_TOPK = 16
B_WINDOW = 512
B_QBLOCK = 64
WIN_QBLOCK = 128

C_WIDTH = D_MODEL
C_IN = 4 * C_WIDTH
CONV_WIDTH = 3

N_A_2 = (DEPTH + 2) // N_MIXERS_2
N_B_2 = (DEPTH + 1) // N_MIXERS_2
N_C = DEPTH // N_MIXERS_2


def rmsnorm(x, g):
    xf = x.astype(jnp.float32)
    y = xf * lax.rsqrt(jnp.mean(xf * xf, axis=-1, keepdims=True) + NORM_EPS_2)
    return (y * g.astype(jnp.float32)).astype(x.dtype)

def rope_tables(positions):
    inv_freq = ROPE_THETA_2 ** (-jnp.arange(0, ROPE_DIM, 2, dtype=jnp.float32) / ROPE_DIM)
    ang = positions.astype(jnp.float32)[..., None] * inv_freq
    return jnp.cos(ang)[:, :, None, :], jnp.sin(ang)[:, :, None, :]

def apply_rope_2(x, cos, sin):
    half = ROPE_DIM // 2
    x1 = x[..., :half].astype(jnp.float32)
    x2 = x[..., half:ROPE_DIM].astype(jnp.float32)
    r1 = x1 * cos - x2 * sin
    r2 = x2 * cos + x1 * sin
    return jnp.concatenate([r1.astype(x.dtype), r2.astype(x.dtype), x[..., ROPE_DIM:]], axis=-1)

def banded_attention(q, k, v, window, qblock, sinks=None):
    Bn, S, G, Hg, hd = q.shape
    nqb = S // qblock
    span = window + qblock
    scale = hd ** -0.5
    k_pad = jnp.pad(k, ((0, 0), (window, 0), (0, 0), (0, 0)))
    v_pad = jnp.pad(v, ((0, 0), (window, 0), (0, 0), (0, 0)))
    q_blocks = q.reshape(Bn, nqb, qblock, G, Hg, hd).swapaxes(0, 1)
    starts = jnp.arange(nqb, dtype=jnp.int32) * qblock
    rel = jnp.arange(qblock)[:, None] - jnp.arange(span)[None, :] + window
    band = (rel >= 0) & (rel < window)

    def step(args):
        qb, s0 = args
        kb = lax.dynamic_slice_in_dim(k_pad, s0, span, axis=1).astype(jnp.float32)
        vb = lax.dynamic_slice_in_dim(v_pad, s0, span, axis=1).astype(jnp.float32)
        s = jnp.einsum('bqghd,bkgd->bghqk', qb.astype(jnp.float32), kb) * scale
        valid = band & ((s0 - window + jnp.arange(span)) >= 0)[None, :]
        s = jnp.where(valid, s, -jnp.inf)
        if sinks is None:
            p = jax.nn.softmax(s, axis=-1)
        else:
            sk = sinks.astype(jnp.float32)[None, :, :, None, None]
            m = jnp.maximum(jnp.max(s, axis=-1, keepdims=True), sk)
            e = jnp.exp(s - m)
            p = e / (jnp.sum(e, axis=-1, keepdims=True) + jnp.exp(sk - m))
        o = jnp.einsum('bghqk,bkgd->bqghd', p, vb)
        return o.astype(q.dtype)

    o = lax.map(step, (q_blocks, starts))
    return o.swapaxes(0, 1).reshape(Bn, S, G, Hg, hd)

def mixer_a(h, w_in, sinks, w_out, cos, sin):
    Bn, S, _ = h.shape
    proj = h @ w_in
    q, k, v, z = jnp.split(proj, [A_WIDTH, A_WIDTH + A_KV_WIDTH, A_WIDTH + 2 * A_KV_WIDTH], axis=-1)
    q = apply_rope_2(q.reshape(Bn, S, A_HEADS, HEAD_DIM), cos, sin).reshape(Bn, S, A_KV_HEADS, A_GROUP, HEAD_DIM)
    k = apply_rope_2(k.reshape(Bn, S, A_KV_HEADS, HEAD_DIM), cos, sin)
    v = v.reshape(Bn, S, A_KV_HEADS, HEAD_DIM)
    o = banded_attention(q, k, v, A_WINDOW, A_QBLOCK, sinks.reshape(A_KV_HEADS, A_GROUP))
    o = o.reshape(Bn, S, A_WIDTH)
    return (o * jax.nn.silu(z)) @ w_out

def compress(k, pos, w1, w2):
    Bn, S, G, hd = k.shape
    nc = (S - CMP_BLOCK) // CMP_STRIDE + 1
    idx = np.arange(nc)[:, None] * CMP_STRIDE + np.arange(CMP_BLOCK)[None, :]
    blocks = k[:, idx] + pos[None, None, :, None, :]
    blocks = jnp.moveaxis(blocks, 3, 2).reshape(Bn, nc, G, CMP_BLOCK * hd)
    return jax.nn.gelu(blocks @ w1) @ w2

def nsa_cmp_slc(q, kcmp, vcmp, ks, vs):
    Bn, S, G, Hg, hd = q.shape
    nc = kcmp.shape[1]
    nsel = S // SLC_BLOCK
    n_top = min(SLC_TOPK, nsel)
    nqb = S // B_QBLOCK
    scale = hd ** -0.5
    c_start = np.arange(nc) * CMP_STRIDE
    c_end = c_start + CMP_BLOCK
    s_start = np.arange(nsel) * SLC_BLOCK
    s_end = s_start + SLC_BLOCK
    overlap = np.clip(np.minimum(c_end[:, None], s_end[None, :]) - np.maximum(c_start[:, None], s_start[None, :]), 0, None)
    overlap = jnp.asarray(overlap / CMP_BLOCK, jnp.float32)
    c_last = jnp.asarray(c_end - 1, jnp.int32)
    kcmp_f = kcmp.astype(jnp.float32)
    vcmp_f = vcmp.astype(jnp.float32)
    ks_blk = ks.reshape(Bn, nsel, SLC_BLOCK, G, hd).transpose(0, 1, 3, 2, 4)
    vs_blk = vs.reshape(Bn, nsel, SLC_BLOCK, G, hd).transpose(0, 1, 3, 2, 4)
    q_blocks = q.reshape(Bn, nqb, B_QBLOCK, G, Hg, hd).swapaxes(0, 1)
    starts = jnp.arange(nqb, dtype=jnp.int32) * B_QBLOCK
    bi = jnp.arange(Bn)[:, None, None, None]
    gi = jnp.arange(G)[None, None, :, None]
    blk = jnp.arange(nsel)

    def step(args):
        qb, s0 = args
        t = s0 + jnp.arange(B_QBLOCK)
        qf = qb.astype(jnp.float32)
        sc = jnp.einsum('bqghd,bcgd->bghqc', qf, kcmp_f) * scale
        sc = jnp.where(c_last[None, :] <= t[:, None], sc, -jnp.inf)
        m = jnp.max(sc, axis=-1, keepdims=True)
        m = jnp.where(jnp.isfinite(m), m, 0.0)
        e = jnp.exp(sc - m)
        p_cmp = e / jnp.maximum(jnp.sum(e, axis=-1, keepdims=True), 1e-30)
        o_cmp = jnp.einsum('bghqc,bcgd->bqghd', p_cmp, vcmp_f)
        imp = jnp.einsum('bghqc,cn->bgqn', p_cmp, overlap)
        cur = t // SLC_BLOCK
        forced = (blk[None, :] == 0) | (blk[None, :] == cur[:, None]) | (blk[None, :] == cur[:, None] - 1)
        future = blk[None, :] * SLC_BLOCK > t[:, None]
        imp = jnp.where(forced, jnp.inf, imp)
        imp = jnp.where(future, -jnp.inf, imp)
        _, sel = lax.top_k(imp, n_top)
        sel = sel.transpose(0, 2, 1, 3)
        kg = ks_blk[bi, sel, gi].astype(jnp.float32)
        vg = vs_blk[bi, sel, gi].astype(jnp.float32)
        ss = jnp.einsum('bqghd,bqgnld->bghqnl', qf, kg) * scale
        kpos = sel[..., None] * SLC_BLOCK + jnp.arange(SLC_BLOCK)
        valid = (kpos <= t[None, :, None, None, None]).transpose(0, 2, 1, 3, 4)[:, :, None]
        ss = jnp.where(valid, ss, -jnp.inf)
        shp = ss.shape
        p_slc = jax.nn.softmax(ss.reshape(shp[:4] + (n_top * SLC_BLOCK,)), axis=-1).reshape(shp)
        o_slc = jnp.einsum('bghqnl,bqgnld->bqghd', p_slc, vg)
        return o_cmp.astype(q.dtype), o_slc.astype(q.dtype)

    o_cmp, o_slc = lax.map(step, (q_blocks, starts))
    o_cmp = o_cmp.swapaxes(0, 1).reshape(Bn, S, G, Hg, hd)
    o_slc = o_slc.swapaxes(0, 1).reshape(Bn, S, G, Hg, hd)
    return o_cmp, o_slc

def mixer_b(h, w_in, kc_pos, kc_w1, kc_w2, vc_pos, vc_w1, vc_w2, w_out, cos, sin):
    Bn, S, _ = h.shape
    proj = h @ w_in
    cuts = [B_WIDTH + i * B_KV_WIDTH for i in range(7)] + [B_WIDTH + 6 * B_KV_WIDTH + B_N_BRANCH * B_HEADS]
    q, kc, vc, ks, vs, kw, vw, gates, z = jnp.split(proj, cuts, axis=-1)
    q = apply_rope_2(q.reshape(Bn, S, B_HEADS, HEAD_DIM), cos, sin).reshape(Bn, S, B_KV_GROUPS, B_GROUP, HEAD_DIM)
    kv_shape = (Bn, S, B_KV_GROUPS, HEAD_DIM)
    ks = apply_rope_2(ks.reshape(kv_shape), cos, sin)
    kw = apply_rope_2(kw.reshape(kv_shape), cos, sin)
    kcmp = compress(kc.reshape(kv_shape), kc_pos, kc_w1, kc_w2)
    vcmp = compress(vc.reshape(kv_shape), vc_pos, vc_w1, vc_w2)
    o_cmp, o_slc = nsa_cmp_slc(q, kcmp, vcmp, ks, vs.reshape(kv_shape))
    o_win = banded_attention(q, kw, vw.reshape(kv_shape), B_WINDOW, WIN_QBLOCK)
    g = jax.nn.sigmoid(gates.astype(jnp.float32)).reshape(Bn, S, B_N_BRANCH, B_KV_GROUPS, B_GROUP, 1)
    o = (g[:, :, 0] * o_cmp.astype(jnp.float32) + g[:, :, 1] * o_slc.astype(jnp.float32)
         + g[:, :, 2] * o_win.astype(jnp.float32)).astype(h.dtype)
    o = o.reshape(Bn, S, B_WIDTH)
    return (o * jax.nn.silu(z)) @ w_out

def mixer_c(h, w_in, conv_w, w_out):
    u, b_gate, c_gate, z = jnp.split(h @ w_in, 4, axis=-1)
    v = c_gate * u
    y = lax.conv_general_dilated(v, conv_w[:, None, :], window_strides=(1,), padding=[(CONV_WIDTH - 1, 0)],
                                 dimension_numbers=('NWC', 'WIO', 'NWC'), feature_group_count=C_WIDTH)
    y = b_gate * y
    return (y * jax.nn.silu(z)) @ w_out

def second_inputs(seed: int = 0) -> dict:
    key = jax.random.key(seed)
    ks = jax.random.split(key, 20)

    def dense(k, shape, fan_in):
        return jax.random.normal(k, shape, jnp.float32) * fan_in ** -0.5

    x = jax.random.normal(ks[0], (BATCH, SEQ, D_MODEL), jnp.float32)
    positions = (jnp.arange(SEQ, dtype=jnp.int32)[None, :]
                 + jax.random.randint(ks[1], (BATCH, 1), 0, 1024, dtype=jnp.int32))
    norm_w = 1.0 + 0.02 * jax.random.normal(ks[2], (DEPTH, D_MODEL), jnp.float32)
    final_norm_w = 1.0 + 0.02 * jax.random.normal(ks[3], (D_MODEL,), jnp.float32)
    a_w_in = dense(ks[4], (N_A_2, D_MODEL, A_IN), D_MODEL)
    a_sinks = jax.random.normal(ks[5], (N_A_2, A_HEADS), jnp.float32)
    a_w_out = dense(ks[6], (N_A_2, A_WIDTH, D_MODEL), A_WIDTH)
    b_w_in = dense(ks[7], (N_B_2, D_MODEL, B_IN), D_MODEL)
    b_cmp_k_pos = 0.1 * jax.random.normal(ks[8], (N_B_2, CMP_BLOCK, HEAD_DIM), jnp.float32)
    b_cmp_k_w1 = dense(ks[9], (N_B_2, CMP_BLOCK * HEAD_DIM, CMP_HIDDEN), CMP_BLOCK * HEAD_DIM)
    b_cmp_k_w2 = dense(ks[10], (N_B_2, CMP_HIDDEN, HEAD_DIM), CMP_HIDDEN)
    b_cmp_v_pos = 0.1 * jax.random.normal(ks[11], (N_B_2, CMP_BLOCK, HEAD_DIM), jnp.float32)
    b_cmp_v_w1 = dense(ks[12], (N_B_2, CMP_BLOCK * HEAD_DIM, CMP_HIDDEN), CMP_BLOCK * HEAD_DIM)
    b_cmp_v_w2 = dense(ks[13], (N_B_2, CMP_HIDDEN, HEAD_DIM), CMP_HIDDEN)
    b_w_out = dense(ks[14], (N_B_2, B_WIDTH, D_MODEL), B_WIDTH)
    c_w_in = dense(ks[15], (N_C, D_MODEL, C_IN), D_MODEL)
    c_conv_w = dense(ks[16], (N_C, CONV_WIDTH, C_WIDTH), CONV_WIDTH)
    c_w_out = dense(ks[17], (N_C, C_WIDTH, D_MODEL), C_WIDTH)
    return {"x": x, "positions": positions, "norm_w": norm_w, "final_norm_w": final_norm_w,
            "a_w_in": a_w_in, "a_sinks": a_sinks, "a_w_out": a_w_out,
            "b_w_in": b_w_in, "b_cmp_k_pos": b_cmp_k_pos, "b_cmp_k_w1": b_cmp_k_w1, "b_cmp_k_w2": b_cmp_k_w2,
            "b_cmp_v_pos": b_cmp_v_pos, "b_cmp_v_w1": b_cmp_v_w1, "b_cmp_v_w2": b_cmp_v_w2, "b_w_out": b_w_out,
            "c_w_in": c_w_in, "c_conv_w": c_conv_w, "c_w_out": c_w_out}

def second_block(x, positions, norm_w, final_norm_w, a_w_in, a_sinks, a_w_out,
              b_w_in, b_cmp_k_pos, b_cmp_k_w1, b_cmp_k_w2, b_cmp_v_pos, b_cmp_v_w1, b_cmp_v_w2, b_w_out,
              c_w_in, c_conv_w, c_w_out):
    cos, sin = rope_tables(positions)
    for i in range(DEPTH):
        h = rmsnorm(x, norm_w[i])
        kind, j = i % N_MIXERS_2, i // N_MIXERS_2
        if kind == 0:
            out = mixer_a(h, a_w_in[j], a_sinks[j], a_w_out[j], cos, sin)
        elif kind == 1:
            out = mixer_b(h, b_w_in[j], b_cmp_k_pos[j], b_cmp_k_w1[j], b_cmp_k_w2[j],
                          b_cmp_v_pos[j], b_cmp_v_w1[j], b_cmp_v_w2[j], b_w_out[j], cos, sin)
        else:
            out = mixer_c(h, c_w_in[j], c_conv_w[j], c_w_out[j])
        x = x + out.astype(x.dtype)
    return rmsnorm(x, final_norm_w)


def setup_inputs(seed=0):
    out = dict(first_inputs(seed))
    for name, value in second_inputs(seed + 1).items():
        if name != "x":
            out[name + "_2"] = value
    return out


def reference(
    x, c, ada_w, ada_b, pre_g, post_g, sgu_w_in, sgu_norm_g, sgu_w_s, sgu_b_s, sgu_w_out,
    mla_w_in, mla_q_norm_g, mla_kv_norm_g, mla_w_uq, mla_w_ukv, mla_w_out, positions_2,
    norm_w_2, final_norm_w_2, a_w_in_2, a_sinks_2, a_w_out_2, b_w_in_2, b_cmp_k_pos_2,
    b_cmp_k_w1_2, b_cmp_k_w2_2, b_cmp_v_pos_2, b_cmp_v_w1_2, b_cmp_v_w2_2, b_w_out_2, c_w_in_2,
    c_conv_w_2, c_w_out_2,
):
    x = first_block(
        x, c, ada_w, ada_b, pre_g, post_g, sgu_w_in, sgu_norm_g, sgu_w_s, sgu_b_s, sgu_w_out,
        mla_w_in, mla_q_norm_g, mla_kv_norm_g, mla_w_uq, mla_w_ukv, mla_w_out,
    )
    return second_block(
        x, positions_2, norm_w_2, final_norm_w_2, a_w_in_2, a_sinks_2, a_w_out_2, b_w_in_2,
        b_cmp_k_pos_2, b_cmp_k_w1_2, b_cmp_k_w2_2, b_cmp_v_pos_2, b_cmp_v_w1_2, b_cmp_v_w2_2,
        b_w_out_2, c_w_in_2, c_conv_w_2, c_w_out_2,
    )


_drawn_inputs = setup_inputs


def setup_inputs(seed=0):
    import zlib

    import numpy as np

    out = dict(_drawn_inputs(seed))
    spreads = {}
    factors = {'ada_b': 2.928,
     'sgu_norm_g': 5.804,
     'sgu_b_s': 4.799,
     'mla_q_norm_g': 8.0,
     'mla_kv_norm_g': 3.65,
     'norm_w_2': 8.0,
     'final_norm_w_2': 7.806,
     'a_sinks_2': 4.903,
     'b_cmp_k_pos_2': 8.0,
     'b_cmp_v_pos_2': 16.032}
    for name, (base, spread) in spreads.items():
        noise = np.random.default_rng([zlib.crc32(name.encode()), seed]).standard_normal(out[name].shape)
        drawn = base * np.exp(spread * noise) if base else spread * noise
        out[name] = __import__('jax').numpy.asarray(drawn.astype(out[name].dtype))
    for name, factor in factors.items():
        out[name] = (out[name] * factor).astype(out[name].dtype)
    return out
```

```python
from contextlib import ExitStack

import numpy as np

import concourse.bass as bass
from concourse import mybir
from concourse.alu_op_type import AluOpType as ALU

F32 = mybir.dt.float32
I32 = mybir.dt.int32
ACT = mybir.ActivationFunctionType
AX = mybir.AxisListType.X
ds = bass.ds

P = 128
S = 256
TB = S // P
D = 2048
KT = D // P
NB = 512
CHUNK_KT = 4
RING = 4
CPB = KT // CHUNK_KT
SGU_W = 2 * D
SGU_G = 16
SGU_GD = SGU_W // SGU_G
GPB = NB // SGU_GD
EPS1, EPS2 = 1e-6, 1e-5
MLA_H, QL, KVL, NOPE, ROPE, VH = 16, 448, 512, 128, 64, 128
QKD = NOPE + ROPE
MLA_SCALE = float(QKD) ** -0.5
QL_P = QL // 4
HPP = 2
HD = 64
NKV = 4
HG = 8
HW = HG * HD
RD = 8
SCALE2 = float(HD) ** -0.5
NCMP = (S - 32) // 16 + 1
CL, CS, CH = 32, 16, 256
ADA_C = 1024
NEG = -1e30
SCW = 3 * P
STAGES = 5

CONST_COLS = {"ident": P,  "mask_chunk": SCW, "mask_causal": SCW, "mask_window": SCW,
              "mask_cmp": TB * NCMP, "mask_sgu": P, "cos": TB * 32, "sin": TB * 32,
              "spread": HG * NCMP, "mask_bd": HW, "inv_freq": RD}
VEC_COLS = {"c": KT, "pre_g0": KT, "pre_g1": KT, "norm_w0": KT, "norm_w1": KT,
            "q_g": 4, "kv_g": 4, "b_s": SGU_G, "w_s": SGU_G * P, "pos_k": CL, "pos_v": CL}


def offsets(cols):
    at, out = 0, {}
    for name, n in cols.items():
        out[name] = (at, n)
        at += n
    return out, at


CONST_AT, CONST_N = offsets(CONST_COLS)
VEC_AT, VEC_N = offsets(VEC_COLS)


def shape_constants():
    q, k = np.arange(P)[:, None], np.arange(P)[None, :]
    f = np.float32
    add = lambda ok: np.where(ok, 0.0, NEG).astype(f)
    zero = np.zeros((P, P), f)
    chunk = add(k // 64 <= q // 64)
    causal = add(k <= q)
    out = {"ident": np.eye(P, dtype=f),
           "mask_chunk": np.concatenate([chunk, zero, chunk], 1),
           "mask_causal": np.concatenate([causal, zero, causal], 1),
           "mask_window": np.concatenate([causal, add(k > q), causal], 1),
           "mask_sgu": (q // 64 <= k // 64).astype(f)}
    tok = np.arange(S).reshape(TB, P).T[:, :, None]
    last = np.arange(NCMP) * CS + CL - 1
    out["mask_cmp"] = add(last[None, None, :] <= tok).reshape(P, -1)
    inv = (f(10000.0) ** (-np.arange(0, ROPE, 2, dtype=f) / f(ROPE))).astype(f)
    ang = tok.astype(f) * inv[None, None, :]
    out["cos"] = np.cos(ang).reshape(P, -1)
    out["sin"] = np.sin(ang).reshape(P, -1)
    n, hn = np.arange(P)[:, None], np.arange(HG * NCMP)[None, :]
    out["spread"] = (n == hn % NCMP).astype(f)
    out["mask_bd"] = (n // NCMP == np.arange(HW)[None, :] // HD).astype(f)
    inv2 = (f(500000.0) ** (-np.arange(0, 2 * RD, 2, dtype=f) / f(2 * RD))).astype(f)
    out["inv_freq"] = np.broadcast_to(inv2, (P, RD))
    return np.ascontiguousarray(np.concatenate([out[n] for n in CONST_COLS], 1).astype(f))


def build(nc, T, stages=STAGES):
    es = ExitStack()
    with es:
        def sb(name, cols, dt=F32):
            return es.enter_context(nc.sbuf_tensor(name, [P, cols], dt))

        def sem(name):
            return es.enter_context(nc.semaphore(name))

        reg_a = sb("reg_a", 2 * TB * D)
        reg_b = sb("reg_b", 2 * TB * D)
        reg_h = sb("reg_h", KT * S)
        reg_w = sb("reg_w", RING * CHUNK_KT * NB)
        reg_c = sb("reg_c", 10240)
        reg_d = sb("reg_d", 5120)
        cst_sb = sb("cst_sb", CONST_N)
        vec_sb = sb("vec_sb", VEC_N)
        small = sb("small", 640)
        ps = es.enter_context(nc.psum_tensor("ps", [P, 8, NB], F32))

        x_sb = reg_a[:, 0:TB * D].rearrange("p (t n) -> p t n", t=TB)
        y_sb = reg_a[:, TB * D:].rearrange("p (t n) -> p t n", t=TB)
        v_sb = reg_a[:, :].rearrange("p (t n) -> p t n", t=TB)
        yT = reg_b[:, :].rearrange("p (k s) -> p k s", s=S)
        oT = reg_b[:, 0:KT * S].rearrange("p (k s) -> p k s", s=S)
        z_sb = reg_b[:, KT * S:].rearrange("p (t n) -> p t n", t=TB)
        hT = reg_h[:, :].rearrange("p (k s) -> p k s", s=S)
        ring = reg_w[:, :].rearrange("p (r k n) -> p r k n", r=RING, k=CHUNK_KT)
        ada_buf = reg_c[:, 0:4 * ADA_C].rearrange("p (j n) -> p j n", j=4)
        ada_acc = reg_c[:, 4096:8192]
        gate_g = reg_c[:, 8192:10240]

        def cst(name, lo=0, n=None):
            at, w = CONST_AT[name]
            return cst_sb[:, at + lo:at + lo + (w - lo if n is None else n)]

        def vec(name, lo=0, n=None):
            at, w = VEC_AT[name]
            return vec_sb[:, at + lo:at + lo + (w - lo if n is None else n)]

        small_at = [0]

        def sm(n):
            small_at[0] += n
            assert small_at[0] <= 640
            return small[:, small_at[0] - n:small_at[0]]

        ident = cst("ident")
        cond = sm(KT)
        wait_cell = sm(1)
        aff_a = sm(KT)
        aff_b = sm(KT)
        sumsq = sm(TB)
        rms = sm(2 * TB)
        rstd = sm(2 * TB)
        ysq = sm(TB * 4)
        bn_mv = sm(TB * 2)
        last_gain = reg_h[:, 0:D]
        ones = sb("ones", P)

        u_t = reg_d[:, 0:1024].rearrange("p (t n) -> p t n", t=TB)
        z_t = reg_d[:, 1024:2048].rearrange("p (t n) -> p t n", t=TB)
        y_t = reg_d[:, 2048:3072].rearrange("p (t n) -> p t n", t=TB)
        g_blk = reg_d[:, 3072:3584]
        w_cur = reg_d[:, 3584:3840].rearrange("p (g n) -> p g n", g=GPB)
        b_cur = sm(GPB)
        sq_junk = reg_d[:, 4096:4608]
        bn_st = reg_d[:, 3840:3840 + TB * 8 * 6].rearrange("p (t n c) -> p t n c", t=TB, c=6)

        craw = reg_c[:, 0:2048].rearrange("p (t n) -> p t n", t=TB)
        cqT = reg_c[:, 2048:3072].rearrange("p (k s) -> p k s", s=S)
        ckvT = reg_c[:, 3072:4096].rearrange("p (k s) -> p k s", s=S)
        pool_at = {"c": [4096, 8192], "d": [0, 5120]}

        def take(n, reg=None):
            for key, r_ in (("c", reg_c), ("d", reg_d)):
                lo, hi = pool_at[key]
                if lo + n <= hi and reg in (None, key):
                    pool_at[key][0] += n
                    return r_[:, lo:lo + n]
            raise ValueError("scratch")

        rope_t = [take(TB * HPP * 32, "d") for _ in range(4)]
        krT = take(S)
        q_sb = [take(TB * HPP * QKD).rearrange("p (t n) -> p t n", t=TB) for _ in range(2)]
        kv_sb = [take(TB * NB).rearrange("p (t n) -> p t n", t=TB) for _ in range(2)]
        qT = take(HPP * S).rearrange("p (h s) -> p h s", h=HPP)
        qrT = take(HPP * S).rearrange("p (h s) -> p h s", h=HPP)
        kT = take(HPP * S).rearrange("p (h s) -> p h s", h=HPP)
        prob = [take(SCW) for _ in range(HPP)]
        probT = [take(SCW) for _ in range(HPP)]
        og = take(TB * HPP * VH).rearrange("p (t n) -> p t n", t=TB)
        c_sq = sm(2 * TB)
        mx = sm(HPP * TB)
        nmx = sm(HPP * TB)
        sums = sm(HPP * TB)
        rinv = sm(HPP * TB)

        cols = lambda reg, lo, n: reg[:, lo:lo + n]
        tn = lambda ap: ap.rearrange("p (t n) -> p t n", t=TB)
        raw = [tn(cols(reg_c, m * 1024, 1024)) for m in range(3)]
        kT_all = [cols(reg_c, 3072 + m * 1024, 1024).rearrange("p (g s) -> p g s", g=NKV) for m in range(2)]
        q_grp = tn(cols(reg_c, 5120, 1024))
        qT_grp = cols(reg_c, 6144, 1024).rearrange("p (j s) -> p j s", j=4)
        o_grp = tn(cols(reg_c, 7168, 1024))
        prob4 = [cols(reg_c, 8192 + m * SCW, SCW) for m in range(4)]
        kT_grp = [cols(reg_c, 9728 + m * S, S) for m in range(2)]
        probT2 = [cols(reg_d, m * SCW, SCW) for m in range(2)]
        o_tmp = tn(cols(reg_d, 768, 1024))
        rope2_t = [cols(reg_d, 1792 + m * 128, 128) for m in range(4)]
        p_cmp = cols(reg_d, 2304, TB * HG * NCMP)
        pT_cmp = cols(reg_d, 2544, S).rearrange("p (t n) -> p t n", t=TB)
        v_bd = cols(reg_d, 2800, HW)
        gates = tn(cols(reg_d, 3312, TB * 96))
        kcmp_all = cols(reg_d, 3504, NKV * NCMP)
        kcmp_grp = cols(reg_d, 3564, NCMP)
        vcmp = cols(reg_d, 3580, NKV * HD)
        w2k = cols(reg_d, 4608, 256).rearrange("p (k n) -> p k n", k=2)
        w2v = cols(reg_d, 4864, 128).rearrange("p (k n) -> p k n", k=2)
        hidT = cols(reg_d, 4992, 120).rearrange("p (k n) -> p k n", k=2)
        k_dup = [tn(cols(reg_c, 5120 + m * 1024, 1024)) for m in range(2)]
        kcT = [cols(r_, lo, 1024).rearrange("p (g s) -> p g s", g=NKV) for r_, lo in ((reg_c, 7168), (reg_d, 768))]
        unfold = cols(reg_c, 8192, CL * NKV * NCMP).rearrange("p (l g n) -> p l g n", l=CL, g=NKV)
        pos_i = es.enter_context(nc.sbuf_tensor("pos_i", [P, TB], I32))
        pos_f = sm(TB)
        ang = sm(TB * RD)
        red = sm(TB * RD)
        turns = sm(TB * RD)
        cos2 = sm(TB * RD)
        sin2 = sm(TB * RD)
        sinks = sm(NKV * HG)
        sink_grp = sm(HG)
        sink_e = sm(TB * HG)
        mx2 = sm(TB * HG)
        nmx2 = sm(TB * HG)
        sums2 = [sm(TB * HG) for _ in range(3)]
        coef = sm(TB * HG)
        t8 = lambda ap: ap.rearrange("p (t h) -> p t h", t=TB)

        consts_in = sem("consts_in")
        x_in = sem("x_in")
        x_back = sem("x_back")
        ones_set = sem("ones_set")
        cond_done = sem("cond_done")
        w_full = [sem(f"w_full{s}") for s in range(RING)]
        w_used = sem("w_used")
        proj_free = sem("proj_free")
        ada_full = [sem(f"ada_full{j}") for j in range(4)]
        ada_used = sem("ada_used")
        acc_zero = sem("acc_zero")
        acc_init = sem("acc_init")
        cols_done = sem("cols_done")
        aff_ready = sem("aff_ready")
        gate_rows = sem("gate_rows")
        gate_read = sem("gate_read")
        gate_ready = sem("gate_ready")
        postg_in = sem("postg_in")
        dve_step = sem("dve_step")
        act_step = sem("act_step")
        x_ready = sem("x_ready")
        ssq_done = sem("ssq_done")
        ms_done = sem("ms_done")
        rms_done = sem("rms_done")
        xn_done = sem("xn_done")
        xT_done = sem("xT_done")
        xT_free = [sem("xT_free_act"), sem("xT_free_dve")]
        out_in = sem("out_in")
        gain_in = sem("gain_in")
        v_norm = sem("v_norm")
        vstat_done = sem("vstat_done")
        g_in = sem("g_in")
        wcur_done = sem("wcur_done")
        mix_done = sem("mix_done")
        y_done = sem("y_done")
        yt_done = sem("yt_done")
        yT_done = sem("yT_done")
        craw_done = sem("craw_done")
        c_ssq = sem("c_ssq")
        c_normed = sem("c_normed")
        cT_turned = sem("cT_turned")
        cT_act = sem("cT_act")
        cT_dve = sem("cT_dve")
        q_roped = sem("q_roped")
        turned_q = sem("turned_q")
        turned_k = sem("turned_k")
        turned_r = sem("turned_r")
        qT_copied = sem("qT_copied")
        kT_copied = sem("kT_copied")
        scores_done = sem("scores_done")
        max_done = sem("max_done")
        exp_done = sem("exp_done")
        pt_done = sem("pt_done")
        ptc_act = sem("ptc_act")
        ptc_dve = sem("ptc_dve")
        pv_done = sem("pv_done")
        og_done = sem("og_done")
        ogt_done = sem("ogt_done")
        ogc_done = sem("ogc_done")
        pos_in = sem("pos_in")
        trig_in = sem("trig_in")
        trig_done = sem("trig_done")
        sinks_in = sem("sinks_in")
        w2_in = sem("w2_in")

        class Mixer:

            def __init__(self, name, branches):
                self.name, self.branches, self.units = name, branches, branches * HG
                self.reads = branches + (name == "b")
                self.kdup = sem(f"{name}_kdup")
                self.k_turned = sem(f"{name}_k_turned")
                self.kT_act = sem(f"{name}_kT_act")
                self.kT_dve = sem(f"{name}_kT_dve")
                self.q_roped = sem(f"{name}_q_roped")
                self.turned = sem(f"{name}_turned")
                self.qT_act = sem(f"{name}_qT_act")
                self.qT_dve = sem(f"{name}_qT_dve")
                self.k_ready = sem(f"{name}_k_ready")
                self.scores = sem(f"{name}_scores")
                self.max_done = sem(f"{name}_max_done")
                self.exp_done = sem(f"{name}_exp_done")
                self.pt_done = sem(f"{name}_pt_done")
                self.ptc_act = sem(f"{name}_ptc_act")
                self.ptc_dve = sem(f"{name}_ptc_dve")
                self.pv_done = sem(f"{name}_pv_done")
                self.o_read = sem(f"{name}_o_read")
                self.og_done = sem(f"{name}_og_done")
                self.ogt_done = sem(f"{name}_ogt_done")
                self.ogc_act = sem(f"{name}_ogc_act")
                self.ogc_dve = sem(f"{name}_ogc_dve")
                self.sink_in = sem(f"{name}_sink_in")
                self.sink_exp = sem(f"{name}_sink_exp")

        ma = mb = None
        if stages >= 3:
            ma = Mixer("a", 1)
        if stages >= 4:
            mb = Mixer("b", 2)
        cmp_scores = sem("cmp_scores")
        cmp_shifted = sem("cmp_shifted")
        cmp_exp = sem("cmp_exp")
        cmp_turned = sem("cmp_turned")
        cmp_copied = sem("cmp_copied")
        vbd_done = sem("vbd_done")
        cmp_pv = sem("cmp_pv")
        c_turned = sem("c_turned")
        c_copied = sem("c_copied")
        unfolded = sem("unfolded")
        hid_done = sem("hid_done")
        gelu_done = sem("gelu_done")
        cmp_w2 = sem("cmp_w2")
        cmp_kv = sem("cmp_kv")
        gates_done = sem("gates_done")
        ysq_done = sem("ysq_done")

        chunk_base, block_base, chunks_per = {}, {}, {}
        c_at = b_at = 0
        for name, blocks, chunks in (
                ("sgu_v", 8, CPB), ("sgu_uz", 16, CPB), ("sgu_out", 4, 2 * CPB),
                ("mla_in", 6, CPB), ("mla_heads", 16, 1), ("mla_out", 4, CPB),
                ("a_kvz", 5, CPB), ("a_q", 4, CPB), ("a_out", 4, CPB),
                ("b_kv", 4, CPB), ("b_z", 4, CPB), ("b_cmp", 0, 0), ("b_q", 4, CPB), ("b_out", 4, CPB)):
            chunk_base[name], block_base[name], chunks_per[name] = c_at, b_at, chunks
            c_at += blocks * chunks if name != "b_cmp" else 2 * CPB
            b_at += blocks
            assert c_at % RING == 0

        def block_done(name, b):
            return (b + 1) * chunks_per[name] + chunk_base[name]

        def filled(c_base, c):
            return 16 * (c_base // RING + c // RING + 1)

        def filled_at(c_base, c, j):
            if isinstance(c, int):
                return filled(c_base, c + j)
            return c * 4 + (16 * (c_base // RING + j // RING + 1))

        CREDIT = {"ptc_act": 1, "ptc_dve": 1, "ogc_done": 1, "og_done": 1, "pt_done": 2, "pv_done": 1,
                  "ogt_done": 1}

        block = es.enter_context(nc.Block())

        @block.sync
        def _(sp):
            sp.dma_start(cst_sb[:, :], T["consts"]).then_inc(consts_in, 16)
            sp.dma_start(vec_sb[:, :], T["vecs"]).then_inc(consts_in, 16)
            sp.dma_start(x_sb, T["x"][0].rearrange("(t p) n -> p t n", p=P)).then_inc(x_in, 16)

            def chunk(c, src, rows=P, slot=None, dst=None):
                if not (isinstance(c, int) and c < RING):
                    sp.wait_ge(w_used, c - RING + 1)
                if dst is None:
                    dst = ring[0:rows, slot, :, 0:src.shape[-1]]
                    src = src.rearrange("(k p) n -> p k n", p=rows)
                sp.dma_start(dst, src).then_inc(w_full[slot], 16)

            def stream(c_base, n0, n1, w, col0, cpb=CPB, width=NB):
                def body(n):
                    for j in range(cpb):
                        chunk(c_base + cpb * (n - n0) + j,
                              w[j * 512:(j + 1) * 512, ds(col0 + (n - n0) * NB, width)], slot=j % RING)
                n = n0
                if c_base == 0:
                    body(n)
                    n += 1
                if n1 - n == 1:
                    body(n)
                else:
                    with sp.Fori(n, n1) as i:
                        body(i)

            sp.dma_start(pos_i[:, :], T["pos"]).then_inc(pos_in, 16)
            sp.dma_start(sinks, T["a_sinks_2"][0:1, :].to_broadcast([P, NKV * HG])).then_inc(sinks_in, 16)
            w_in = T["sgu_w_in"][0]
            stream(chunk_base["sgu_v"], 0, 8, w_in, SGU_W)

            def uz_block(n):
                for part in range(2):
                    if part:
                        if not (isinstance(n, int) and n == 0):
                            sp.wait_ge(y_done, n)
                        sp.dma_start(g_blk, T["sgu_norm_g"][0:1, ds(n * NB, NB)].to_broadcast([P, NB])
                                     ).then_inc(g_in, 16)
                    for j in range(CPB):
                        chunk(chunk_base["sgu_uz"] + 2 * CPB * n + part * CPB + j,
                              w_in[j * 512:(j + 1) * 512, ds(part * 2 * SGU_W + n * NB, NB)], slot=j)

            uz_block(0)
            with sp.Fori(1, 8) as n:
                uz_block(n)
            stream(chunk_base["sgu_out"], 0, 4, T["sgu_w_out"][0], 0, cpb=2 * CPB)
            if stages >= 2:
                stream(chunk_base["mla_in"], 0, 6, T["mla_w_in"][0], 0)
                with sp.Fori(0, 4) as i:
                    for u in range(2):
                        pair = 2 * i + u
                        chunk(chunk_base["mla_heads"] + 2 * pair, T["mla_w_uq"][0][:, ds(pair * HPP * QKD, HPP * QKD)],
                              rows=QL_P, slot=2 * u)
                        chunk(chunk_base["mla_heads"] + 2 * pair + 1,
                              T["mla_w_ukv"][0][:, ds(pair * NB, NB)], slot=2 * u + 1)
                stream(chunk_base["mla_out"], 0, 4, T["mla_w_out"][0], 0)
            if stages >= 3:
                w = T["a_w_in_2"][0]
                stream(chunk_base["a_kvz"], 0, 5, w, D)
                stream(chunk_base["a_q"], 0, 4, w, 0)
                stream(chunk_base["a_out"], 0, 4, T["a_w_out_2"][0], 0)
            if stages >= 4:
                w = T["b_w_in_2"][0]
                stream(chunk_base["b_kv"], 0, 3, w, D)
                stream(chunk_base["b_kv"] + 3 * CPB, 0, 1, w, D + 6 * NKV * HD, width=96)
                stream(chunk_base["b_z"], 0, 4, w, D + 6 * NKV * HD + 96)
                w2 = T["b_cmp_k_w2_2"][0].rearrange("(k p) n -> p k n", p=P)
                for m in range(2):
                    sp.dma_start(w2k[:, :, m * HD:(m + 1) * HD], w2).then_inc(w2_in, 16)
                sp.dma_start(w2v, T["b_cmp_v_w2_2"][0].rearrange("(k p) n -> p k n", p=P)).then_inc(w2_in, 16)
                for m, name in enumerate(("b_cmp_k_w1_2", "b_cmp_v_w1_2")):
                    for j in range(CPB):
                        chunk(chunk_base["b_cmp"] + m * CPB + j,
                              T[name][0][j * 512:(j + 1) * 512, :].rearrange("(l d) n -> d l n", d=HD),
                              slot=j, dst=reg_w[0:HD, j * 2048:(j + 1) * 2048].rearrange("p (l n) -> p l n", n=CH))
                stream(chunk_base["b_q"], 0, 4, w, 0)
                stream(chunk_base["b_out"], 0, 4, T["b_w_out_2"][0], 0)
            sp.wait_ge(x_ready, stages)
            sp.dma_start(T["out"][0].rearrange("(t p) n -> p t n", p=P), x_sb if stages < 5 else y_sb).then_inc(out_in, 16)
            sp.wait_ge(out_in, 16)


        ADA_STAGES = (((0, 0), (0, D)), ((0, 2 * D), (1, 0)), ((1, D), (1, 2 * D)))

        @block.gpsimd
        def _(pool):
            pool.memset(ones[:, :], 1.0).then_inc(ones_set, 1)

            def ada_chunks(stage, t, T_):
                for j in range(4):
                    layer, col = ADA_STAGES[stage][j // 2]
                    if isinstance(T_, int) and T_ == 0:
                        pass
                    else:
                        pool.wait_ge(ada_used, 4 * T_ + j - 3)
                    pool.dma_start(ada_buf[:, j, :],
                                   T["ada_w"][layer][ds(t * P, P), col + (j % 2) * ADA_C:col + (j % 2 + 1) * ADA_C]
                                   ).then_inc(ada_full[j], 16)

            def init_acc(stage):
                if stage == 1:
                    pool.wait_ge(cols_done, 1)
                if stage == 2:
                    pool.wait_ge(cols_done, 2)
                    pool.wait_ge(gate_rows, 4)
                pool.memset(ada_acc, 0.0).then_inc(acc_zero, 1)
                pool.wait_ge(acc_zero, stage + 1)
                for m, (layer, col) in enumerate(ADA_STAGES[stage]):
                    pool.dma_start(ada_acc[0:1, m * D:(m + 1) * D], T["ada_b"][layer:layer + 1, col:col + D]
                                   ).then_inc(acc_init, 16)

            init_acc(0)
            ada_chunks(0, 0, 0)
            with pool.Fori(1, KT) as t:
                ada_chunks(0, t, t)
            pool.dma_start(gate_g, T["post_g"][0:1, :].to_broadcast([P, D])).then_inc(postg_in, 16)
            for stage in (1, 2):
                init_acc(stage)
                with pool.Fori(0, KT) as t:
                    ada_chunks(stage, t, t + KT * stage)
                if stage == 1:
                    pass
            pool.wait_ge(mix_done, 8)
            pool.dma_start(x_sb, T["x"][0].rearrange("(t p) n -> p t n", p=P)).then_inc(x_back, 16)
            if stages >= 2:
                pool.wait_ge(x_ready, 1)
                pool.dma_start(gate_g, T["post_g"][1:2, :].to_broadcast([P, D])).then_inc(postg_in, 16)
            if stages >= 5:
                pool.wait_ge(w_used, block_done("b_q", NKV - 1))
                pool.dma_start(last_gain, T["final_norm_w_2"].rearrange("(a n) -> a n", a=1).to_broadcast([P, D])
                               ).then_inc(gain_in, 16)

        N_NORMS = min(stages + 1, 5)

        @block.tensor
        def _(pe):
            pe.wait_ge(consts_in, 32)
            pe.wait_ge(ones_set, 1)

            def gemm_k(k, lhs, bank, c_base, c, n_k, width=NB, rows=P):
                j = k // CHUNK_KT
                slot = (c_base + c + j) % RING if isinstance(c, int) else j % RING
                if k % CHUNK_KT == 0:
                    pe.wait_ge(w_full[slot], filled_at(c_base, c, j))
                for tb in range(TB):
                    mm = pe.matmul(ps[:, bank + tb, 0:width], lhs[0:rows, k, tb * P:(tb + 1) * P],
                                   ring[0:rows, slot, k % CHUNK_KT, 0:width], start=(k == 0), stop=(k == n_k - 1))
                if k % CHUNK_KT == CHUNK_KT - 1:
                    mm.then_inc(w_used, 1)

            def gemm(lhs, bank, c_base, c, n_k=KT, width=NB, rows=P):
                for k in range(n_k):
                    gemm_k(k, lhs, bank, c_base, c, n_k, width, rows)

            def norm_transposes(idx):
                pe.wait_ge(xn_done, idx + 1)
                for kp in range(KT // 2):
                    n = idx * KT // 2 + kp
                    if n >= 2:
                        pe.wait_ge(xT_free[kp % 2], n // 2)
                    for k in range(2):
                        for tb in range(TB):
                            f = (2 * kp + k) * P
                            mm = pe.transpose(ps[:, 6 + kp % 2, k * S + tb * P:k * S + (tb + 1) * P],
                                              y_sb[:, tb, f:f + P], ident)
                    mm.then_inc(xT_done, 1)

            def wait_hT(idx):
                for e in range(2):
                    pe.wait_ge(xT_free[e], (idx + 1) * KT // 4)

            def ada_columns(n_cols, acc_lo, at):
                for f in range(n_cols):
                    mm = pe.matmul(ps[:, 4, at + f:at + f + 1], ada_acc[:, acc_lo + f * P:acc_lo + (f + 1) * P],
                                   ones[:, 0:1], start=True, stop=True)
                return mm

            def gate_row_sums(acc_lo, n0):
                for q in range(4):
                    if n0 + q >= 1:
                        pe.wait_ge(gate_read, n0 + q)
                    pe.matmul(ps[:, 5, :], ones[:, :], ada_acc[:, acc_lo + q * NB:acc_lo + (q + 1) * NB],
                              start=True, stop=True).then_inc(gate_rows, 1)

            pe.wait_ge(ada_used, 4 * KT)
            ada_columns(2 * KT, 0, 0).then_inc(cols_done, 1)
            norm_transposes(0)

            wait_hT(0)
            def v_blocks(i, first=False):
                for u in range(2):
                    if not first:
                        pe.wait_ge(proj_free, 2 * i + u - 1)
                    gemm(hT, 2 * u, chunk_base["sgu_v"], 2 * CPB * i + CPB * u)

            v_blocks(0, first=True)
            with pe.Fori(1, 4) as i:
                v_blocks(i)
            pe.wait_ge(ada_used, 8 * KT)
            gate_row_sums(0, 0)
            ada_columns(KT, D, 0).then_inc(cols_done, 1)

            def mix(n):
                pe.wait_ge(wcur_done, n + 1)
                for tb in range(TB):
                    for g in range(GPB):
                        mm = pe.matmul(ps[:, 4 + tb, g * SGU_GD:(g + 1) * SGU_GD], w_cur[:, g, :],
                                       v_sb[:, tb, ds(n * NB + g * SGU_GD, SGU_GD)], start=True, stop=True)
                mm.then_inc(mix_done, 1)

            def y_transposes(n):
                pe.wait_ge(y_done, n + 1)
                if not (isinstance(n, int) and n == 0):
                    pe.wait_ge(yT_done, n)
                for tb in range(TB):
                    for k in range(NB // P):
                        mm = pe.transpose(ps[:, 6 + tb, k * P:(k + 1) * P], y_t[:, tb, k * P:(k + 1) * P], ident)
                mm.then_inc(yt_done, 1)

            def uz(n, first=False):
                b0 = block_base["sgu_uz"]
                if not first:
                    pe.wait_ge(proj_free, b0 + 2 * n - 1)
                gemm(hT, 0, chunk_base["sgu_uz"], 2 * CPB * n)
                if not first:
                    y_transposes(n - 1)
                mix(n)
                if not first:
                    pe.wait_ge(proj_free, b0 + 2 * n)
                gemm(hT, 2, chunk_base["sgu_uz"], 2 * CPB * n + CPB)

            pe.wait_ge(proj_free, block_base["sgu_uz"])
            pe.wait_ge(v_norm, 1)
            pe.wait_ge(aff_ready, 2)
            pe.wait_ge(gate_read, 4)
            uz(0, first=True)
            with pe.Fori(1, 8) as n:
                uz(n)
            y_transposes(7)

            pe.wait_ge(yT_done, 8)
            pe.wait_ge(proj_free, block_base["sgu_out"])
            with pe.Fori(0, 2) as i:
                for u in range(2):
                    pe.wait_ge(proj_free, block_base["sgu_out"] + 2 * i + max(u - 1, 0))
                    gemm(yT, 2 * u, chunk_base["sgu_out"], 4 * CPB * i + 2 * CPB * u, n_k=2 * KT)
            pe.wait_ge(ada_used, 12 * KT)
            ada_columns(KT, 0, KT).then_inc(cols_done, 1)
            if stages >= 2:
                norm_transposes(1)
                wait_hT(1)
                pe.wait_ge(aff_ready, 3)

                def in_blocks(name, i, first=False):
                    for u in range(2):
                        if not first:
                            pe.wait_ge(proj_free, block_base[name] + 2 * i + u - 1)
                        gemm(hT, 2 * u, chunk_base[name], 2 * CPB * i + CPB * u)

                pe.wait_ge(proj_free, block_base["mla_in"])
                in_blocks("mla_in", 0, first=True)
                with pe.Fori(1, 3) as i:
                    in_blocks("mla_in", i)
                gate_row_sums(D, 4)

                pe.wait_ge(c_normed, 1)
                pe.wait_ge(proj_free, block_base["mla_heads"])
                pe.wait_ge(gate_read, 8)
                for k in range(4):
                    for tb in range(TB):
                        at = (k % 2) * S + tb * P
                        pe.transpose(ps[0:QL_P, 6 + k // 2, at:at + P], craw[:, tb, k * QL_P:(k + 1) * QL_P], ident)
                        pe.transpose(ps[:, 4 + k // 2, at:at + P],
                                     craw[:, tb, QL + k * P:QL + (k + 1) * P], ident)
                for tb in range(TB):
                    mm = pe.transpose(ps[0:ROPE, 2, tb * P:(tb + 1) * P], craw[:, tb, QL + KVL:QL + KVL + ROPE], ident)
                mm.then_inc(cT_turned, 1)
                pe.wait_ge(cT_act, 1)
                pe.wait_ge(cT_dve, 1)

                c0, b0 = chunk_base["mla_heads"], block_base["mla_heads"]

                def q_gemm(pair, par):
                    for k in range(4):
                        gemm_k4(k, cqT, 0, pair, 2 * par, HPP * QKD, QL_P)

                def kv_gemm(pair, par, ks=range(4)):
                    for k in ks:
                        gemm_k4(k, ckvT, 2, pair, 2 * par + 1, NB, P)

                def gemm_k4(k, lhs, bank, pair, slot, width, rows):
                    if k == 0:
                        pe.wait_ge(w_full[slot], pair_filled(pair))
                    for tb in range(TB):
                        mm = pe.matmul(ps[:, bank + tb, 0:width], lhs[0:rows, k, tb * P:(tb + 1) * P],
                                       ring[0:rows, slot, k, 0:width], start=(k == 0), stop=(k == 3))
                    if k == 3:
                        mm.then_inc(w_used, 1)

                def pair_filled(pair):
                    i, par = pair
                    return 16 * (c0 // RING + 1) + 16 * i

                def heads(i, par, last=False):
                    p = 2 * i + par
                    pe.wait_ge(proj_free, b0 + 2 * p + 2)
                    pe.wait_ge(q_roped, p + 1)
                    pe.wait_ge(ptc_act, CREDIT["ptc_act"] + p)
                    pe.wait_ge(ptc_dve, CREDIT["ptc_dve"] + p)
                    for h in range(HPP):
                        for tb in range(TB):
                            at = h * S + tb * P
                            mm = pe.transpose(ps[:, 6, at:at + P], q_sb[par][:, tb, h * QKD:h * QKD + NOPE], ident)
                    mm.then_inc(turned_q, 1)
                    for h in range(HPP):
                        for tb in range(TB):
                            at = h * S + tb * P
                            mm = pe.transpose(ps[:, 7, at:at + P], kv_sb[par][:, tb, h * S:h * S + NOPE], ident)
                    mm.then_inc(turned_k, 1)
                    pe.wait_ge(consts_in, 32)
                    pe.wait_ge(ogc_done, CREDIT["ogc_done"] + p)
                    for h in range(HPP):
                        for tb in range(TB):
                            at = h * S + tb * P
                            mm = pe.transpose(ps[0:ROPE, 5, at:at + P],
                                              q_sb[par][:, tb, h * QKD + NOPE:(h + 1) * QKD], ident)
                    mm.then_inc(turned_r, 1)
                    pe.wait_ge(kT_copied, p + 1)
                    pe.wait_ge(qT_copied, 2 * p + 2)
                    pe.wait_ge(og_done, CREDIT["og_done"] + p)
                    for h in range(HPP):
                        for tb in range(TB):
                            out = ps[:, 4 + h, tb * P:tb * P + (tb + 1) * P]
                            keys = slice(0, (tb + 1) * P)
                            pe.matmul(out, qT[:, h, tb * P:(tb + 1) * P], kT[:, h, keys], start=True, stop=False)
                            mm = pe.matmul(out, qrT[0:ROPE, h, tb * P:(tb + 1) * P], krT[0:ROPE, keys],
                                           start=False, stop=True)
                        mm.then_inc(scores_done, 1)
                    if not last:
                        nxt = (i, 1) if par == 0 else (i + 1, 0)
                        q_gemm(nxt, nxt[1])
                    for h in range(HPP):
                        pe.wait_ge(exp_done, 2 * p + h + 1)
                        for b in range(3):
                            mm = pe.transpose(ps[:, 6 + h, b * P:(b + 1) * P], prob[h][:, b * P:(b + 1) * P], ident)
                        mm.then_inc(pt_done, 1)
                    if not last:
                        kv_gemm(nxt, nxt[1], (0, 1))
                    pe.wait_ge(ptc_act, CREDIT["ptc_act"] + p + 1)
                    pe.wait_ge(ptc_dve, CREDIT["ptc_dve"] + p + 1)
                    for h in range(HPP):
                        v = lambda tb: kv_sb[par][:, tb, h * S + NOPE:(h + 1) * S]
                        at = h * S
                        pe.matmul(ps[:, 4, at:at + P], probT[h][:, 0:P], v(0), start=True, stop=True)
                        pe.matmul(ps[:, 4, at + P:at + 2 * P], probT[h][:, P:2 * P], v(0), start=True, stop=False)
                        mm = pe.matmul(ps[:, 4, at + P:at + 2 * P], probT[h][:, 2 * P:3 * P], v(1),
                                       start=False, stop=True)
                    mm.then_inc(pv_done, 1)
                    if not last:
                        kv_gemm(nxt, nxt[1], (2, 3))
                    pe.wait_ge(og_done, CREDIT["og_done"] + p + 1)
                    for h in range(HPP):
                        for tb in range(TB):
                            at = h * S + tb * P
                            mm = pe.transpose(ps[:, 5, at:at + P], og[:, tb, h * VH:(h + 1) * VH], ident)
                    mm.then_inc(ogt_done, 1)

                q_gemm((0, 0), 0)
                kv_gemm((0, 0), 0)
                with pe.Fori(0, 3) as i:
                    for par in range(2):
                        heads(i, par)
                heads(3, 0)
                heads(3, 1, last=True)

                def out_blocks(name, lhs):
                    pe.wait_ge(proj_free, block_base[name])
                    with pe.Fori(0, 2) as i:
                        for u in range(2):
                            pe.wait_ge(proj_free, block_base[name] + 2 * i + max(u - 1, 0))
                            gemm(lhs, 2 * u, chunk_base[name], 2 * CPB * i + CPB * u)

                pe.wait_ge(ogc_done, CREDIT["ogc_done"] + 8)
                out_blocks("mla_out", oT)
            def kvz(m):
                name = m.name
                if m.branches == 1:
                    gemm(hT, 0, chunk_base["a_kvz"], 0)
                    z_name, z_at = "a_kvz", 1
                else:
                    b0 = block_base["b_kv"]
                    for b in range(4):
                        if b >= 2:
                            pe.wait_ge(proj_free, b0 + b - 1)
                        gemm(hT, 2 * (b % 2), chunk_base["b_kv"], CPB * b, width=NB if b < 3 else 96)
                    z_name, z_at = "b_z", 0
                b0 = block_base[z_name] + z_at

                def z_blocks(i, us=range(2)):
                    for u in us:
                        b = 2 * i + u
                        pe.wait_ge(proj_free, b0 + b - 1)
                        gemm(hT, 2 * ((z_at + u) % 2), chunk_base[z_name], CPB * (b + z_at))

                z_blocks(0)
                for br in range(m.branches):
                    pe.wait_ge(m.kdup, br + 1)
                    if br:
                        pe.wait_ge(m.kT_act, br)
                        pe.wait_ge(m.kT_dve, br)
                    for g in range(NKV):
                        for tb in range(TB):
                            at = (g % 2) * S + tb * P
                            mm = pe.transpose(ps[:, 4 + g // 2, at:at + P], k_dup[br][:, tb, g * P:(g + 1) * P], ident)
                    mm.then_inc(m.k_turned, 1)
                if m.branches == 2:
                    for c in range(2):
                        if c:
                            pe.wait_ge(c_copied, 1)
                        for g in range(NKV):
                            for tb in range(TB):
                                at = (g % 2) * S + tb * P
                                lo = c * NKV * HD + g * HD
                                mm = pe.transpose(ps[0:HD, 6 + g // 2, at:at + P], raw[0][:, tb, lo:lo + HD], ident)
                        mm.then_inc(c_turned, 1)
                z_blocks(1)

            def compress():
                for c in range(2):
                    pe.wait_ge(unfolded, c + 1)
                    if c:
                        pe.wait_ge(gelu_done, 1)
                    for l in range(CL):
                        j = l // 8
                        if l % 8 == 0:
                            pe.wait_ge(w_full[j], filled(chunk_base["b_cmp"], c * CPB + j))
                        for hh in range(2):
                            mm = pe.matmul(ps[:, 4 + hh, 0:NKV * NCMP],
                                           reg_w[0:HD, l * CH + hh * P:l * CH + (hh + 1) * P],
                                           unfold[0:HD, l, :, :].rearrange("p g n -> p (g n)"),
                                           start=(l == 0), stop=(l == CL - 1))
                        if l % 8 == 7:
                            mm.then_inc(w_used, 1)
                    pe.wait_ge(gelu_done, c + 1)
                    pe.wait_ge(w2_in, 48)
                    if c == 0:
                        for hh in range(2):
                            mm = pe.matmul(ps[:, 6, 0:NKV * NCMP], w2k[:, hh, :], hidT[:, hh, :],
                                           start=(hh == 0), stop=(hh == 1))
                    else:
                        for g in range(NKV):
                            for hh in range(2):
                                mm = pe.matmul(ps[0:NCMP, 7, g * HD:(g + 1) * HD],
                                               hidT[:, hh, g * NCMP:(g + 1) * NCMP], w2v[:, hh, :],
                                               start=(hh == 0), stop=(hh == 1))
                    mm.then_inc(cmp_w2, 1)

            def groups(m):
                name, NU = m.name + "_q", m.units
                b0 = block_base[name]
                is_b = m.branches == 2

                def rows(h):
                    return slice((h % 2) * HD, (h % 2 + 1) * HD)

                def scores(g, u):
                    h, br = u % HG, u // HG
                    pe.wait_ge(m.max_done, NU * g + u + 1)
                    for tb in range(TB):
                        mm = pe.matmul(ps[:, 2 + u % 2, tb * P:tb * P + (tb + 1) * P],
                                       qT_grp[rows(h), h // 2, tb * P:(tb + 1) * P],
                                       kT_grp[br][rows(h), 0:(tb + 1) * P], start=True, stop=True)
                    mm.then_inc(m.scores, 1)

                def turn_probs(g, u):
                    pe.wait_ge(m.exp_done, NU * g + u + 1)
                    pe.wait_ge(m.ptc_dve if u % 2 else m.ptc_act, (NU // 2) * g + u // 2 + 1)
                    for b in range(3):
                        mm = pe.transpose(ps[:, 4 + u % 2, b * P:(b + 1) * P],
                                          prob4[u % 4][:, b * P:(b + 1) * P], ident)
                    mm.then_inc(m.pt_done, 1)

                def pv(g, u):
                    h, br = u % HG, u // HG
                    pe.wait_ge(m.ptc_dve if u % 2 else m.ptc_act, (NU // 2) * g + u // 2 + 2)
                    if h == 0:
                        pe.wait_ge(m.o_read, m.reads * (g + 1) + br + is_b)
                    src = raw[br + is_b]
                    v = lambda tb: src[:, tb, ds(NKV * HD + g * HD, HD)]
                    pt = probT2[u % 2]
                    pe.matmul(ps[:, 6, h * HD:(h + 1) * HD], pt[:, 0:P], v(0), start=True, stop=True)
                    pe.matmul(ps[:, 7, h * HD:(h + 1) * HD], pt[:, P:2 * P], v(0), start=True, stop=False)
                    pe.matmul(ps[:, 7, h * HD:(h + 1) * HD], pt[:, 2 * P:3 * P], v(1),
                              start=False, stop=True).then_inc(m.pv_done, 1)

                def group(g, last=False):
                    pe.wait_ge(m.q_roped, g + 1)
                    for bank in range(2):
                        pe.wait_ge((m.ptc_act, m.ptc_dve)[bank], (NU // 2) * g + 1)
                        pe.wait_ge((m.ogc_act, m.ogc_dve)[bank], g + 1)
                        for j in range(2):
                            for tb in range(TB):
                                pair = 2 * bank + j
                                mm = pe.transpose(ps[:, 4 + bank, j * S + tb * P:j * S + (tb + 1) * P],
                                                  q_grp[:, tb, pair * P:(pair + 1) * P], ident)
                        mm.then_inc(m.turned, 1)
                    k_next = [0]

                    def next_queries(n):
                        for _ in range(0 if last else n):
                            if k_next[0] == 0:
                                pe.wait_ge(proj_free, b0 + g + 1)
                            gemm_k(k_next[0], hT, 0, chunk_base[name], CPB * (g + 1), KT)
                            k_next[0] += 1

                    pe.wait_ge(m.qT_act, g + 1)
                    pe.wait_ge(m.qT_dve, g + 1)
                    pe.wait_ge(m.k_ready, g + 1)
                    if is_b:
                        pe.wait_ge(m.o_read, m.reads * (g + 1))
                        pe.matmul(ps[0:HG * NCMP, 6, 256:256 + HD], cst("spread")[0:NCMP, :],
                                  vcmp[0:NCMP, ds(g * HD, HD)], start=True, stop=True)
                        for tb in range(TB):
                            for h in range(HG):
                                at = (tb * HG // 2 + h // 2) * NCMP
                                mm = pe.matmul(ps[:, 6 + h % 2, at:at + NCMP], qT_grp[rows(h), h // 2, tb * P:(tb + 1) * P],
                                               kcmp_grp[rows(h), :], start=True, stop=True)
                        mm.then_inc(cmp_scores, 1)
                    scores(g, 0)
                    scores(g, 1)
                    if is_b:
                        next_queries(1)
                        pe.wait_ge(cmp_exp, g + 1)
                        for tb in range(TB):
                            mm = pe.transpose(ps[0:HG * NCMP, 7, tb * P:(tb + 1) * P],
                                              p_cmp[:, tb * HG * NCMP:(tb + 1) * HG * NCMP], ident)
                        mm.then_inc(cmp_turned, 1)
                        next_queries(1)
                        pe.wait_ge(cmp_copied, g + 1)
                        pe.wait_ge(vbd_done, g + 1)
                        for tb in range(TB):
                            mm = pe.matmul(ps[:, 6 + tb, :], pT_cmp[0:HG * NCMP, tb, :], v_bd[0:HG * NCMP, :],
                                           start=True, stop=True)
                        mm.then_inc(cmp_pv, 1)
                    for u in range(NU):
                        turn_probs(g, u)
                        if u + 2 < NU:
                            scores(g, u + 2)
                        next_queries(1 if is_b and u < 14 else 3 if u < 4 else 2 if u < 6 else 0)
                        pv(g, u)
                    assert last or k_next[0] == KT
                    pe.wait_ge(m.og_done, g + 2)
                    for bank in range(2):
                        for j in range(2):
                            for tb in range(TB):
                                pair = 2 * bank + j
                                mm = pe.transpose(ps[:, 4 + bank, j * S + tb * P:j * S + (tb + 1) * P],
                                                  o_grp[:, tb, pair * P:(pair + 1) * P], ident)
                        mm.then_inc(m.ogt_done, 1)

                pe.wait_ge(proj_free, b0)
                gemm(hT, 0, chunk_base[name], 0)
                with pe.Fori(0, NKV - 1) as g:
                    group(g)
                group(NKV - 1, last=True)
                pe.wait_ge(m.ogc_act, NKV + 1)
                pe.wait_ge(m.ogc_dve, NKV + 1)

            for m, idx in ((ma, 2), (mb, 3)):
                if m is not None:
                    norm_transposes(idx)
                    wait_hT(idx)
                    pe.wait_ge(proj_free, block_base["a_kvz" if idx == 2 else "b_kv"])
                    kvz(m)
                    if idx == 3:
                        compress()
                    groups(m)
                    out_blocks(f"{m.name}_out", oT)

        @block.scalar
        def _(act):
            act_n = [0]

            def norm_stats(idx):
                act.wait_ge(x_ready, idx) if idx else act.wait_ge(x_in, 16)
                for tb in range(TB):
                    mm = act.activation(y_sb[:, tb, :], x_sb[:, tb, :], ACT.Square, accum_out=sumsq[:, tb:tb + 1])
                mm.then_inc(ssq_done, 1)
                root()

            roots = [0]

            def root(n=TB):
                roots[0] += 1
                act.wait_ge(ms_done, roots[0])
                act.activation(rms[:, 0:n], rms[:, 0:n], ACT.Sqrt).then_inc(rms_done, 1)

            def hT_copies(idx):
                if idx < 2:
                    act.wait_ge(aff_ready, 1 if idx == 0 else 3)
                for kp in range(0, KT // 2, 2):
                    act.wait_ge(xT_done, idx * KT // 2 + kp + 1)
                    for k in (2 * kp, 2 * kp + 1):
                        src = ps[:, 6, (k % 2) * S:(k % 2 + 1) * S]
                        if idx < 2:
                            a = act.activation(hT[:, k, :], src, ACT.Identity, scale=aff_a[:, k:k + 1],
                                               bias=aff_b[:, k:k + 1])
                        else:
                            a = act.activation(hT[:, k, :], src, ACT.Copy,
                                               scale=vec(f"norm_w{idx - 2}")[:, k:k + 1])
                    a.then_inc(xT_free[0], 1)

            act.wait_ge(consts_in, 32)
            act.activation(cond, vec("c"), ACT.Silu).then_inc(cond_done, 1)
            norm_stats(0)
            hT_copies(0)
            with act.Fori(0, 4) as i:
                for u in range(2):
                    act.wait_ge(w_used, block_done("sgu_v", 2 * i + u))
                    act.activation(v_sb[:, :, ds(i * 2 * NB + u * NB, NB)], ps[:, 2 * u:2 * u + 2, :], ACT.Gelu
                                   ).then_inc(proj_free, 1)
            root()

            def y_copies(n):
                act.wait_ge(yt_done, n + 1)
                for tb in range(TB):
                    a = act.activation(yT[:, ds(n * 4, 4), tb * P:(tb + 1) * P],
                                       ps[:, 6 + tb, :].rearrange("p (k s) -> p k s", k=4), ACT.Copy)
                a.then_inc(yT_done, 1)

            def uz(n, first=False):
                b0 = block_base["sgu_uz"]
                if not first:
                    act.wait_ge(y_done, n)
                act.wait_ge(w_used, block_done("sgu_uz", 2 * n))
                act.activation(u_t, ps[:, 0:2, :], ACT.Gelu).then_inc(proj_free, 1)
                if not first:
                    y_copies(n - 1)
                act.wait_ge(w_used, block_done("sgu_uz", 2 * n + 1))
                act.activation(z_t, ps[:, 2:4, :], ACT.Silu).then_inc(proj_free, 1)

            uz(0, first=True)
            with act.Fori(1, 8) as n:
                uz(n)
            y_copies(7)

            squares = [0]

            def square_blocks(name):
                for b in range(4):
                    act.wait_ge(w_used, block_done(name, b))
                    for tb in range(TB):
                        if squares[0]:
                            act.wait_ge(ysq_done, squares[0])
                        squares[0] += 1
                        act.activation(sq_junk, ps[:, 2 * (b % 2) + tb, :], ACT.Square,
                                           accum_out=ysq[:, tb * 4 + b:tb * 4 + b + 1]).then_inc(ysq_done, 1)

            square_blocks("sgu_out")
            root()
            if stages > 1:
                norm_stats(1)
            if stages >= 2:
                hT_copies(1)
                for b in range(2):
                    act.wait_ge(w_used, block_done("mla_in", b))
                    act.activation(craw[:, :, b * NB:(b + 1) * NB], ps[:, 2 * b:2 * b + 2, :], ACT.Copy
                                   ).then_inc(proj_free, 1)
                act.wait_ge(proj_free, block_base["mla_in"] + 2)
                for m, (lo, n) in enumerate(((0, QL), (QL, KVL))):
                    for tb in range(TB):
                        if m or tb:
                            act.wait_ge(c_ssq, m * TB + tb)
                        act.activation(sq_junk[:, 0:n], craw[:, tb, lo:lo + n], ACT.Square,
                                       accum_out=c_sq[:, m * TB + tb:m * TB + tb + 1]).then_inc(c_ssq, 1)
                root(2 * TB)
                with act.Fori(0, 2) as i:
                    for u in range(2):
                        act.wait_ge(w_used, block_done("mla_in", 2 * i + u + 2))
                        act.activation(z_sb[:, :, ds((2 * i + u) * NB, NB)], ps[:, 2 * u:2 * u + 2, :], ACT.Silu
                                       ).then_inc(proj_free, 1)
                act.wait_ge(cT_turned, 1)
                for k in range(4):
                    a = act.activation(cqT[0:QL_P, k, :], ps[0:QL_P, 6 + k // 2, (k % 2) * S:(k % 2 + 1) * S],
                                       ACT.Copy, scale=vec("q_g")[0:QL_P, k:k + 1])
                a.then_inc(cT_act, 1)

                c0, b0 = chunk_base["mla_heads"], block_base["mla_heads"]

                def q_copy(p, par):
                    act.wait_ge(w_used, c0 + 2 * p + 1)
                    act.activation(q_sb[par], ps[:, 0:2, 0:HPP * QKD], ACT.Copy).then_inc(proj_free, 1)

                def kv_copy(p, par):
                    act.wait_ge(w_used, c0 + 2 * p + 2)
                    act.activation(kv_sb[par], ps[:, 2:4, :], ACT.Copy).then_inc(proj_free, 1)

                def heads(i, par, last=False):
                    p = 2 * i + par
                    act.wait_ge(turned_q, p + 1)
                    act.activation(qT, ps[:, 6, :].rearrange("p (h s) -> p h s", h=HPP), ACT.Copy
                                   ).then_inc(qT_copied, 1)
                    act.wait_ge(turned_r, p + 1)
                    act.activation(qrT[0:ROPE], ps[0:ROPE, 5, :].rearrange("p (h s) -> p h s", h=HPP), ACT.Copy
                                   ).then_inc(qT_copied, 1)
                    for h in range(HPP):
                        act.wait_ge(max_done, 2 * p + h + 1)
                        for tb in range(TB):
                            blk = prob[h][:, tb * P:tb * P + (tb + 1) * P]
                            n = h * TB + tb
                            a = act.activation(blk, blk, ACT.Exp, bias=nmx[:, n:n + 1], accum_out=sums[:, n:n + 1])
                        a.then_inc(exp_done, 1)
                    if not last:
                        q_copy(p + 1, 1 - par)
                    act.wait_ge(pt_done, CREDIT["pt_done"] + 2 * p + 1)
                    act.wait_ge(pv_done, CREDIT["pv_done"] + p)
                    act.activation(probT[0], ps[:, 6, 0:SCW], ACT.Copy).then_inc(ptc_act, 1)
                    if not last:
                        kv_copy(p + 1, 1 - par)
                    act.wait_ge(ogt_done, CREDIT["ogt_done"] + p + 1)
                    act.activation(oT[:, ds(HPP * p, HPP), :], ps[:, 5, :].rearrange("p (h s) -> p h s", h=HPP),
                                   ACT.Copy).then_inc(ogc_done, 1)

                act.sem_inc(ptc_act, CREDIT["ptc_act"])
                act.sem_inc(ogc_done, CREDIT["ogc_done"])
                act.sem_inc(pv_done, CREDIT["pv_done"])
                q_copy(0, 0)
                kv_copy(0, 0)
                with act.Fori(0, 3) as i:
                    for par in range(2):
                        heads(i, par)
                heads(3, 0)
                heads(3, 1, last=True)
                square_blocks("mla_out")
                root()
                if stages > 2:
                    norm_stats(2)
            def rotation_angles():
                act.wait_ge(trig_in, 1)
                act.activation(sin2, red, ACT.Sin)
                act.activation(cos2, turns, ACT.Sin).then_inc(trig_done, 1)

            def kvz(m):
                if m.branches == 1:
                    act.wait_ge(w_used, block_done("a_kvz", 0))
                    act.activation(raw[0], ps[:, 0:2, :], ACT.Copy).then_inc(proj_free, 1)
                    z_name, z_at = "a_kvz", 1
                else:
                    for b in range(3):
                        act.wait_ge(w_used, block_done("b_kv", b))
                        act.activation(raw[b], ps[:, 2 * (b % 2):2 * (b % 2) + 2, :], ACT.Copy).then_inc(proj_free, 1)
                    act.wait_ge(w_used, block_done("b_kv", 3))
                    act.activation(gates, ps[:, 2:4, 0:96], ACT.Sigmoid).then_inc(proj_free, 1)
                    z_name, z_at = "b_z", 0

                def z_block(b):
                    act.wait_ge(w_used, block_done(z_name, b + z_at))
                    bank = 2 * ((b + z_at) % 2)
                    act.activation(z_sb[:, :, b * NB:(b + 1) * NB], ps[:, bank:bank + 2, :], ACT.Silu
                                   ).then_inc(proj_free, 1)

                z_block(0)
                z_block(1)
                for br in range(m.branches):
                    act.wait_ge(m.k_turned, br + 1)
                    act.activation(kT_all[br][:, 0:2, :], ps[:, 4, :].rearrange("p (g s) -> p g s", g=2), ACT.Copy
                                   ).then_inc(m.kT_act, 1)
                if m.branches == 2:
                    for c in range(2):
                        act.wait_ge(c_turned, c + 1)
                        for bank in range(2):
                            a = act.activation(kcT[c][0:HD, 2 * bank:2 * bank + 2, :],
                                               ps[0:HD, 6 + bank, :].rearrange("p (g s) -> p g s", g=2), ACT.Copy)
                        a.then_inc(c_copied, 1)
                z_block(2)
                z_block(3)

            def compress():
                for c in range(2):
                    act.wait_ge(w_used, chunk_base["b_cmp"] + (c + 1) * CPB)
                    if c:
                        act.wait_ge(cmp_w2, 1)
                    act.activation(hidT, ps[:, 4:6, 0:NKV * NCMP], ACT.Gelu_apprx_tanh).then_inc(gelu_done, 1)

            def groups(m):
                name, NU = m.name + "_q", m.units
                is_b = m.branches == 2

                def q_copy(g):
                    act.wait_ge(w_used, block_done(name, g))
                    act.activation(q_grp, ps[:, 0:2, :], ACT.Copy).then_inc(proj_free, 1)

                def exps(g, u):
                    h, br = u % HG, u // HG
                    act.wait_ge(m.max_done, 2 + NU * g + u + 1)
                    for tb in range(TB):
                        n = tb * HG + h
                        blk = prob4[u % 4][:, tb * P:tb * P + (tb + 1) * P]
                        a = act.activation(blk, blk, ACT.Exp, bias=nmx2[:, n:n + 1],
                                           accum_out=sums2[br][:, n:n + 1])
                    a.then_inc(m.exp_done, 1)

                def group(g, last=False):
                    act.wait_ge(m.turned, 2 * g + 1)
                    act.activation(qT_grp[:, 0:2, :], ps[:, 4, :].rearrange("p (j s) -> p j s", j=2), ACT.Copy
                                   ).then_inc(m.qT_act, 1)
                    if is_b:
                        act.wait_ge(cmp_shifted, g + 1)
                        act.activation(p_cmp, p_cmp, ACT.Exp, scale=SCALE2).then_inc(cmp_exp, 1)
                    act.wait_ge(m.og_done, g + 1)
                    exps(g, 0)
                    exps(g, 1)
                    if is_b:
                        act.wait_ge(cmp_turned, g + 1)
                        act.activation(pT_cmp[0:HG * NCMP], ps[0:HG * NCMP, 7, 0:S].rearrange("p (t n) -> p t n", t=TB),
                                       ACT.Copy).then_inc(cmp_copied, 1)
                    for u in range(NU):
                        if u % 2 == 0:
                            act.wait_ge(m.pt_done, 4 + NU * g + u + 1)
                            act.wait_ge(m.pv_done, NU * g + u + 1)
                            act.activation(probT2[0], ps[:, 4, 0:SCW], ACT.Copy).then_inc(m.ptc_act, 1)
                        if u == NU - 2 and not last:
                            q_copy(g + 1)
                        if u + 2 < NU:
                            exps(g, u + 2)
                    if not is_b:
                        act.wait_ge(m.sink_in, g + 1)
                        act.activation(sink_e, sink_e, ACT.Exp).then_inc(m.sink_exp, 1)
                    act.wait_ge(m.ogt_done, 2 * g + 1)
                    act.activation(oT[:, ds(4 * g, 2), :], ps[:, 4, :].rearrange("p (j s) -> p j s", j=2), ACT.Copy
                                   ).then_inc(m.ogc_act, 1)

                act.sem_inc(m.ptc_act, 1)
                act.sem_inc(m.ogc_act, 1)
                q_copy(0)
                with act.Fori(0, NKV - 1) as g:
                    group(g)
                group(NKV - 1, last=True)

            for m, idx in ((ma, 2), (mb, 3)):
                if m is not None:
                    hT_copies(idx)
                    if idx == 2:
                        rotation_angles()
                    kvz(m)
                    if idx == 3:
                        compress()
                    groups(m)
                    if stages > idx + 1:
                        norm_stats(idx + 1)

        @block.vector
        def _(dve):
            steps = [0]

            def link(ins):
                steps[0] += 1
                ins.then_inc(dve_step, 1)
                dve.wait_ge(dve_step, steps[0])

            roots = [0]

            def take_waits():
                dve.memset(wait_cell, 0.0)

            def inverse_root(dst=rstd[:, 0:TB]):
                roots[0] += 1
                dve.wait_ge(rms_done, roots[0])
                link(dve.reciprocal(dst, rms[:, 0:dst.shape[-1]]))

            def norm_x(idx, eps, final=False):
                dve.wait_ge(ssq_done, idx + 1)
                dve.tensor_scalar(rms[:, 0:TB], sumsq, 1.0 / D, eps, ALU.mult, ALU.add).then_inc(ms_done, 1)
                inverse_root()
                if final:
                    dve.wait_ge(gain_in, 16)
                    for tb in range(TB):
                        v = dve.scalar_tensor_tensor(out=y_sb[:, tb, :], in0=x_sb[:, tb, :], scalar=rstd[:, tb:tb + 1],
                                                     in1=last_gain, op0=ALU.mult, op1=ALU.mult)
                    v.then_inc(x_ready, 1)
                    return
                for tb in range(TB):
                    v = dve.tensor_scalar(y_sb[:, tb, :], x_sb[:, tb, :], rstd[:, tb:tb + 1], None, ALU.mult)
                v.then_inc(xn_done, 1)

            def hT_copies(idx):
                for kp in range(1, KT // 2, 2):
                    dve.wait_ge(xT_done, idx * KT // 2 + kp + 1)
                    for k in (2 * kp, 2 * kp + 1):
                        src = ps[:, 7, (k % 2) * S:(k % 2 + 1) * S]
                        if idx < 2:
                            v = dve.tensor_scalar(hT[:, k, :], src, aff_a[:, k:k + 1], aff_b[:, k:k + 1],
                                                  ALU.mult, ALU.add)
                        else:
                            v = dve.tensor_scalar(hT[:, k, :], src, vec(f"norm_w{idx - 2}")[:, k:k + 1], None,
                                                  ALU.mult)
                    v.then_inc(xT_free[1], 1)

            def ada_gemv(t, T_):
                for j in range(4):
                    dve.wait_ge(ada_full[j], 16 * T_ + 16)
                    if not (isinstance(T_, int) and T_ == 0):
                        dve.wait_ge(ada_used, 4 * T_ + j - 3)
                    acc = ada_acc[:, j * ADA_C:(j + 1) * ADA_C]
                    dve.scalar_tensor_tensor(out=acc, in0=ada_buf[:, j, :], scalar=cond[:, ds(t, 1)], in1=acc,
                                             op0=ALU.mult, op1=ALU.add).then_inc(ada_used, 1)

            dve.wait_ge(consts_in, 32)
            dve.wait_ge(cond_done, 1)
            dve.wait_ge(acc_init, 32)
            dve.wait_ge(acc_zero, 1)
            norm_x(0, EPS1)
            ada_gemv(0, 0)
            with dve.Fori(1, KT) as t:
                ada_gemv(t, t)
            dve.wait_ge(cols_done, 1)
            link(dve.tensor_copy(aff_b, ps[:, 4, 0:KT]))
            dve.scalar_tensor_tensor(out=aff_a, in0=ps[:, 4, KT:2 * KT], scalar=1.0, in1=vec("pre_g0"),
                                     op0=ALU.add, op1=ALU.mult).then_inc(aff_ready, 1)
            dve.wait_ge(aff_ready, 1)
            hT_copies(0)

            dve.wait_ge(acc_init, 64)
            with dve.Fori(0, 4) as i:
                for u in range(2):
                    ada_gemv(4 * i + 2 * u, 4 * i + 2 * u + KT)
                    ada_gemv(4 * i + 2 * u + 1, 4 * i + 2 * u + 1 + KT)
                    dve.wait_ge(proj_free, block_base["sgu_v"] + 2 * i + u + 1)
                    for tb in range(TB):
                        v = dve.bn_stats(bn_st[:, tb, ds(2 * i + u, 1), :],
                                         v_sb[:, tb, ds(i * 2 * NB + u * NB, NB)])
                    v.then_inc(vstat_done, 1)
            dve.wait_ge(vstat_done, 8)
            for tb in range(TB):
                link(dve.bn_aggr(bn_mv[:, 2 * tb:2 * tb + 2], bn_st[:, tb, :, :]))
            dve.tensor_scalar(rms[:, 0:TB], bn_mv.rearrange("p (t c) -> p t c", c=2)[:, :, 1], EPS1, None, ALU.add
                              ).then_inc(ms_done, 1)
            inverse_root()
            for tb in range(TB):
                v = dve.tensor_scalar(v_sb[:, tb, :], v_sb[:, tb, :], bn_mv[:, 2 * tb:2 * tb + 1],
                                      rstd[:, tb:tb + 1], ALU.subtract, ALU.mult)
            v.then_inc(v_norm, 1)

            def gate_gain(n0):
                dve.wait_ge(postg_in, 16 * (n0 // 4 + 1))
                for q in range(4):
                    dve.wait_ge(gate_rows, n0 + q + 1)
                    blk = gate_g[:, q * NB:(q + 1) * NB]
                    dve.tensor_tensor(blk, ps[:, 5, :], blk, ALU.mult).then_inc(gate_read, 1)

            gate_gain(0)
            dve.wait_ge(cols_done, 2)
            dve.tensor_copy(aff_b, ps[:, 4, 0:KT]).then_inc(aff_ready, 1)

            def uz(n, first=False):
                if not first:
                    dve.wait_ge(mix_done, n)
                dve.tensor_tensor(w_cur, vec("w_s").rearrange("p (g s) -> p g s", g=SGU_G)[:, ds(GPB * n, GPB), :],
                                  cst("mask_sgu").rearrange("p (g s) -> p g s", g=1).to_broadcast([P, GPB, P]),
                                  ALU.mult).then_inc(wcur_done, 1)
                link_at(n, 0, dve.tensor_copy(b_cur, vec("b_s")[:, ds(GPB * n, GPB)]))
                for t in range(2):
                    ada_gemv(2 * n + t, 2 * n + t + 2 * KT)
                dve.wait_ge(mix_done, n + 1)
                dve.wait_ge(g_in, 16 * n + 16)
                if not first:
                    dve.wait_ge(yt_done, n)
                link_at(n, 1, dve.tensor_tensor(y_t, ps[:, 4:6, :],
                                                g_blk.rearrange("p (t n) -> p t n", t=1).to_broadcast([P, TB, NB]),
                                                ALU.mult))
                dve.wait_ge(proj_free, block_base["sgu_uz"] + 2 * n + 1)
                for g in range(GPB):
                    cols = slice(g * SGU_GD, (g + 1) * SGU_GD)
                    v = dve.scalar_tensor_tensor(out=y_t[:, :, cols], in0=y_t[:, :, cols], scalar=b_cur[:, g:g + 1],
                                                 in1=u_t[:, :, cols], op0=ALU.add, op1=ALU.mult)
                link_at(n, 2, v)
                dve.wait_ge(proj_free, block_base["sgu_uz"] + 2 * n + 2)
                dve.tensor_tensor(y_t, y_t, z_t, ALU.mult).then_inc(y_done, 1)

            uz_base = steps[0]

            def link_at(n, k, ins):
                ins.then_inc(dve_step, 1)
                dve.wait_ge(dve_step, uz_base + 3 * n + k + 1)

            dve.wait_ge(acc_init, 96)
            uz(0, first=True)
            with dve.Fori(1, 8) as n:
                uz(n)
            steps[0] += 3 * 8

            def copy_blocks(name):
                for b in range(4):
                    dve.wait_ge(w_used, block_done(name, b))
                    dve.wait_ge(ysq_done, TB * (copies[0] + 1))
                    copies[0] += 1
                    dve.tensor_copy(y_sb[:, :, b * NB:(b + 1) * NB], ps[:, 2 * (b % 2):2 * (b % 2) + 2, :]
                                    ).then_inc(proj_free, 1)

            copies = [0]

            def post_norm(idx):
                dve.wait_ge(proj_free, block_base[("sgu_out", "mla_out")[idx]] + 4)
                link(dve.tensor_reduce(rms[:, 0:TB], ysq.rearrange("p (t b) -> p t b", t=TB), AX, ALU.add))
                dve.tensor_scalar(rms[:, 0:TB], rms[:, 0:TB], 1.0 / D, EPS1, ALU.mult, ALU.add).then_inc(ms_done, 1)
                inverse_root()
                if idx == 0:
                    dve.wait_ge(x_back, 16)
                for tb in range(TB):
                    link(dve.scalar_tensor_tensor(out=y_sb[:, tb, :], in0=y_sb[:, tb, :], scalar=rstd[:, tb:tb + 1],
                                                  in1=gate_g, op0=ALU.mult, op1=ALU.mult))
                dve.tensor_tensor(x_sb, x_sb, y_sb, ALU.add).then_inc(x_ready, 1)

            copy_blocks("sgu_out")
            post_norm(0)
            if stages > 1:
                norm_x(1, EPS1)
                dve.wait_ge(cols_done, 3)
                dve.scalar_tensor_tensor(out=aff_a, in0=ps[:, 4, KT:2 * KT], scalar=1.0, in1=vec("pre_g1"),
                                         op0=ALU.add, op1=ALU.mult).then_inc(aff_ready, 1)
                dve.wait_ge(aff_ready, 3)
            if stages >= 2:
                hT_copies(1)
                dve.wait_ge(c_ssq, 2 * TB)
                for m, n in enumerate((QL, KVL)):
                    v = dve.tensor_scalar(rms[:, m * TB:(m + 1) * TB], c_sq[:, m * TB:(m + 1) * TB], 1.0 / n, EPS1,
                                          ALU.mult, ALU.add)
                v.then_inc(ms_done, 1)
                inverse_root(rstd)
                for m, (lo, n) in enumerate(((0, QL), (QL, KVL))):
                    for tb in range(TB):
                        blk = craw[:, tb, lo:lo + n]
                        dve.tensor_scalar(blk, blk, rstd[:, m * TB + tb:m * TB + tb + 1], None, ALU.mult)

                def rope(x1, x2, cos, sin, temps, last_sem):
                    a, b, c, d = temps
                    dve.tensor_tensor(a, x1, cos, ALU.mult)
                    dve.tensor_tensor(b, x2, sin, ALU.mult)
                    dve.tensor_tensor(c, x1, sin, ALU.mult)
                    link(dve.tensor_tensor(d, x2, cos, ALU.mult))
                    dve.tensor_tensor(x1, a, b, ALU.subtract)
                    dve.tensor_tensor(x2, c, d, ALU.add).then_inc(last_sem, 1)

                cos = cst("cos").rearrange("p (t n) -> p t n", t=TB)
                sin = cst("sin").rearrange("p (t n) -> p t n", t=TB)
                kr = craw[:, :, QL + KVL:QL + KVL + ROPE]
                rope(kr[:, :, 0:32], kr[:, :, 32:64], cos, sin,
                     [t[:, 0:TB * 32].rearrange("p (t n) -> p t n", t=TB) for t in rope_t], c_normed)
                gate_gain(4)
                dve.wait_ge(cT_turned, 1)
                for k in range(4):
                    dve.tensor_scalar(ckvT[:, k, :], ps[:, 4 + k // 2, (k % 2) * S:(k % 2 + 1) * S],
                                      vec("kv_g")[:, k:k + 1], None, ALU.mult)
                dve.tensor_copy(krT[0:ROPE, :], ps[0:ROPE, 2, 0:S]).then_inc(cT_dve, 1)

                b0 = block_base["mla_heads"]
                heads_base = [0]

                def step(p, k, ins):
                    ins.then_inc(dve_step, 1)
                    dve.wait_ge(dve_step, heads_base[0] + HEAD_STEPS * p + k + 1)

                HEAD_STEPS = 4

                def rope_q(p, par, k):
                    dve.wait_ge(proj_free, b0 + 2 * p + 1)
                    x = q_sb[par].rearrange("p t (h n) -> p t h n", h=HPP)
                    x1, x2 = x[:, :, :, NOPE:NOPE + 32], x[:, :, :, NOPE + 32:QKD]
                    a, b, c, d = (t.rearrange("p (t h n) -> p t h n", t=TB, h=HPP) for t in rope_t)
                    cs, sn = (t.rearrange("p t (h n) -> p t h n", h=1).to_broadcast([P, TB, HPP, 32])
                              for t in (cos, sin))
                    dve.tensor_tensor(a, x1, cs, ALU.mult)
                    dve.tensor_tensor(b, x2, sn, ALU.mult)
                    dve.tensor_tensor(c, x1, sn, ALU.mult)
                    v = dve.tensor_tensor(d, x2, cs, ALU.mult)
                    if k is None:
                        link(v)
                    else:
                        step(k[0], k[1], v)
                    dve.tensor_tensor(x1, a, b, ALU.subtract)
                    dve.tensor_tensor(x2, c, d, ALU.add).then_inc(q_roped, 1)

                def heads(i, par, last=False):
                    p = 2 * i + par
                    dve.wait_ge(turned_k, p + 1)
                    dve.tensor_copy(kT, ps[:, 7, :].rearrange("p (h s) -> p h s", h=HPP)).then_inc(kT_copied, 1)
                    for h in range(HPP):
                        dve.wait_ge(scores_done, 2 * p + h + 1)
                        dve.wait_ge(pt_done, CREDIT["pt_done"] + 2 * p + h - 1)
                        take_waits()
                        for tb in range(TB):
                            lo, hi = tb * P, tb * P + (tb + 1) * P
                            v = dve.tensor_tensor_reduce(prob[h][:, lo:hi], ps[:, 4 + h, lo:hi],
                                                         cst("mask_chunk")[:, lo:hi], MLA_SCALE, -3e38, ALU.add,
                                                         ALU.max, mx[:, h * TB + tb:h * TB + tb + 1])
                        step(p, h, v)
                        cols = slice(h * TB, (h + 1) * TB)
                        dve.tensor_scalar(nmx[:, cols], mx[:, cols], -1.0, None, ALU.mult).then_inc(max_done, 1)
                    dve.wait_ge(pt_done, CREDIT["pt_done"] + 2 * p + 2)
                    dve.wait_ge(pv_done, CREDIT["pv_done"] + p)
                    dve.tensor_copy(probT[1], ps[:, 7, 0:SCW]).then_inc(ptc_dve, 1)
                    dve.wait_ge(exp_done, 2 * p + 2)
                    step(p, 2, dve.reciprocal(rinv, sums))
                    if not last:
                        rope_q(p + 1, 1 - par, (p, 3))
                    else:
                        step(p, 3, dve.reciprocal(rinv, sums))
                    dve.wait_ge(pv_done, CREDIT["pv_done"] + p + 1)
                    dve.wait_ge(ogt_done, CREDIT["ogt_done"] + p)
                    for h in range(HPP):
                        for tb in range(TB):
                            n = h * TB + tb
                            v = dve.scalar_tensor_tensor(out=og[:, tb, h * VH:(h + 1) * VH],
                                                         in0=ps[:, 4, n * P:(n + 1) * P], scalar=rinv[:, n:n + 1],
                                                         in1=z_sb[:, tb, ds(p * HPP * VH + h * VH, VH)],
                                                         op0=ALU.mult, op1=ALU.mult)
                    v.then_inc(og_done, 1)

                dve.sem_inc(ptc_dve, CREDIT["ptc_dve"])
                dve.sem_inc(og_done, CREDIT["og_done"])
                dve.sem_inc(pt_done, CREDIT["pt_done"])
                dve.sem_inc(ogt_done, CREDIT["ogt_done"])
                rope_q(0, 0, None)
                heads_base[0] = steps[0]
                with dve.Fori(0, 3) as i:
                    for par in range(2):
                        heads(i, par)
                heads(3, 0)
                heads(3, 1, last=True)
                steps[0] += HEAD_STEPS * 8
                copy_blocks("mla_out")
                post_norm(1)
                if stages > 2:
                    norm_x(2, EPS2)
            def rotation_angles():
                two_pi = 2 * np.pi
                parts, rest = [], two_pi
                for bits in (8, 8, 8):
                    scale = 2.0 ** (bits - 1 - np.floor(np.log2(rest)))
                    part = np.floor(rest * scale) / scale
                    parts.append(float(part))
                    rest -= part
                parts.append(float(rest))
                dve.wait_ge(pos_in, 16)
                link(dve.tensor_copy(pos_f, pos_i[:, :]))
                for tb in range(TB):
                    v = dve.tensor_scalar(ang[:, tb * RD:(tb + 1) * RD], cst("inv_freq"), pos_f[:, tb:tb + 1], None,
                                          ALU.mult)
                link(v)
                magic = 1.5 * 2.0 ** 23
                link(dve.tensor_scalar(turns, ang, 1 / two_pi, magic, ALU.mult, ALU.add))
                link(dve.tensor_scalar(turns, turns, -magic, None, ALU.add))
                for n, part in enumerate(parts):
                    link(dve.scalar_tensor_tensor(out=red, in0=turns, scalar=-part, in1=red if n else ang,
                                                  op0=ALU.mult, op1=ALU.add))
                link(dve.tensor_scalar(red, red, 3.141592, -3.141592, ALU.min, ALU.max))
                link(dve.scalar_tensor_tensor(out=turns, in0=red, scalar=-1.0, in1=red, op0=ALU.mult, op1=ALU.max))
                dve.tensor_scalar(turns, turns, -1.0, float(np.pi / 2), ALU.mult, ALU.add).then_inc(trig_in, 1)
                dve.wait_ge(trig_done, 1)

            def rotate(x, heads, after=None):
                x = x.rearrange("p t (h n) -> p t h n", h=heads)
                x1, x2 = x[:, :, :, 0:RD], x[:, :, :, RD:2 * RD]
                a, b, c, d = (t[:, 0:TB * heads * RD].rearrange("p (t h n) -> p t h n", t=TB, h=heads)
                              for t in rope2_t)
                cs, sn = (t.rearrange("p (t h n) -> p t h n", t=TB, h=1).to_broadcast([P, TB, heads, RD])
                          for t in (cos2, sin2))
                dve.tensor_tensor(a, x1, cs, ALU.mult)
                dve.tensor_tensor(b, x2, sn, ALU.mult)
                dve.tensor_tensor(c, x1, sn, ALU.mult)
                (after or link)(dve.tensor_tensor(d, x2, cs, ALU.mult))
                dve.tensor_tensor(x1, a, b, ALU.subtract)
                return dve.tensor_tensor(x2, d, c, ALU.add)

            def kvz(m):
                for br in range(m.branches):
                    src = raw[br + (m.branches == 2)]
                    dve.wait_ge(proj_free, block_base["a_kvz" if m.branches == 1 else "b_kv"] + br + m.branches)
                    link(rotate(src[:, :, 0:NKV * HD], NKV))
                    for tb in range(TB):
                        v = dve.tensor_copy(k_dup[br][:, tb, :].rearrange("p (g e n) -> p g e n", g=NKV, e=2),
                                            src[:, tb, 0:NKV * HD].rearrange("p (g e n) -> p g e n", g=NKV, e=1)
                                            .to_broadcast([P, NKV, 2, HD]))
                    v.then_inc(m.kdup, 1)
                for br in range(m.branches):
                    dve.wait_ge(m.k_turned, br + 1)
                    dve.tensor_copy(kT_all[br][:, 2:4, :], ps[:, 5, :].rearrange("p (g s) -> p g s", g=2)
                                    ).then_inc(m.kT_dve, 1)

            def compress():
                for c, pos in enumerate(("pos_k", "pos_v")):
                    dve.wait_ge(c_copied, c + 1)
                    if c:
                        dve.wait_ge(w_used, chunk_base["b_cmp"] + CPB)
                    for a in range(2):
                        half = slice(a * CS, (a + 1) * CS)
                        v = None
                        for g in range(NKV):
                            src = kcT[c][0:HD, g, :].rearrange("p (n b) -> p n b", b=CS)[:, a:a + NCMP, :]
                            v = dve.tensor_tensor(unfold[0:HD, half, g, :], src.rearrange("p n b -> p b n"),
                                                  vec(pos)[0:HD, half].rearrange("p (b n) -> p b n", n=1)
                                                  .to_broadcast([HD, CS, NCMP]), ALU.add)
                    v.then_inc(unfolded, 1)
                dve.wait_ge(cmp_w2, 1)
                dve.tensor_copy(kcmp_all, ps[:, 6, 0:NKV * NCMP])
                dve.wait_ge(cmp_w2, 2)
                link(dve.tensor_copy(vcmp[0:NCMP, :], ps[0:NCMP, 7, 0:NKV * HD]))

            def groups(m):
                name, NU = m.name + "_q", m.units
                is_b = m.branches == 2
                b0 = block_base[name]
                GROUP_STEPS = NU + (2 if not is_b else 13) + 2
                mask = cst("mask_causal" if is_b else "mask_window")
                base, k_at = [0], [0]

                def mark(g):
                    def step(ins):
                        k_at[0] += 1
                        ins.then_inc(dve_step, 1)
                        dve.wait_ge(dve_step, base[0] + GROUP_STEPS * g + k_at[0])
                    return step

                def softmax(g, u, step):
                    h = u % HG
                    dve.wait_ge(m.scores, 1 + NU * g + u + 1)
                    dve.wait_ge(m.pt_done, NU * g + u + 1)
                    take_waits()
                    for tb in range(TB):
                        n = tb * HG + h
                        lo, hi = tb * P, tb * P + (tb + 1) * P
                        v = dve.tensor_tensor_reduce(prob4[u % 4][:, lo:hi], ps[:, 2 + u % 2, lo:hi], mask[:, lo:hi],
                                                     SCALE2, -3e38 if is_b else sink_grp[:, h:h + 1], ALU.add,
                                                     ALU.max, mx2[:, n:n + 1])
                    step(v)
                    dve.tensor_scalar(t8(nmx2)[:, :, h], t8(mx2)[:, :, h], -1.0, None, ALU.mult
                                      ).then_inc(m.max_done, 1)

                def finish(g, read, step):
                    br = read - is_b
                    den = sums2[br]
                    if is_b and read == 0:
                        dve.wait_ge(cmp_pv, g + 1)
                        den = sums2[2]
                    else:
                        dve.wait_ge(m.exp_done, NU * g + HG * (br + 1))
                        dve.wait_ge(m.pv_done, 2 + NU * g + HG * (br + 1))
                    if not is_b:
                        dve.wait_ge(m.sink_exp, g + 1)
                        step(dve.tensor_tensor(den, den, sink_e, ALU.add))
                    step(dve.reciprocal(coef, den))
                    if is_b:
                        step(dve.tensor_tensor(t8(coef), t8(coef), gates[:, :, ds(32 * read + HG * g, HG)], ALU.mult))
                    dst = o_tmp if is_b and read else o_grp
                    v4 = lambda ap: ap.rearrange("p t (h n) -> p t h n", h=HG)
                    o = dve.tensor_tensor(v4(dst), v4(ps[:, 6:8, :]),
                                          coef.rearrange("p (t h n) -> p t h n", t=TB, n=1)
                                          .to_broadcast([P, TB, HG, HD]), ALU.mult)
                    o.then_inc(m.o_read, 1)
                    dve.wait_ge(m.o_read, m.reads * (g + 1) + read + 1)
                    if is_b and read:
                        step(dve.tensor_tensor(o_grp, o_grp, o_tmp, ALU.add))
                    if read == m.reads - 1:
                        dve.tensor_tensor(o_grp, o_grp, z_sb[:, :, ds(g * HW, HW)], ALU.mult).then_inc(m.og_done, 1)

                def rope_q(g, after):
                    dve.wait_ge(proj_free, b0 + g + 1)
                    rotate(q_grp, HG, after).then_inc(m.q_roped, 1)

                def group(g, last=False):
                    k_at[0] = 0
                    step = mark(g)
                    dve.wait_ge(m.scores, NU * g + 1)
                    for br in range(m.branches):
                        v = dve.tensor_copy(kT_grp[br].rearrange("p (g s) -> p g s", g=1), kT_all[br][:, ds(g, 1), :])
                    if is_b:
                        v = dve.tensor_copy(kcmp_grp, kcmp_all[:, ds(g * NCMP, NCMP)])
                    else:
                        v = dve.tensor_copy(sink_grp, sinks[:, ds(g * HG, HG)])
                    v.then_inc(m.k_ready, 1)
                    dve.wait_ge(m.k_ready, g + 1)
                    dve.wait_ge(m.turned, 2 * g + 2)
                    dve.tensor_copy(qT_grp[:, 2:4, :], ps[:, 5, :].rearrange("p (j s) -> p j s", j=2)
                                    ).then_inc(m.qT_dve, 1)
                    if is_b:
                        pc = p_cmp.rearrange("p (t h n) -> p t h n", t=TB, h=HG)
                        cm = sums2[2]
                        dve.wait_ge(cmp_scores, g + 1)
                        half = HG // 2
                        for e in range(2):
                            v = dve.tensor_tensor(p_cmp.rearrange("p (t j e n) -> p t j e n", t=TB, j=half, e=2)[:, :, :, e, :],
                                                  ps[:, 6 + e, 0:TB * half * NCMP]
                                                  .rearrange("p (t j n) -> p t j n", t=TB, j=half),
                                                  cst("mask_cmp").rearrange("p (t j n) -> p t j n", t=TB, j=1)
                                                  .to_broadcast([P, TB, half, NCMP]), ALU.add)
                        step(v)
                        step(dve.tensor_reduce(cm, p_cmp.rearrange("p (m n) -> p m n", n=NCMP), AX, ALU.max))
                        step(dve.tensor_scalar(cm, cm, NEG / 100, None, ALU.max))
                        dve.tensor_tensor(pc, pc, cm.rearrange("p (t h n) -> p t h n", t=TB, n=1)
                                          .to_broadcast([P, TB, HG, NCMP]), ALU.subtract).then_inc(cmp_shifted, 1)
                        dve.tensor_tensor(v_bd[0:HG * NCMP].rearrange("p (h n) -> p h n", h=HG),
                                          ps[0:HG * NCMP, 6, 256:256 + HD].rearrange("p (h n) -> p h n", h=1)
                                          .to_broadcast([HG * NCMP, HG, HD]),
                                          cst("mask_bd")[0:HG * NCMP].rearrange("p (h n) -> p h n", h=HG),
                                          ALU.mult).then_inc(vbd_done, 1)
                    softmax(g, 0, step)
                    softmax(g, 1, step)
                    if is_b:
                        dve.wait_ge(cmp_exp, g + 1)
                        step(dve.tensor_reduce(cm, p_cmp.rearrange("p (m n) -> p m n", n=NCMP), AX, ALU.add))
                        step(dve.tensor_scalar(cm, cm, 1e-30, None, ALU.max))
                        finish(g, 0, step)
                    for u in range(NU):
                        if u % 2:
                            dve.wait_ge(m.pt_done, 4 + NU * g + u + 1)
                            dve.wait_ge(m.pv_done, NU * g + u + 1)
                            dve.tensor_copy(probT2[1], ps[:, 5, 0:SCW]).then_inc(m.ptc_dve, 1)
                        if u + 2 < NU:
                            softmax(g, u + 2, step)
                        if is_b and u == HG:
                            finish(g, 1, step)
                    if not is_b:
                        dve.wait_ge(m.max_done, 2 + NU * (g + 1))
                        dve.tensor_tensor(t8(sink_e), t8(nmx2), sink_grp.rearrange("p (t h) -> p t h", t=1)
                                          .to_broadcast([P, TB, HG]), ALU.add).then_inc(m.sink_in, 1)
                    if not last:
                        rope_q(g + 1, step)
                    finish(g, m.reads - 1, step)
                    dve.wait_ge(m.ogt_done, 2 * g + 2)
                    dve.tensor_copy(oT[:, ds(4 * g + 2, 2), :], ps[:, 5, :].rearrange("p (j s) -> p j s", j=2)
                                    ).then_inc(m.ogc_dve, 1)
                    while k_at[0] < GROUP_STEPS:
                        k_at[0] += 1
                        dve.sem_inc(dve_step, 1)

                for what, n in ((m.max_done, 2), (m.pt_done, 4), (m.pv_done, 2), (m.ptc_dve, 1), (m.scores, 1),
                                (m.ogc_dve, 1), (m.o_read, m.reads), (m.og_done, 1)):
                    dve.sem_inc(what, n)
                rope_q(0, None)
                base[0] = steps[0]
                with dve.Fori(0, NKV - 1) as g:
                    group(g)
                group(NKV - 1, last=True)
                steps[0] += GROUP_STEPS * NKV

            def residual(m):
                for b in range(4):
                    dve.wait_ge(w_used, block_done(f"{m.name}_out", b))
                    blk = x_sb[:, :, b * NB:(b + 1) * NB]
                    v = dve.tensor_tensor(blk, blk, ps[:, 2 * (b % 2):2 * (b % 2) + 2, :], ALU.add)
                    v.then_inc(proj_free, 1)
                dve.wait_ge(proj_free, block_base[f"{m.name}_out"] + 4)
                dve.sem_inc(x_ready, 1)

            for m, idx in ((ma, 2), (mb, 3)):
                if m is not None:
                    hT_copies(idx)
                    if idx == 2:
                        rotation_angles()
                    kvz(m)
                    if idx == 3:
                        compress()
                    groups(m)
                    residual(m)
                    if stages > idx + 1:
                        norm_x(idx + 1, EPS2, final=(idx == 3))


INPUTS = ("x", "ada_w", "ada_b", "post_g", "sgu_w_in", "sgu_norm_g", "sgu_w_out", "mla_w_in", "mla_w_uq",
          "mla_w_ukv", "mla_w_out", "final_norm_w_2", "a_w_in_2", "a_sinks_2", "a_w_out_2",
          "b_w_in_2", "b_cmp_k_w1_2", "b_cmp_k_w2_2", "b_cmp_v_w1_2",
          "b_cmp_v_w2_2", "b_w_out_2")


def kernel(**inputs):
    import concourse.bacc as bacc
    from concourse.bass_utils import run_bass_kernel_spmd

    nc = bacc.Bacc("TRN2", target_bir_lowering=False, num_devices=1)
    arrays = {n: np.ascontiguousarray(inputs[n]) for n in INPUTS}
    a = {n: np.asarray(v) for n, v in inputs.items()}

    def columns(v, rows=P):
        out = np.zeros((P, v.size // rows), np.float32)
        out[:rows] = v.reshape(-1, rows).T
        return out

    def rows(v):
        return np.concatenate([v, np.zeros((P - v.shape[0], v.shape[1]), np.float32)])

    vecs = {"c": columns(a["c"][0]), "pre_g0": columns(a["pre_g"][0]), "pre_g1": columns(a["pre_g"][1]),
            "norm_w0": columns(a["norm_w_2"][0]), "norm_w1": columns(a["norm_w_2"][1]),
            "q_g": columns(a["mla_q_norm_g"][0], QL_P), "kv_g": columns(a["mla_kv_norm_g"][0]),
            "b_s": a["sgu_b_s"][0].T, "w_s": a["sgu_w_s"][0].transpose(2, 0, 1).reshape(P, -1),
            "pos_k": rows(a["b_cmp_k_pos_2"][0].T), "pos_v": rows(a["b_cmp_v_pos_2"][0].T)}
    arrays["vecs"] = np.ascontiguousarray(np.concatenate([vecs[n] for n in VEC_COLS], 1))
    arrays["consts"] = shape_constants()
    arrays["pos"] = np.ascontiguousarray(a["positions_2"].reshape(TB, P).T)
    T = {n: nc.dram_tensor(n, v.shape, mybir.dt.from_np(v.dtype), kind="ExternalInput").ap()
         for n, v in arrays.items()}
    T["out"] = nc.dram_tensor("out", (1, S, D), F32, kind="ExternalOutput").ap()
    build(nc, T)
    r = run_bass_kernel_spmd(nc, [arrays], core_ids=[0])
    return r.results[0]["out"]
```

```python
from contextlib import ExitStack

import numpy as np

import concourse.bass as bass
from concourse import mybir
from concourse.alu_op_type import AluOpType as ALU

F32 = mybir.dt.float32
F32R = mybir.dt.float32r
I32 = mybir.dt.int32
ACT = mybir.ActivationFunctionType
AX = mybir.AxisListType.X
ds = bass.ds

P = 128
S = 256
TB = S // P
D = 2048
KT = D // P
NB = 512
CHUNK_KT = 4
SPLIT_KT = 2
RING = 4
CPB = KT // CHUNK_KT
SCPB = KT // SPLIT_KT
LEAD = RING - 1
HT_NEXT = KT // 2 + 1
SGU_W = 2 * D
SGU_G = 16
SGU_GD = SGU_W // SGU_G
GPB = NB // SGU_GD
EPS1, EPS2 = 1e-6, 1e-5
MLA_H, QL, KVL, NOPE, ROPE, VH = 16, 448, 512, 128, 64, 128
QKD = NOPE + ROPE
MLA_SCALE = float(QKD) ** -0.5
QL_P = QL // 4
HPP = 2
HD = 64
NKV = 4
HG = 8
HW = HG * HD
RD = 8
SCALE2 = float(HD) ** -0.5
NCMP = (S - 32) // 16 + 1
CL, CS, CH = 32, 16, 256
ADA_C = 512
ADA_N = D // ADA_C
NEG = -1e30
SCW = 3 * P
STAGES = 5

CONST_COLS = {"ident": P,  "mask_chunk": SCW, "mask_causal": SCW, "mask_window": SCW,
              "mask_cmp": TB * NCMP, "mask_sgu": P, "cos": TB * 32, "sin": TB * 32,
              "spread": HG * NCMP, "mask_bd": HW, "inv_freq": RD}
VEC_COLS = {"c": KT, "pre_g0": KT, "pre_g1": KT, "norm_w0": KT, "norm_w1": KT,
            "q_g": 4, "kv_g": 4, "b_s": SGU_G, "pos_k": CL // 2, "pos_v": CL // 2}


def offsets(cols):
    at, out = 0, {}
    for name, n in cols.items():
        out[name] = (at, n)
        at += n
    return out, at


CONST_AT, CONST_N = offsets(CONST_COLS)
VEC_AT, VEC_N = offsets(VEC_COLS)


def shape_constants():
    q, k = np.arange(P)[:, None], np.arange(P)[None, :]
    f = np.float32
    add = lambda ok: np.where(ok, 0.0, NEG).astype(f)
    zero = np.zeros((P, P), f)
    chunk = add(k // 64 <= q // 64)
    causal = add(k <= q)
    out = {"ident": np.eye(P, dtype=f),
           "mask_chunk": np.concatenate([chunk, zero, chunk], 1),
           "mask_causal": np.concatenate([causal, zero, causal], 1),
           "mask_window": np.concatenate([causal, add(k > q), causal], 1),
           "mask_sgu": (q // 64 <= k // 64).astype(f)}
    tok = np.arange(S).reshape(TB, P).T[:, :, None]
    last = np.arange(NCMP) * CS + CL - 1
    out["mask_cmp"] = add(last[None, None, :] <= tok).reshape(P, -1)
    inv = (f(10000.0) ** (-np.arange(0, ROPE, 2, dtype=f) / f(ROPE))).astype(f)
    ang = tok.astype(f) * inv[None, None, :]
    out["cos"] = np.cos(ang).reshape(P, -1)
    out["sin"] = np.sin(ang).reshape(P, -1)
    n, hn = np.arange(P)[:, None], np.arange(HG * NCMP)[None, :]
    out["spread"] = (n == hn % NCMP).astype(f)
    out["mask_bd"] = (n // NCMP == np.arange(HW)[None, :] // HD).astype(f)
    inv2 = (f(500000.0) ** (-np.arange(0, 2 * RD, 2, dtype=f) / f(2 * RD))).astype(f)
    out["inv_freq"] = np.broadcast_to(inv2, (P, RD))
    return np.ascontiguousarray(np.concatenate([out[n] for n in CONST_COLS], 1).astype(f))


def build(nc, T, stages=STAGES):
    es = ExitStack()
    with es:
        def sb(name, cols, dt=F32):
            return es.enter_context(nc.sbuf_tensor(name, [P, cols], dt))

        def sem(name):
            return es.enter_context(nc.semaphore(name))

        def sb_both(name, cols):
            at = -(-nc.sbuf_base // 32) * 32
            plain = sb(name, cols)
            return plain, nc.alloc_sbuf_tensor_at(name + "_r", [P, cols], F32R, offset=at)

        reg_a, reg_a_r = sb_both("reg_a", 2 * TB * D)
        reg_b, reg_b_r = sb_both("reg_b", 2 * TB * D)
        reg_h, reg_h_r = sb_both("reg_h", 2 * KT * S)
        reg_w, reg_w_r = sb_both("reg_w", RING * CHUNK_KT * NB)
        reg_raw = sb("reg_raw", RING * SPLIT_KT * NB)
        reg_c = sb("reg_c", 10465)
        cst_sb = sb("cst_sb", CONST_N)
        vec_sb = sb("vec_sb", VEC_N)
        small = sb("small", 640)
        ps = es.enter_context(nc.psum_tensor("ps", [P, 8, NB], F32))

        x_sb = reg_a[:, 0:TB * D].rearrange("p (t n) -> p t n", t=TB)
        y_sb = reg_a[:, TB * D:].rearrange("p (t n) -> p t n", t=TB)
        v_sb = reg_a[:, :].rearrange("p (t n) -> p t n", t=TB)
        x_sgu = reg_h[:, 0:TB * D].rearrange("p (t n) -> p t n", t=TB)
        y_sgu = reg_h[:, TB * D:].rearrange("p (t n) -> p t n", t=TB)
        kts = lambda ap: ap.rearrange("p (k s) -> p k s", s=S)
        hT_hi, hT_lo = kts(reg_h_r[:, 0:KT * S]), kts(reg_h_r[:, KT * S:])
        hT_lo_f, hT = kts(reg_h[:, KT * S:]), kts(reg_h[:, 0:KT * S])
        yT_hi = kts(reg_b_r[:, :])
        yT_lo = reg_a_r[:, :].rearrange("p (a n j s) -> p n a j s", a=2, j=2, s=S)
        oT_mla = (hT_hi, hT_lo)
        oT_mix = (kts(reg_b_r[:, 0:KT * S]), hT_lo)
        z_sb = reg_b[:, KT * S:].rearrange("p (t n) -> p t n", t=TB)
        ring = reg_w[:, :].rearrange("p (r k n) -> p r k n", r=RING, k=CHUNK_KT)
        raw_ring = reg_raw[:, :].rearrange("p (r k n) -> p r k n", r=RING, k=SPLIT_KT)
        split_ring = reg_w_r[:, :].rearrange("p (r e k n) -> p r e k n", r=RING, e=2, k=SPLIT_KT)
        ada0_buf = reg_b[:, :].rearrange("p (j n) -> p j n", j=4)
        ada_buf = reg_c[:, 0:4 * ADA_C].rearrange("p (j n) -> p j n", j=4)
        ada_acc = reg_c[:, 2048:6144]
        gate_g = sb("gate_g", D)

        def cst(name, lo=0, n=None):
            at, w = CONST_AT[name]
            return cst_sb[:, at + lo:at + lo + (w - lo if n is None else n)]

        def vec(name, lo=0, n=None):
            at, w = VEC_AT[name]
            return vec_sb[:, at + lo:at + lo + (w - lo if n is None else n)]

        small_at = [0]

        def sm(n):
            small_at[0] += n
            assert small_at[0] <= 640
            return small[:, small_at[0] - n:small_at[0]]

        ident = cst("ident")
        cond = sm(KT)
        wait_cell = sm(1)
        aff_a = sm(KT)
        aff_b = sm(KT)
        rms = sm(2 * TB)
        rstd = sm(2 * TB)
        ysq = sm(TB * 4)
        bn_mv = sm(TB * 2)
        last_gain = reg_h[:, 0:D]
        ones = sb("ones", P)
        diag = sb("diag", TB * P)[:, :].rearrange("p (t n) -> p t n", t=TB)
        xsq = sm(TB * 4)

        u_t = reg_c[:, 6144:7168].rearrange("p (t n) -> p t n", t=TB)
        z_t = reg_c[:, 7168:8192].rearrange("p (t n) -> p t n", t=TB)
        y_t = reg_c[:, 8192:9216].rearrange("p (t n) -> p t n", t=TB)
        g_blk = reg_c[:, 9216:9728]
        w_cur = reg_c[:, 9728:9984].rearrange("p (g n) -> p g n", g=GPB)
        b_cur = sm(GPB)
        sq_junk = reg_c[:, 9953:10465]
        bn_st = reg_c[:, 9984:9984 + TB * 8 * 6].rearrange("p (t n c) -> p t n c", t=TB, c=6)

        craw = reg_a[:, 4096:6144].rearrange("p (t n) -> p t n", t=TB)
        cqT = reg_b[:, 0:1024].rearrange("p (k s) -> p k s", s=S)
        ckvT = reg_b[:, 1024:2048].rearrange("p (k s) -> p k s", s=S)
        taken = [6144]

        def take(n):
            if taken[0] < 6144 or taken[0] + n > 9953:
                if taken[0] >= 6144:
                    taken[0] = 2048
                assert taken[0] + n <= 6144
            taken[0] += n
            return reg_c[:, taken[0] - n:taken[0]]

        rope_t = [take(TB * HPP * 32) for _ in range(4)]
        krT = take(S)
        q_sb = [take(TB * HPP * QKD).rearrange("p (t n) -> p t n", t=TB) for _ in range(2)]
        kv_sb = [reg_b[:, 2048 + m * TB * NB:2048 + (m + 1) * TB * NB].rearrange("p (t n) -> p t n", t=TB)
                 for m in range(2)]
        qT = take(HPP * S).rearrange("p (h s) -> p h s", h=HPP)
        qrT = take(HPP * S).rearrange("p (h s) -> p h s", h=HPP)
        kT = take(HPP * S).rearrange("p (h s) -> p h s", h=HPP)
        prob = [take(SCW) for _ in range(HPP)]
        probT = [take(SCW) for _ in range(HPP)]
        og = take(TB * HPP * VH).rearrange("p (t n) -> p t n", t=TB)
        c_sq = sm(2 * TB)
        mx = sm(HPP * TB)
        nmx = sm(HPP * TB)
        sums = sm(HPP * TB)
        rinv = sm(HPP * TB)

        cols = lambda reg, lo, n: reg[:, lo:lo + n]
        tn = lambda ap: ap.rearrange("p (t n) -> p t n", t=TB)
        raw = [tn(cols(reg_c, m * 1024, 1024)) for m in range(3)]
        kT_all = [cols(reg_c, 3072 + m * 1024, 1024).rearrange("p (g s) -> p g s", g=NKV) for m in range(2)]
        q_grp = tn(cols(reg_c, 5120, 1024))
        qT_grp = cols(reg_c, 6144, 1024).rearrange("p (j s) -> p j s", j=4)
        o_grp = tn(cols(reg_c, 7168, 1024))
        prob4 = [cols(reg_c, 8192 + m * SCW, SCW) for m in range(4)]
        kT_grp = [cols(reg_c, 9728 + m * S, S) for m in range(2)]
        scr = reg_a[:, TB * D:]
        probT2 = [cols(scr, m * SCW, SCW) for m in range(2)]
        o_tmp = tn(cols(scr, 768, 1024))
        rope2_t = [cols(scr, 1792 + m * 128, 128) for m in range(4)]
        p_cmp = cols(scr, 2304, TB * HG * NCMP)
        pT_cmp = cols(scr, 2544, S).rearrange("p (t n) -> p t n", t=TB)
        v_bd = cols(scr, 2800, HW)
        gates = tn(cols(scr, 3312, TB * 96))
        kcmp_all = cols(scr, 3504, NKV * NCMP)
        kcmp_grp = cols(reg_c, 10360, 2 * NCMP)
        vcmp = cols(scr, 3580, NKV * HD)
        w2k = cols(scr, 3836, 256).rearrange("p (k n) -> p k n", k=2)
        w2v = cols(scr, 2544, 128).rearrange("p (k n) -> p k n", k=2)
        hidT = [ap.rearrange("p (k n) -> p k n", k=2)
                for ap in (cols(reg_c, 10240, 120), sb("hidden_v", 120)[:, :])]
        k_dup = [tn(cols(reg_c, 5120 + m * 1024, 1024)) for m in range(2)]
        kcT = [cols(r_, lo, 1024).rearrange("p (g s) -> p g s", g=NKV) for r_, lo in ((reg_c, 7168), (scr, 768))]
        unfold = [cols(reg_c, 8192 + m * 960, 960).rearrange("p (k g n) -> p k g n", k=CL // 2, g=NKV) for m in range(2)]
        kc_dup = tn(gate_g[:, :])
        w1_ring = reg_raw[:, :].rearrange("p (r k n) -> p r k n", r=RING, k=4)
        pos_i = es.enter_context(nc.sbuf_tensor("pos_i", [P, TB], I32))
        pos_f = sm(TB)
        ang = sm(TB * RD)
        red = sm(TB * RD)
        turns = sm(TB * RD)
        cos2 = sm(TB * RD)
        sin2 = sm(TB * RD)
        sinks = sm(NKV * HG)
        sink_grp = sm(HG)
        sink_e = sm(TB * HG)
        mx2 = sm(TB * HG)
        nmx2 = sm(TB * HG)
        sums2 = [sm(TB * HG) for _ in range(3)]
        coef = sm(TB * HG)
        t8 = lambda ap: ap.rearrange("p (t h) -> p t h", t=TB)

        consts_in = sem("consts_in")
        x_in = sem("x_in")
        x_back = sem("x_back")
        ones_set = sem("ones_set")
        cond_done = sem("cond_done")
        w_full = [sem(f"w_full{s}") for s in range(RING)]
        raw_full = [sem(f"raw_full{s}") for s in range(RING)]
        hi_done = sem("hi_done")
        lo_done = sem("lo_done")
        w_used = sem("w_used")
        hT_up = sem("hT_up")
        hT_whole = sem("hT_whole")
        ada0_full = [sem(f"ada0_full{j}") for j in range(4)]
        ada0_used = sem("ada0_used")
        proj_free = sem("proj_free")
        ada_full = [sem(f"ada_full{j}") for j in range(4)]
        ada_used = sem("ada_used")
        acc_zero = sem("acc_zero")
        acc_init = sem("acc_init")
        cols_done = sem("cols_done")
        aff_ready = sem("aff_ready")
        gate_rows = sem("gate_rows")
        gate_read = sem("gate_read")
        gate_ready = sem("gate_ready")
        postg_in = sem("postg_in")
        dve_step = sem("dve_step")
        act_step = sem("act_step")
        x_blk = sem("x_blk")
        out_ready = sem("out_ready")
        ssq_done = sem("ssq_done")
        ms_done = sem("ms_done")
        rms_done = sem("rms_done")
        xn_done = sem("xn_done")
        xT_done = sem("xT_done")
        xT_free = [sem("xT_free0"), sem("xT_free1")]
        out_in = sem("out_in")
        gain_in = sem("gain_in")
        v_norm = sem("v_norm")
        vstat_done = sem("vstat_done")
        g_in = sem("g_in")
        wcur_in = sem("wcur_in")
        wcur_done = sem("wcur_done")
        mix_done = sem("mix_done")
        y_done = sem("y_done")
        yt_done = sem("yt_done")
        yT_up = sem("yT_up")
        yT_done = sem("yT_done")
        craw_done = sem("craw_done")
        c_ssq = sem("c_ssq")
        c_normed = sem("c_normed")
        cT_turned = sem("cT_turned")
        cT_act = sem("cT_act")
        cT_dve = sem("cT_dve")
        q_roped = sem("q_roped")
        turned_q = sem("turned_q")
        turned_k = sem("turned_k")
        turned_r = sem("turned_r")
        qT_copied = sem("qT_copied")
        kT_copied = sem("kT_copied")
        scores_done = sem("scores_done")
        max_done = sem("max_done")
        exp_done = sem("exp_done")
        pt_done = sem("pt_done")
        ptc_act = sem("ptc_act")
        ptc_dve = sem("ptc_dve")
        pv_done = sem("pv_done")
        og_done = sem("og_done")
        ogt_done = sem("ogt_done")
        ogc_up = sem("ogc_up")
        ogc_done = sem("ogc_done")
        pos_in = sem("pos_in")
        trig_in = sem("trig_in")
        trig_done = sem("trig_done")
        sinks_in = sem("sinks_in")
        w2_in = sem("w2_in")

        class Mixer:

            def __init__(self, name, branches):
                self.name, self.branches, self.units = name, branches, branches * HG
                self.reads = branches + (name == "b")
                self.kdup = sem(f"{name}_kdup")
                self.k_turned = sem(f"{name}_k_turned")
                self.kT_act = sem(f"{name}_kT_act")
                self.kT_dve = sem(f"{name}_kT_dve")
                self.q_roped = sem(f"{name}_q_roped")
                self.turned = sem(f"{name}_turned")
                self.qT_act = sem(f"{name}_qT_act")
                self.qT_dve = sem(f"{name}_qT_dve")
                self.k_ready = sem(f"{name}_k_ready")
                self.scores = sem(f"{name}_scores")
                self.max_done = sem(f"{name}_max_done")
                self.exp_done = sem(f"{name}_exp_done")
                self.pt_done = sem(f"{name}_pt_done")
                self.ptc_act = sem(f"{name}_ptc_act")
                self.ptc_dve = sem(f"{name}_ptc_dve")
                self.pv_done = sem(f"{name}_pv_done")
                self.o_read = sem(f"{name}_o_read")
                self.og_done = sem(f"{name}_og_done")
                self.ogt_done = sem(f"{name}_ogt_done")
                self.ogc_up = sem(f"{name}_ogc_up")
                self.ogc_done = sem(f"{name}_ogc_done")
                self.sink_in = sem(f"{name}_sink_in")
                self.sink_exp = sem(f"{name}_sink_exp")

        ma = mb = None
        if stages >= 3:
            ma = Mixer("a", 1)
        if stages >= 4:
            mb = Mixer("b", 2)
        cmp_scores = sem("cmp_scores")
        cmp_shifted = sem("cmp_shifted")
        cmp_exp = sem("cmp_exp")
        cmp_turned = sem("cmp_turned")
        cmp_copied = sem("cmp_copied")
        vbd_done = sem("vbd_done")
        cmp_pv = sem("cmp_pv")
        c_turned = sem("c_turned")
        c_copied = sem("c_copied")
        unfolded = sem("unfolded")
        w1_full = [sem(f"w1_full{j}") for j in range(RING)]
        w1_used = sem("w1_used")
        hid_done = sem("hid_done")
        gelu_done = sem("gelu_done")
        cmp_w2 = sem("cmp_w2")
        cmp_kv = sem("cmp_kv")
        gates_done = sem("gates_done")
        ysq_done = sem("ysq_done")

        chunk_base, block_base, chunks_per, split_base, whole_base = {}, {}, {}, {}, {}
        c_at = b_at = s_at = 0
        for name, blocks, chunks, split in (
                ("sgu_v", 8, SCPB, 1), ("sgu_uz", 16, SCPB, 1), ("sgu_out", 4, 2 * SCPB, 1),
                ("mla_in", 6, SCPB, 1), ("mla_heads", 16, 1, 0), ("mla_out", 4, SCPB, 1),
                ("a_kvz", 5, SCPB, 1), ("a_q", 4, CPB, 0), ("a_out", 4, SCPB, 1),
                ("b_kv", 4, SCPB, 1), ("b_z", 4, SCPB, 1), ("b_q", 4, CPB, 0),
                ("b_out", 4, SCPB, 1)):
            chunk_base[name], block_base[name], chunks_per[name], split_base[name] = c_at, b_at, chunks, s_at
            whole_base[name] = c_at - s_at
            n_chunks = blocks * chunks
            c_at += n_chunks
            s_at += n_chunks * split
            b_at += blocks
            assert c_at % RING == 0

        def x_final(idx, b):
            if idx <= 2:
                return x_blk, 4 * (idx - 1) + b + 1
            return proj_free, block_base[("a_out", "b_out")[idx - 3]] + b + 1

        more_after = {"sgu_out": stages >= 2, "mla_out": stages >= 3, "a_out": stages >= 4}

        def block_done(name, b):
            return (b + 1) * chunks_per[name] + chunk_base[name]

        def filled(c_base, c):
            return 16 * (c_base // RING + c // RING + 1)

        def filled_at(c_base, c, j):
            if isinstance(c, int):
                return filled(c_base, c + j)
            return c * 4 + (16 * (c_base // RING + j // RING + 1))

        CREDIT = {"ptc_act": 1, "ptc_dve": 1, "ogc_done": 1, "og_done": 1, "ada_used": ADA_N, "pt_done": 2, "pv_done": 1,
                  "ogt_done": 1}

        block = es.enter_context(nc.Block())

        @block.sync
        def _(sp):
            sp.dma_start(cst_sb[:, :], T["consts"]).then_inc(consts_in, 16)
            sp.dma_start(vec_sb[:, :], T["vecs"]).then_inc(consts_in, 16)
            sp.dma_start(x_sb, T["x"][0].rearrange("(t p) n -> p t n", p=P)).then_inc(x_in, 16)

            def chunk(c, src, rows=P, slot=None, dst=None):
                sp.wait_ge(w_used, c - RING + 1)
                if dst is None:
                    dst = ring[0:rows, slot, :, 0:src.shape[-1]]
                    src = src.rearrange("(k p) n -> p k n", p=rows)
                sp.dma_start(dst, src).then_inc(w_full[slot], 16)

            def raw_chunk(name, c, src, slot, first=False):
                if not first:
                    sp.wait_ge(lo_done, c + (split_base[name] - RING + 1))
                sp.dma_start(raw_ring[:, slot, :, 0:src.shape[-1]], src.rearrange("(k p) n -> p k n", p=P)
                             ).then_inc(raw_full[slot], 16)

            def stream(name, n0, n1, w, col0, cpb=SCPB, width=NB):
                def body(n):
                    for j in range(cpb):
                        raw_chunk(name, cpb * n + j, w[j * 256:(j + 1) * 256, ds(col0 + n * NB, width)], j % RING)
                if n1 - n0 == 1:
                    body(n0)
                else:
                    with sp.Fori(n0, n1) as i:
                        body(i)

            def stream_whole(name, w, between=None):
                def body(n):
                    for j in range(CPB):
                        chunk(chunk_base[name] + CPB * n + j, w[j * 512:(j + 1) * 512, ds(n * NB, NB)], slot=j)

                body(0)
                if between is not None:
                    between()
                with sp.Fori(1, 4) as n:
                    body(n)

            w_in = T["sgu_w_in"][0]
            for j in range(RING):
                raw_chunk("sgu_v", j, w_in[j * 256:(j + 1) * 256, SGU_W:SGU_W + NB], j, first=True)

            def ada0_tile(t, us, first=False):
                for u in us:
                    for m in range(2):
                        q = 2 * u + m
                        if not first:
                            sp.wait_ge(ada0_used, 4 * t + q - 3)
                        sp.dma_start(ada0_buf[:, q, :], T["ada_w"][0][ds((2 * t + u) * P, P), m * D:(m + 1) * D]
                                     ).then_inc(ada0_full[q], 16)

            ada0_tile(0, range(2), first=True)
            with sp.Fori(1, KT // 2) as t:
                ada0_tile(t, range(2))
            sp.dma_start(pos_i[:, :], T["pos"]).then_inc(pos_in, 16)
            sp.dma_start(sinks, T["a_sinks_2"][0:1, :].to_broadcast([P, NKV * HG])).then_inc(sinks_in, 16)
            for j in range(RING, SCPB):
                raw_chunk("sgu_v", j, w_in[j * 256:(j + 1) * 256, SGU_W:SGU_W + NB], j % RING)
            stream("sgu_v", 1, 8, w_in, SGU_W)

            def uz_block(n):
                if not (isinstance(n, int) and n == 0):
                    sp.wait_ge(mix_done, n)
                sp.dma_start(w_cur, T["w_s"][:, ds(n * GPB * P, GPB * P)].rearrange("p (g n) -> p g n", g=GPB)
                             ).then_inc(wcur_in, 16)
                for part in range(2):
                    if part:
                        if not (isinstance(n, int) and n == 0):
                            sp.wait_ge(y_done, n)
                        sp.dma_start(g_blk, T["sgu_norm_g"][0:1, ds(n * NB, NB)].to_broadcast([P, NB])
                                     ).then_inc(g_in, 16)
                    for j in range(SCPB):
                        raw_chunk("sgu_uz", 2 * SCPB * n + part * SCPB + j,
                                  w_in[j * 256:(j + 1) * 256, ds(part * 2 * SGU_W + n * NB, NB)], j % RING)

            uz_block(0)
            with sp.Fori(1, 8) as n:
                uz_block(n)
            stream("sgu_out", 0, 4, T["sgu_w_out"][0], 0, cpb=2 * SCPB)
            if stages >= 2:
                stream("mla_in", 0, 6, T["mla_w_in"][0], 0)
                with sp.Fori(0, 4) as i:
                    for u in range(2):
                        pair = 2 * i + u
                        chunk(chunk_base["mla_heads"] + 2 * pair, T["mla_w_uq"][0][:, ds(pair * HPP * QKD, HPP * QKD)],
                              rows=QL_P, slot=2 * u)
                        chunk(chunk_base["mla_heads"] + 2 * pair + 1,
                              T["mla_w_ukv"][0][:, ds(pair * NB, NB)], slot=2 * u + 1)
                stream("mla_out", 0, 4, T["mla_w_out"][0], 0)
            if stages >= 3:
                w = T["a_w_in_2"][0]
                stream("a_kvz", 0, 5, w, D)
                stream_whole("a_q", w)
                stream("a_out", 0, 4, T["a_w_out_2"][0], 0)
            if stages >= 4:
                w = T["b_w_in_2"][0]
                stream("b_kv", 0, 3, w, D)
                stream("b_kv", 3, 4, w, D, width=96)
                stream("b_z", 0, 4, w, D + 6 * NKV * HD + 96)
                w2 = T["b_cmp_k_w2_2"][0].rearrange("(k p) n -> p k n", p=P)
                for m in range(2):
                    sp.dma_start(w2k[:, :, m * HD:(m + 1) * HD], w2).then_inc(w2_in, 16)
                sp.dma_start(w2v, T["b_cmp_v_w2_2"][0].rearrange("(k p) n -> p k n", p=P)).then_inc(w2_in, 16)

                def w1(m, name):
                    for j in range(RING):
                        if m:
                            sp.wait_ge(w1_used, j + 1)
                        else:
                            sp.wait_ge(lo_done, split_base["b_out"] - RING + 1 + j)
                        sp.dma_start(w1_ring[:, j], T[name][0][j * 512:(j + 1) * 512, :]
                                     .rearrange("(k p) n -> p k n", p=P)).then_inc(w1_full[j], 16)

                w1(0, "b_cmp_k_w1_2")
                stream_whole("b_q", w, between=lambda: w1(1, "b_cmp_v_w1_2"))
                sp.wait_ge(w1_used, 2 * RING)
                stream("b_out", 0, 4, T["b_w_out_2"][0], 0)
            if stages < 5:
                sp.wait_ge(*x_final(stages, 3))
            for tb in range(TB):
                if stages == 5:
                    sp.wait_ge(out_ready, tb + 1)
                sp.dma_start(T["out"][0][tb * P:(tb + 1) * P, :], (x_sb if stages < 5 else y_sb)[:, tb, :]
                             ).then_inc(out_in, 16)
            sp.wait_ge(out_in, 16 * TB)


        ADA_STAGES = ((0, 2 * D, 1), (1, 0, 0), (1, D, 1), (1, 2 * D, 0))

        @block.gpsimd
        def _(pool):
            pool.memset(ones[:, :], 1.0).then_inc(ones_set, 1)

            def ada_chunks(stage, t):
                layer, col, _ = ADA_STAGES[stage]
                T_ = t + KT * stage
                for j in range(ADA_N):
                    if not (isinstance(T_, int) and T_ == 0):
                        pool.wait_ge(ada_used, ADA_N * T_ + (j + 1))
                    pool.dma_start(ada_buf[:, j, :],
                                   T["ada_w"][layer][ds(t * P, P), col + j * ADA_C:col + (j + 1) * ADA_C]
                                   ).then_inc(ada_full[j], 16)

            zeroed = [0]

            def init_acc(half, layer, col):
                acc = ada_acc[:, half * D:(half + 1) * D]
                pool.memset(acc, 0.0).then_inc(acc_zero, 1)
                zeroed[0] += 1
                pool.wait_ge(acc_zero, zeroed[0])
                pool.dma_start(acc[0:1, :], T["ada_b"][layer:layer + 1, col:col + D]).then_inc(acc_init, 16)

            init_acc(0, 0, 0)
            init_acc(1, 0, D)
            pool.dma_start(gate_g[:, :], T["post_g"][0:1, :].to_broadcast([P, D])).then_inc(postg_in, 16)
            ada_chunks(0, 0)
            for stage, (layer, col, half) in enumerate(ADA_STAGES):
                if stage < 2:
                    pool.wait_ge(cols_done, 1)
                elif stage == 2:
                    pool.wait_ge(gate_rows, 4)
                else:
                    pool.wait_ge(cols_done, 2)
                init_acc(half, layer, col)
                with pool.Fori(0 if stage else 1, KT) as t:
                    ada_chunks(stage, t)
            pool.wait_ge(w_used, block_done("sgu_uz", 15))
            pool.dma_start(x_sgu, T["x"][0].rearrange("(t p) n -> p t n", p=P)).then_inc(x_back, 16)
            if stages >= 2:
                pool.wait_ge(proj_free, block_base["sgu_out"] + 4)
                pool.dma_start(gate_g[:, :], T["post_g"][1:2, :].to_broadcast([P, D])).then_inc(postg_in, 16)
            if stages >= 5:
                pool.wait_ge(w_used, block_done("b_q", NKV - 1))
                pool.dma_start(last_gain, T["final_norm_w_2"].rearrange("(a n) -> a n", a=1).to_broadcast([P, D])
                               ).then_inc(gain_in, 16)

        N_NORMS = min(stages + 1, 5)

        @block.tensor
        def _(pe):
            pe.wait_ge(consts_in, 32)
            pe.wait_ge(ones_set, 1)

            def gemm_k(k, lhs, bank, c_base, c, n_k, width=NB, rows=P):
                j = k // CHUNK_KT
                slot = (c_base + c + j) % RING if isinstance(c, int) else j % RING
                if k % CHUNK_KT == 0:
                    pe.wait_ge(w_full[slot], filled_at(c_base, c, j))
                for tb in range(TB):
                    mm = pe.matmul(ps[:, bank + tb, 0:width], lhs[0:rows, k, tb * P:(tb + 1) * P],
                                   ring[0:rows, slot, k % CHUNK_KT, 0:width], start=(k == 0), stop=(k == n_k - 1))
                if k % CHUNK_KT == CHUNK_KT - 1:
                    mm.then_inc(w_used, 1)

            def gemm(lhs, bank, c_base, c, n_k=KT, width=NB, rows=P):
                for k in range(n_k):
                    gemm_k(k, lhs, bank, c_base, c, n_k, width, rows)

            def gemm_split(hi, lo, bank, name, c, n_k=KT, width=NB, norm=None):
                for k in range(n_k):
                    j = k // SPLIT_KT
                    if k % SPLIT_KT == 0:
                        pe.wait_ge(lo_done, c + (split_base[name] + j + 1))
                        if norm is not None:
                            pe.wait_ge(xT_free[j % 2], norm * KT // 4 + j // 2 + 1)
                    w_hi, w_lo = (split_ring[:, j % RING, e, k % SPLIT_KT, 0:width] for e in range(2))
                    for tb in range(TB):
                        out = ps[:, bank + tb, 0:width]
                        pe.matmul(out, hi(k, tb), w_hi, start=(k == 0), stop=False)
                        pe.matmul(out, hi(k, tb), w_lo, start=False, stop=False)
                        mm = pe.matmul(out, lo(k, tb), w_hi, start=False, stop=(k == n_k - 1))
                    if k % SPLIT_KT == SPLIT_KT - 1:
                        mm.then_inc(w_used, 1)
                        if norm is not None and j + 2 < KT // 2:
                            norm_transpose(norm, j + 2)

            def parts(pair):
                return [lambda k, tb, t=t: t[:, k, tb * P:(tb + 1) * P] for t in pair]

            hT_parts = parts((hT_hi, hT_lo))
            yT_parts = (parts((yT_hi, yT_hi))[0],
                        lambda k, tb: yT_lo[:, k // 4, k % 4 // 2, k % 2, tb * P:(tb + 1) * P])

            def norm_transpose(idx, kp):
                n = idx * KT // 2 + kp
                if n >= 2:
                    pe.wait_ge(xT_free[kp % 2], n // 2)
                for k in range(2):
                    for tb in range(TB):
                        f = (2 * kp + k) * P
                        mm = pe.matmul(ps[:, 6 + kp % 2, k * S + tb * P:k * S + (tb + 1) * P],
                                       x_sb[:, tb, f:f + P], diag[:, tb, :], start=True, stop=True)
                mm.then_inc(xT_done, 1)

            def norm_start(idx):
                pe.wait_ge(xn_done, idx + 1)
                norm_transpose(idx, 0)
                norm_transpose(idx, 1)

            def ada_columns(n_cols, acc_lo, at):
                for f in range(n_cols):
                    mm = pe.matmul(ps[:, 4, at + f:at + f + 1], ada_acc[:, acc_lo + f * P:acc_lo + (f + 1) * P],
                                   ones[:, 0:1], start=True, stop=True)
                return mm

            def gate_row_sums(acc_lo):
                for q in range(4):
                    pe.matmul(ps[:, 4 + q, :], ones[:, :], ada_acc[:, acc_lo + q * NB:acc_lo + (q + 1) * NB],
                              start=True, stop=True).then_inc(gate_rows, 1)

            pe.wait_ge(ada0_used, 2 * KT)
            ada_columns(2 * KT, 0, 0).then_inc(cols_done, 1)
            norm_start(0)

            def v_blocks(i, first=False):
                for u in range(2):
                    if not first:
                        pe.wait_ge(proj_free, 2 * i + u - 1)
                    gemm_split(*hT_parts, 2 * u, "sgu_v", 2 * SCPB * i + SCPB * u, norm=0 if first and not u else None)

            v_blocks(0, first=True)
            with pe.Fori(1, 4) as i:
                v_blocks(i)
            pe.wait_ge(ada_used, CREDIT["ada_used"] + ADA_N * KT)
            for bank in range(2):
                pe.wait_ge(xT_free[bank], KT // 4)
            gate_row_sums(D)

            def mix(n):
                pe.wait_ge(wcur_done, n + 1)
                for tb in range(TB):
                    for g in range(GPB):
                        mm = pe.matmul(ps[:, 4 + tb, g * SGU_GD:(g + 1) * SGU_GD], w_cur[:, g, :],
                                       v_sb[:, tb, ds(n * NB + g * SGU_GD, SGU_GD)], start=True, stop=True)
                mm.then_inc(mix_done, 1)

            def y_transposes(n):
                pe.wait_ge(y_done, n + 1)
                if not (isinstance(n, int) and n == 0):
                    pe.wait_ge(yT_done, n)
                for tb in range(TB):
                    for k in range(NB // P):
                        mm = pe.transpose(ps[:, 6 + tb, k * P:(k + 1) * P], y_t[:, tb, k * P:(k + 1) * P], ident)
                mm.then_inc(yt_done, 1)

            def uz(n, first=False):
                b0 = block_base["sgu_uz"]
                if not first:
                    pe.wait_ge(proj_free, b0 + 2 * n - 1)
                gemm_split(*hT_parts, 0, "sgu_uz", 2 * SCPB * n)
                if not first:
                    y_transposes(n - 1)
                mix(n)
                if not first:
                    pe.wait_ge(proj_free, b0 + 2 * n)
                gemm_split(*hT_parts, 2, "sgu_uz", 2 * SCPB * n + SCPB)

            pe.wait_ge(proj_free, block_base["sgu_uz"])
            pe.wait_ge(v_norm, 1)
            pe.wait_ge(gate_read, 4)
            uz(0, first=True)
            with pe.Fori(1, 8) as n:
                uz(n)
            y_transposes(7)

            pe.wait_ge(yT_done, 8)
            pe.wait_ge(ada_used, CREDIT["ada_used"] + 3 * KT * ADA_N)
            ada_columns(2 * KT, 0, 0).then_inc(cols_done, 1)
            pe.wait_ge(proj_free, block_base["sgu_out"])
            with pe.Fori(0, 2) as i:
                for u in range(2):
                    pe.wait_ge(proj_free, block_base["sgu_out"] + 2 * i + max(u - 1, 0))
                    gemm_split(*yT_parts, 2 * u, "sgu_out", 4 * SCPB * i + 2 * SCPB * u, n_k=2 * KT)
            if stages >= 2:

                def in_blocks(name, i, first=False):
                    for u in range(2):
                        if not first:
                            pe.wait_ge(proj_free, block_base[name] + 2 * i + u - 1)
                        gemm_split(*hT_parts, 2 * u, name, 2 * SCPB * i + SCPB * u, norm=1 if first and not u else None)

                norm_start(1)
                pe.wait_ge(proj_free, block_base["mla_in"])
                in_blocks("mla_in", 0, first=True)
                with pe.Fori(1, 3) as i:
                    in_blocks("mla_in", i)
                pe.wait_ge(ada_used, CREDIT["ada_used"] + 4 * KT * ADA_N)
                pe.wait_ge(aff_ready, 2)
                for bank in range(2):
                    pe.wait_ge(xT_free[bank], 2 * KT // 4)
                gate_row_sums(0)

                pe.wait_ge(c_normed, 1)
                pe.wait_ge(proj_free, block_base["mla_heads"])
                pe.wait_ge(gate_read, 8)
                for k in range(4):
                    for tb in range(TB):
                        at = (k % 2) * S + tb * P
                        pe.transpose(ps[0:QL_P, 6 + k // 2, at:at + P], craw[:, tb, k * QL_P:(k + 1) * QL_P], ident)
                        pe.transpose(ps[:, 4 + k // 2, at:at + P],
                                     craw[:, tb, QL + k * P:QL + (k + 1) * P], ident)
                for tb in range(TB):
                    mm = pe.transpose(ps[0:ROPE, 2, tb * P:(tb + 1) * P], craw[:, tb, QL + KVL:QL + KVL + ROPE], ident)
                mm.then_inc(cT_turned, 1)
                pe.wait_ge(cT_act, 1)
                pe.wait_ge(cT_dve, 1)

                c0, b0 = chunk_base["mla_heads"], block_base["mla_heads"]

                def q_gemm(pair, par):
                    for k in range(4):
                        gemm_k4(k, cqT, 0, pair, 2 * par, HPP * QKD, QL_P)

                def kv_gemm(pair, par, ks=range(4)):
                    for k in ks:
                        gemm_k4(k, ckvT, 2, pair, 2 * par + 1, NB, P)

                def gemm_k4(k, lhs, bank, pair, slot, width, rows):
                    if k == 0:
                        pe.wait_ge(w_full[slot], pair_filled(pair))
                    for tb in range(TB):
                        mm = pe.matmul(ps[:, bank + tb, 0:width], lhs[0:rows, k, tb * P:(tb + 1) * P],
                                       ring[0:rows, slot, k, 0:width], start=(k == 0), stop=(k == 3))
                    if k == 3:
                        mm.then_inc(w_used, 1)

                def pair_filled(pair):
                    i, par = pair
                    return 16 * (whole_base["mla_heads"] // RING + 1) + 16 * i

                def heads(i, par, last=False):
                    p = 2 * i + par
                    pe.wait_ge(proj_free, b0 + 2 * p + 2)
                    pe.wait_ge(q_roped, p + 1)
                    pe.wait_ge(ptc_act, CREDIT["ptc_act"] + p)
                    pe.wait_ge(ptc_dve, CREDIT["ptc_dve"] + p)
                    for h in range(HPP):
                        for tb in range(TB):
                            at = h * S + tb * P
                            mm = pe.transpose(ps[:, 6, at:at + P], q_sb[par][:, tb, h * QKD:h * QKD + NOPE], ident)
                    mm.then_inc(turned_q, 1)
                    for h in range(HPP):
                        for tb in range(TB):
                            at = h * S + tb * P
                            mm = pe.transpose(ps[:, 7, at:at + P], kv_sb[par][:, tb, h * S:h * S + NOPE], ident)
                    mm.then_inc(turned_k, 1)
                    pe.wait_ge(consts_in, 32)
                    pe.wait_ge(ogc_done, CREDIT["ogc_done"] + p)
                    for h in range(HPP):
                        for tb in range(TB):
                            at = h * S + tb * P
                            mm = pe.transpose(ps[0:ROPE, 5, at:at + P],
                                              q_sb[par][:, tb, h * QKD + NOPE:(h + 1) * QKD], ident)
                    mm.then_inc(turned_r, 1)
                    pe.wait_ge(kT_copied, p + 1)
                    pe.wait_ge(qT_copied, 2 * p + 2)
                    pe.wait_ge(og_done, CREDIT["og_done"] + p)
                    for h in range(HPP):
                        for tb in range(TB):
                            out = ps[:, 4 + h, tb * P:tb * P + (tb + 1) * P]
                            keys = slice(0, (tb + 1) * P)
                            pe.matmul(out, qT[:, h, tb * P:(tb + 1) * P], kT[:, h, keys], start=True, stop=False)
                            mm = pe.matmul(out, qrT[0:ROPE, h, tb * P:(tb + 1) * P], krT[0:ROPE, keys],
                                           start=False, stop=True)
                        mm.then_inc(scores_done, 1)
                    if not last:
                        nxt = (i, 1) if par == 0 else (i + 1, 0)
                        q_gemm(nxt, nxt[1])
                    for h in range(HPP):
                        pe.wait_ge(exp_done, 2 * p + h + 1)
                        for b in range(3):
                            mm = pe.transpose(ps[:, 6 + h, b * P:(b + 1) * P], prob[h][:, b * P:(b + 1) * P], ident)
                        mm.then_inc(pt_done, 1)
                    if not last:
                        kv_gemm(nxt, nxt[1], (0, 1))
                    pe.wait_ge(ptc_act, CREDIT["ptc_act"] + p + 1)
                    pe.wait_ge(ptc_dve, CREDIT["ptc_dve"] + p + 1)
                    for h in range(HPP):
                        v = lambda tb: kv_sb[par][:, tb, h * S + NOPE:(h + 1) * S]
                        at = h * S
                        pe.matmul(ps[:, 4, at:at + P], probT[h][:, 0:P], v(0), start=True, stop=True)
                        pe.matmul(ps[:, 4, at + P:at + 2 * P], probT[h][:, P:2 * P], v(0), start=True, stop=False)
                        mm = pe.matmul(ps[:, 4, at + P:at + 2 * P], probT[h][:, 2 * P:3 * P], v(1),
                                       start=False, stop=True)
                    mm.then_inc(pv_done, 1)
                    if not last:
                        kv_gemm(nxt, nxt[1], (2, 3))
                    pe.wait_ge(og_done, CREDIT["og_done"] + p + 1)
                    for h in range(HPP):
                        for tb in range(TB):
                            at = h * S + tb * P
                            mm = pe.transpose(ps[:, 5, at:at + P], og[:, tb, h * VH:(h + 1) * VH], ident)
                    mm.then_inc(ogt_done, 1)

                q_gemm((0, 0), 0)
                kv_gemm((0, 0), 0)
                with pe.Fori(0, 3) as i:
                    for par in range(2):
                        heads(i, par)
                heads(3, 0)
                heads(3, 1, last=True)

                def out_blocks(name, pair):
                    lhs = parts(pair)
                    pe.wait_ge(proj_free, block_base[name])
                    with pe.Fori(0, 2) as i:
                        for u in range(2):
                            pe.wait_ge(proj_free, block_base[name] + 2 * i + max(u - 1, 0))
                            gemm_split(*lhs, 2 * u, name, 2 * SCPB * i + SCPB * u)

                pe.wait_ge(ogc_done, CREDIT["ogc_done"] + 8)
                out_blocks("mla_out", oT_mla)
            def kvz(m):
                name = m.name
                if m.branches == 1:
                    gemm_split(*hT_parts, 0, "a_kvz", 0, norm=2)
                    z_name, z_at = "a_kvz", 1
                else:
                    b0 = block_base["b_kv"]
                    for b in range(4):
                        if b >= 2:
                            pe.wait_ge(proj_free, b0 + b - 1)
                        gemm_split(*hT_parts, 2 * (b % 2), "b_kv", SCPB * b, width=NB if b < 3 else 96,
                                   norm=None if b else 3)
                    z_name, z_at = "b_z", 0
                b0 = block_base[z_name] + z_at

                def z_blocks(i, us=range(2)):
                    for u in us:
                        b = 2 * i + u
                        pe.wait_ge(proj_free, b0 + b - 1)
                        gemm_split(*hT_parts, 2 * ((z_at + u) % 2), z_name, SCPB * (b + z_at))

                z_blocks(0)
                for br in range(m.branches):
                    pe.wait_ge(m.kdup, br + 1)
                    if br:
                        pe.wait_ge(m.kT_act, br)
                        pe.wait_ge(m.kT_dve, br)
                    for g in range(NKV):
                        for tb in range(TB):
                            at = (g % 2) * S + tb * P
                            mm = pe.transpose(ps[:, 4 + g // 2, at:at + P], k_dup[br][:, tb, g * P:(g + 1) * P], ident)
                    mm.then_inc(m.k_turned, 1)
                if m.branches == 2:
                    for c in range(2):
                        if c:
                            pe.wait_ge(c_copied, 1)
                        for g in range(NKV):
                            for tb in range(TB):
                                at = (g % 2) * S + tb * P
                                lo = (c * NKV + g) * P
                                mm = pe.transpose(ps[:, 6 + g // 2, at:at + P], kc_dup[:, tb, lo:lo + P], ident)
                        mm.then_inc(c_turned, 1)
                z_blocks(1)

            def compress_w1(c):
                pe.wait_ge(unfolded, c + 1)
                if c:
                    pe.wait_ge(c_copied, 2)
                for k in range(CL // 2):
                    j = k // 4
                    if k % 4 == 0:
                        pe.wait_ge(w1_full[j], 16 * (c + 1))
                    for hh in range(2):
                        mm = pe.matmul(ps[:, 4 + 2 * c + hh, 0:NKV * NCMP], w1_ring[:, j, k % 4, hh * P:(hh + 1) * P],
                                       unfold[c][:, k, :, :].rearrange("p g n -> p (g n)"),
                                       start=(k == 0), stop=(k == CL // 2 - 1))
                    if k % 4 == 3:
                        mm.then_inc(w1_used, 1)

            def compress_w2(c):
                pe.wait_ge(gelu_done, c + 1)
                pe.wait_ge(w2_in, 48)
                if c == 0:
                    for hh in range(2):
                        mm = pe.matmul(ps[:, 4, 0:NKV * NCMP], w2k[:, hh, :], hidT[c][:, hh, :],
                                       start=(hh == 0), stop=(hh == 1))
                else:
                    for g in range(NKV):
                        for hh in range(2):
                            mm = pe.matmul(ps[0:NCMP, 5, g * HD:(g + 1) * HD],
                                           hidT[c][:, hh, g * NCMP:(g + 1) * NCMP], w2v[:, hh, :],
                                           start=(hh == 0), stop=(hh == 1))
                mm.then_inc(cmp_w2, 1)

            def groups(m):
                name, NU = m.name + "_q", m.units
                b0 = block_base[name]
                is_b = m.branches == 2

                def rows(h):
                    return slice((h % 2) * HD, (h % 2 + 1) * HD)

                def scores(g, u):
                    h, br = u % HG, u // HG
                    pe.wait_ge(m.max_done, NU * g + u + 1)
                    for tb in range(TB):
                        mm = pe.matmul(ps[:, 2 + u % 2, tb * P:tb * P + (tb + 1) * P],
                                       qT_grp[rows(h), h // 2, tb * P:(tb + 1) * P],
                                       kT_grp[br][rows(h), 0:(tb + 1) * P], start=True, stop=True)
                    mm.then_inc(m.scores, 1)

                def turn_probs(g, u):
                    pe.wait_ge(m.exp_done, NU * g + u + 1)
                    pe.wait_ge(m.ptc_dve if u % 2 else m.ptc_act, (NU // 2) * g + u // 2 + 1)
                    for b in range(3):
                        mm = pe.transpose(ps[:, 4 + u % 2, b * P:(b + 1) * P],
                                          prob4[u % 4][:, b * P:(b + 1) * P], ident)
                    mm.then_inc(m.pt_done, 1)

                def pv(g, u):
                    h, br = u % HG, u // HG
                    pe.wait_ge(m.ptc_dve if u % 2 else m.ptc_act, (NU // 2) * g + u // 2 + 2)
                    if h == 0:
                        pe.wait_ge(m.o_read, m.reads * (g + 1) + br + is_b)
                    src = raw[br + is_b]
                    v = lambda tb: src[:, tb, ds(NKV * HD + g * HD, HD)]
                    pt = probT2[u % 2]
                    pe.matmul(ps[:, 6, h * HD:(h + 1) * HD], pt[:, 0:P], v(0), start=True, stop=True)
                    pe.matmul(ps[:, 7, h * HD:(h + 1) * HD], pt[:, P:2 * P], v(0), start=True, stop=False)
                    pe.matmul(ps[:, 7, h * HD:(h + 1) * HD], pt[:, 2 * P:3 * P], v(1),
                              start=False, stop=True).then_inc(m.pv_done, 1)

                tail = 4 if is_b else 3
                fill = {"start": 2, "turned": 1, "scores": 1}
                fill.update({u: 1 for u in range(0, 14, 2)} if is_b else {0: 2, 1: 2, 2: 2, 3: 2, 4: 1})
                if is_b:
                    fill["cmp"] = 1
                assert tail + sum(fill.values()) == KT

                def first_queries(g):
                    pe.wait_ge(proj_free, b0 + g)
                    for k in range(tail):
                        gemm_k(k, hT, 0, whole_base[name], CPB * g, KT)

                def group(g, last=False, tail_too=True):
                    k_next = [tail]

                    def next_queries(where):
                        for _ in range(0 if last else fill.get(where, 0)):
                            gemm_k(k_next[0], hT, 0, whole_base[name], CPB * (g + 1), KT)
                            k_next[0] += 1

                    next_queries("start")
                    pe.wait_ge(m.q_roped, g + 1)
                    for bank in range(2):
                        pe.wait_ge((m.ptc_act, m.ptc_dve)[bank], (NU // 2) * g + 1)
                        pe.wait_ge(m.ogc_done, g + 1)
                        for j in range(2):
                            for tb in range(TB):
                                pair = 2 * bank + j
                                mm = pe.transpose(ps[:, 4 + bank, j * S + tb * P:j * S + (tb + 1) * P],
                                                  q_grp[:, tb, pair * P:(pair + 1) * P], ident)
                        mm.then_inc(m.turned, 1)
                    next_queries("turned")
                    pe.wait_ge(m.qT_act, g + 1)
                    pe.wait_ge(m.qT_dve, g + 1)
                    pe.wait_ge(m.k_ready, g + 1)
                    if is_b:
                        pe.wait_ge(m.o_read, m.reads * (g + 1))
                        pe.matmul(ps[0:HG * NCMP, 6, 256:256 + HD], cst("spread")[0:NCMP, :],
                                  vcmp[0:NCMP, ds(g * HD, HD)], start=True, stop=True)
                        for tb in range(TB):
                            for j in range(HG // 2):
                                at = (tb * HG + 2 * j) * NCMP
                                mm = pe.matmul(ps[:, 6, at:at + 2 * NCMP], qT_grp[:, j, tb * P:(tb + 1) * P],
                                               kcmp_grp, start=True, stop=True)
                        mm.then_inc(cmp_scores, 1)
                    scores(g, 0)
                    scores(g, 1)
                    next_queries("scores")
                    if is_b:
                        pe.wait_ge(cmp_exp, g + 1)
                        for tb in range(TB):
                            mm = pe.transpose(ps[0:HG * NCMP, 7, tb * P:(tb + 1) * P],
                                              p_cmp[:, tb * HG * NCMP:(tb + 1) * HG * NCMP], ident)
                        mm.then_inc(cmp_turned, 1)
                        next_queries("cmp")
                        pe.wait_ge(cmp_copied, g + 1)
                        pe.wait_ge(vbd_done, g + 1)
                        for tb in range(TB):
                            mm = pe.matmul(ps[:, 6 + tb, :], pT_cmp[0:HG * NCMP, tb, :], v_bd[0:HG * NCMP, :],
                                           start=True, stop=True)
                        mm.then_inc(cmp_pv, 1)
                    for u in range(NU):
                        turn_probs(g, u)
                        if u + 2 < NU:
                            scores(g, u + 2)
                        next_queries(u)
                        pv(g, u)
                    assert last or k_next[0] == KT
                    if not last and tail_too:
                        first_queries(g + 2)
                    pe.wait_ge(m.og_done, g + 2)
                    for bank in range(2):
                        for j in range(2):
                            for tb in range(TB):
                                pair = 2 * bank + j
                                mm = pe.transpose(ps[:, 4 + bank, j * S + tb * P:j * S + (tb + 1) * P],
                                                  o_grp[:, tb, pair * P:(pair + 1) * P], ident)
                        mm.then_inc(m.ogt_done, 1)

                pe.wait_ge(proj_free, b0)
                for q in range(4):
                    pe.wait_ge(hT_whole, 4 * (1 + is_b) - 3 + q)
                    for k in range(4 * q, 4 * q + 4):
                        gemm_k(k, hT, 0, whole_base[name], 0, KT)
                    if is_b and q == 1:
                        compress_w1(1)
                        compress_w2(0)
                if is_b:
                    compress_w2(1)
                    pe.wait_ge(cmp_kv, 1)
                first_queries(1)
                with pe.Fori(0, NKV - 2) as g:
                    group(g)
                group(NKV - 2, tail_too=False)
                group(NKV - 1, last=True)
                pe.wait_ge(m.ogc_done, NKV + 1)

            for m, idx in ((ma, 2), (mb, 3)):
                if m is not None:
                    norm_start(idx)
                    pe.wait_ge(proj_free, block_base["a_kvz" if idx == 2 else "b_kv"])
                    kvz(m)
                    if idx == 3:
                        compress_w1(0)
                    groups(m)
                    out_blocks(f"{m.name}_out", oT_mix)

        @block.scalar
        def _(act):
            act_n = [0]

            def norm_stats(idx):
                if idx == 0:
                    act.wait_ge(x_in, 16)
                for b in range(4):
                    x_squares(idx, b)
                root()

            def x_squares(idx, b):
                if idx:
                    act.wait_ge(*x_final(idx, b))
                for tb in range(TB):
                    blk = slice(b * NB, (b + 1) * NB)
                    a = act.activation(y_sb[:, tb, blk], x_sb[:, tb, blk], ACT.Square,
                                       accum_out=xsq[:, tb * 4 + b:tb * 4 + b + 1])
                if b == 3:
                    a.then_inc(ssq_done, 1)

            roots = [0]

            def root(n=TB):
                roots[0] += 1
                act.wait_ge(ms_done, roots[0])
                act.activation(rms[:, 0:n], rms[:, 0:n], ACT.Sqrt).then_inc(rms_done, 1)

            def split_chunk(name, c, j):
                g, slot = chunk_base[name], j % RING
                act.wait_ge(raw_full[slot], filled_at(split_base[name], c, j))
                if not (isinstance(c, int) and g + c + j < RING):
                    act.wait_ge(w_used, c + (g + j - RING + 1))
                act.activation(split_ring[:, slot, 0], raw_ring[:, slot], ACT.Copy).then_inc(hi_done, 1)

            def splits(name, c, n=SCPB, more=True, start=LEAD):
                for j in range(start, LEAD + n if more else n):
                    split_chunk(name, c, j)

            def hT_copies(idx, name):
                if idx < 2:
                    act.wait_ge(aff_ready, idx + 1)
                for kp in range(KT // 2):
                    act.wait_ge(xT_done, idx * KT // 2 + kp + 1)
                    for k in (2 * kp, 2 * kp + 1):
                        src = ps[:, 6 + kp % 2, (k % 2) * S:(k % 2 + 1) * S]
                        if idx < 2:
                            a = act.activation(hT_hi[:, k, :], src, ACT.Identity, scale=aff_a[:, k:k + 1],
                                               bias=aff_b[:, k:k + 1])
                        else:
                            a = act.activation(hT_hi[:, k, :], src, ACT.Copy,
                                               scale=vec(f"norm_w{idx - 2}")[:, k:k + 1])
                    a.then_inc(hT_up, 1)
                    if kp >= 2:
                        split_chunk(name, 0, kp + 1)

            act.wait_ge(consts_in, 32)
            act.activation(cond, vec("c"), ACT.Silu).then_inc(cond_done, 1)
            norm_stats(0)
            for j in range(LEAD):
                split_chunk("sgu_v", 0, j)
            hT_copies(0, "sgu_v")

            def v_blocks(i, first=False):
                for u in range(2):
                    splits("sgu_v", 2 * SCPB * i + SCPB * u, start=HT_NEXT if first and not u else LEAD)
                    act.wait_ge(w_used, block_done("sgu_v", 2 * i + u))
                    act.activation(v_sb[:, :, ds(i * 2 * NB + u * NB, NB)], ps[:, 2 * u:2 * u + 2, :], ACT.Gelu
                                   ).then_inc(proj_free, 1)

            v_blocks(0, first=True)
            with act.Fori(1, 4) as i:
                v_blocks(i)
            root()

            def y_copies(n):
                act.wait_ge(yt_done, n + 1)
                for tb in range(TB):
                    a = act.activation(yT_hi[:, ds(n * 4, 4), tb * P:(tb + 1) * P],
                                       ps[:, 6 + tb, :].rearrange("p (k s) -> p k s", k=4), ACT.Copy)
                a.then_inc(yT_up, 1)

            def uz(n, first=False):
                b0 = block_base["sgu_uz"]
                splits("sgu_uz", 2 * SCPB * n)
                if not first:
                    act.wait_ge(y_done, n)
                act.wait_ge(w_used, block_done("sgu_uz", 2 * n))
                act.activation(u_t, ps[:, 0:2, :], ACT.Gelu).then_inc(proj_free, 1)
                if not first:
                    y_copies(n - 1)
                splits("sgu_uz", 2 * SCPB * n + SCPB)
                act.wait_ge(w_used, block_done("sgu_uz", 2 * n + 1))
                act.activation(z_t, ps[:, 2:4, :], ACT.Silu).then_inc(proj_free, 1)

            uz(0, first=True)
            with act.Fori(1, 8) as n:
                uz(n)
            y_copies(7)

            squares = [0]

            def square_blocks(name):
                n = chunks_per[name]
                for b in range(4):
                    splits(name, n * b, n, more=b < 3 or more_after[name])
                    act.wait_ge(w_used, block_done(name, b))
                    for tb in range(TB):
                        if squares[0]:
                            act.wait_ge(ysq_done, squares[0])
                        squares[0] += 1
                        act.activation(sq_junk, ps[:, 2 * (b % 2) + tb, :], ACT.Square,
                                           accum_out=ysq[:, tb * 4 + b:tb * 4 + b + 1]).then_inc(ysq_done, 1)

            square_blocks("sgu_out")
            root()
            if stages > 1:
                norm_stats(1)
            if stages >= 2:
                hT_copies(1, "mla_in")
                for b in range(2):
                    splits("mla_in", SCPB * b, start=LEAD if b else HT_NEXT)
                    act.wait_ge(w_used, block_done("mla_in", b))
                    act.activation(craw[:, :, b * NB:(b + 1) * NB], ps[:, 2 * b:2 * b + 2, :], ACT.Copy
                                   ).then_inc(proj_free, 1)
                act.wait_ge(proj_free, block_base["mla_in"] + 2)
                for m, (lo, n) in enumerate(((0, QL), (QL, KVL))):
                    for tb in range(TB):
                        if m or tb:
                            act.wait_ge(c_ssq, m * TB + tb)
                        act.activation(sq_junk[:, 0:n], craw[:, tb, lo:lo + n], ACT.Square,
                                       accum_out=c_sq[:, m * TB + tb:m * TB + tb + 1]).then_inc(c_ssq, 1)
                splits("mla_in", 2 * SCPB)
                root(2 * TB)
                for b in range(4):
                    if b:
                        splits("mla_in", (b + 2) * SCPB, more=b < 3)
                    act.wait_ge(w_used, block_done("mla_in", b + 2))
                    act.activation(z_sb[:, :, b * NB:(b + 1) * NB], ps[:, 2 * (b % 2):2 * (b % 2) + 2, :], ACT.Silu
                                   ).then_inc(proj_free, 1)
                act.wait_ge(cT_turned, 1)
                for k in range(4):
                    a = act.activation(cqT[0:QL_P, k, :], ps[0:QL_P, 6 + k // 2, (k % 2) * S:(k % 2 + 1) * S],
                                       ACT.Copy, scale=vec("q_g")[0:QL_P, k:k + 1])
                a.then_inc(cT_act, 1)

                c0, b0 = chunk_base["mla_heads"], block_base["mla_heads"]

                def q_copy(p, par):
                    act.wait_ge(w_used, c0 + 2 * p + 1)
                    act.activation(q_sb[par], ps[:, 0:2, 0:HPP * QKD], ACT.Copy).then_inc(proj_free, 1)

                def kv_copy(p, par):
                    act.wait_ge(w_used, c0 + 2 * p + 2)
                    act.activation(kv_sb[par], ps[:, 2:4, :], ACT.Copy).then_inc(proj_free, 1)

                def heads(i, par, last=False):
                    p = 2 * i + par
                    act.wait_ge(turned_q, p + 1)
                    act.activation(qT, ps[:, 6, :].rearrange("p (h s) -> p h s", h=HPP), ACT.Copy
                                   ).then_inc(qT_copied, 1)
                    act.wait_ge(turned_r, p + 1)
                    act.activation(qrT[0:ROPE], ps[0:ROPE, 5, :].rearrange("p (h s) -> p h s", h=HPP), ACT.Copy
                                   ).then_inc(qT_copied, 1)
                    for h in range(HPP):
                        act.wait_ge(max_done, 2 * p + h + 1)
                        for tb in range(TB):
                            blk = prob[h][:, tb * P:tb * P + (tb + 1) * P]
                            n = h * TB + tb
                            a = act.activation(blk, blk, ACT.Exp, bias=nmx[:, n:n + 1], accum_out=sums[:, n:n + 1])
                        a.then_inc(exp_done, 1)
                    if not last:
                        q_copy(p + 1, 1 - par)
                    act.wait_ge(pt_done, CREDIT["pt_done"] + 2 * p + 1)
                    act.wait_ge(pv_done, CREDIT["pv_done"] + p)
                    act.activation(probT[0], ps[:, 6, 0:SCW], ACT.Copy).then_inc(ptc_act, 1)
                    if not last:
                        kv_copy(p + 1, 1 - par)
                    act.wait_ge(ogt_done, CREDIT["ogt_done"] + p + 1)
                    act.activation(oT_mla[0][:, ds(HPP * p, HPP), :], ps[:, 5, :].rearrange("p (h s) -> p h s", h=HPP),
                                   ACT.Copy).then_inc(ogc_up, 1)

                act.sem_inc(ptc_act, CREDIT["ptc_act"])
                act.sem_inc(pv_done, CREDIT["pv_done"])
                q_copy(0, 0)
                kv_copy(0, 0)
                with act.Fori(0, 3) as i:
                    for par in range(2):
                        heads(i, par)
                heads(3, 0)
                for j in range(LEAD):
                    split_chunk("mla_out", 0, j)
                heads(3, 1, last=True)
                square_blocks("mla_out")
                root()
                if stages > 2:
                    norm_stats(2)
            def rotation_angles():
                act.wait_ge(trig_in, 1)
                act.activation(sin2, red, ACT.Sin)
                act.activation(cos2, turns, ACT.Sin).then_inc(trig_done, 1)

            def kvz(m):
                if m.branches == 1:
                    splits("a_kvz", 0, start=HT_NEXT)
                    act.wait_ge(w_used, block_done("a_kvz", 0))
                    act.activation(raw[0], ps[:, 0:2, :], ACT.Copy).then_inc(proj_free, 1)
                    z_name, z_at = "a_kvz", 1
                else:
                    for b in range(3):
                        splits("b_kv", SCPB * b, start=LEAD if b else HT_NEXT)
                        act.wait_ge(w_used, block_done("b_kv", b))
                        if b == 0:
                            for e in range(2):
                                a = act.activation(kc_dup.rearrange("p t (g e n) -> p t g e n", e=2, n=HD)[:, :, :, e, :],
                                                   ps[:, 0:2, :].rearrange("p t (g n) -> p t g n", n=HD), ACT.Copy)
                            a.then_inc(proj_free, 1)
                            continue
                        act.activation(raw[b], ps[:, 2 * (b % 2):2 * (b % 2) + 2, :], ACT.Copy).then_inc(proj_free, 1)
                    splits("b_kv", 3 * SCPB)
                    act.wait_ge(w_used, block_done("b_kv", 3))
                    act.activation(gates, ps[:, 2:4, 0:96], ACT.Sigmoid).then_inc(proj_free, 1)
                    z_name, z_at = "b_z", 0

                def z_block(b):
                    splits(z_name, SCPB * (b + z_at), more=b < 3)
                    act.wait_ge(w_used, block_done(z_name, b + z_at))
                    bank = 2 * ((b + z_at) % 2)
                    act.activation(z_sb[:, :, b * NB:(b + 1) * NB], ps[:, bank:bank + 2, :], ACT.Silu
                                   ).then_inc(proj_free, 1)

                z_block(0)
                z_block(1)
                for br in range(m.branches):
                    act.wait_ge(m.k_turned, br + 1)
                    act.activation(kT_all[br][:, 0:2, :], ps[:, 4, :].rearrange("p (g s) -> p g s", g=2), ACT.Copy
                                   ).then_inc(m.kT_act, 1)
                if m.branches == 2:
                    for c in range(2):
                        act.wait_ge(c_turned, c + 1)
                        for bank in range(2):
                            a = act.activation(kcT[c][:, 2 * bank:2 * bank + 2, :],
                                               ps[:, 6 + bank, :].rearrange("p (g s) -> p g s", g=2), ACT.Copy)
                        a.then_inc(c_copied, 1)
                z_block(2)
                z_block(3)

            def compress():
                for c in range(2):
                    act.wait_ge(w1_used, (c + 1) * RING)
                    act.activation(hidT[c], ps[:, 4 + 2 * c:6 + 2 * c, 0:NKV * NCMP], ACT.Gelu_apprx_tanh).then_inc(gelu_done, 1)

            def groups(m):
                name, NU = m.name + "_q", m.units
                is_b = m.branches == 2

                def q_copy(g):
                    act.wait_ge(w_used, block_done(name, g))
                    act.activation(q_grp, ps[:, 0:2, :], ACT.Copy).then_inc(proj_free, 1)

                def exps(g, u):
                    h, br = u % HG, u // HG
                    act.wait_ge(m.max_done, 2 + NU * g + u + 1)
                    for tb in range(TB):
                        n = tb * HG + h
                        blk = prob4[u % 4][:, tb * P:tb * P + (tb + 1) * P]
                        a = act.activation(blk, blk, ACT.Exp, bias=nmx2[:, n:n + 1],
                                           accum_out=sums2[br][:, n:n + 1])
                    a.then_inc(m.exp_done, 1)

                def group(g, last=False):
                    act.wait_ge(m.turned, 2 * g + 1)
                    act.activation(qT_grp[:, 0:2, :], ps[:, 4, :].rearrange("p (j s) -> p j s", j=2), ACT.Copy
                                   ).then_inc(m.qT_act, 1)
                    if is_b:
                        act.wait_ge(cmp_shifted, g + 1)
                        act.activation(p_cmp, p_cmp, ACT.Exp, scale=SCALE2).then_inc(cmp_exp, 1)
                    act.wait_ge(m.og_done, g + 1)
                    exps(g, 0)
                    exps(g, 1)
                    if is_b:
                        act.wait_ge(cmp_turned, g + 1)
                        act.activation(pT_cmp[0:HG * NCMP], ps[0:HG * NCMP, 7, 0:S].rearrange("p (t n) -> p t n", t=TB),
                                       ACT.Copy).then_inc(cmp_copied, 1)
                    for u in range(NU):
                        if u % 2 == 0:
                            act.wait_ge(m.pt_done, 4 + NU * g + u + 1)
                            act.wait_ge(m.pv_done, NU * g + u + 1)
                            act.activation(probT2[0], ps[:, 4, 0:SCW], ACT.Copy).then_inc(m.ptc_act, 1)
                        if u == NU - 2 and not last:
                            q_copy(g + 1)
                        if u + 2 < NU:
                            exps(g, u + 2)
                    if not is_b:
                        act.wait_ge(m.sink_in, g + 1)
                        act.activation(sink_e, sink_e, ACT.Exp).then_inc(m.sink_exp, 1)
                    act.wait_ge(m.ogt_done, 2 * g + 1)
                    for bank in range(2):
                        if bank:
                            act.wait_ge(m.ogt_done, 2 * g + 2)
                        act.activation(oT_mix[0][:, ds(4 * g + 2 * bank, 2), :],
                                       ps[:, 4 + bank, :].rearrange("p (j s) -> p j s", j=2), ACT.Copy
                                       ).then_inc(m.ogc_up, 1)

                act.sem_inc(m.ptc_act, 1)
                q_copy(0)
                with act.Fori(0, NKV - 1) as g:
                    group(g)
                for j in range(LEAD):
                    split_chunk(f"{m.name}_out", 0, j)
                group(NKV - 1, last=True)

            for m, idx in ((ma, 2), (mb, 3)):
                if m is not None:
                    hT_copies(idx, ("a_kvz", "b_kv")[idx - 2])
                    if idx == 2:
                        rotation_angles()
                    kvz(m)
                    if idx == 3:
                        compress()
                    groups(m)
                    name = f"{m.name}_out"
                    for b in range(4):
                        splits(name, SCPB * b, more=b < 3 or more_after.get(name, False))
                        if stages > idx + 1:
                            x_squares(idx + 1, b)
                    if stages > idx + 1:
                        root()

        @block.vector
        def _(dve):
            steps = [0]

            def link(ins):
                steps[0] += 1
                ins.then_inc(dve_step, 1)
                dve.wait_ge(dve_step, steps[0])

            roots = [0]

            def take_waits():
                dve.memset(wait_cell, 0.0)

            def inverse_root(dst=rstd[:, 0:TB]):
                roots[0] += 1
                dve.wait_ge(rms_done, roots[0])
                link(dve.reciprocal(dst, rms[:, 0:dst.shape[-1]]))

            def norm_x(idx, eps, final=False):
                dve.wait_ge(ssq_done, idx + 1)
                link(dve.tensor_reduce(rms[:, 0:TB], xsq.rearrange("p (t b) -> p t b", t=TB), AX, ALU.add))
                dve.tensor_scalar(rms[:, 0:TB], rms[:, 0:TB], 1.0 / D, eps, ALU.mult, ALU.add).then_inc(ms_done, 1)
                inverse_root()
                if final:
                    dve.wait_ge(gain_in, 16)
                    for tb in range(TB):
                        v = dve.scalar_tensor_tensor(out=y_sb[:, tb, :], in0=x_sb[:, tb, :], scalar=rstd[:, tb:tb + 1],
                                                     in1=last_gain, op0=ALU.mult, op1=ALU.mult)
                        v.then_inc(out_ready, 1)
                    return
                for tb in range(TB):
                    v = dve.tensor_scalar(diag[:, tb, :], ident, rstd[:, tb:tb + 1], None, ALU.mult)
                v.then_inc(xn_done, 1)

            def split_chunk(name, c, j):
                slot = j % RING
                dve.wait_ge(hi_done, c + (split_base[name] + j + 1))
                dve.tensor_tensor(split_ring[:, slot, 1], raw_ring[:, slot], split_ring[:, slot, 0].bitcast(F32),
                                  ALU.subtract).then_inc(lo_done, 1)

            def splits(name, c, n=SCPB, more=True, between=(), start=LEAD):
                between = list(between)
                todo = range(start, LEAD + n if more else n)
                for i, j in enumerate(todo):
                    split_chunk(name, c, j)
                    for _ in range(-(-len(between) // (len(todo) - i))):
                        between.pop(0)()

            def hT_copies(idx, name):
                for kp in range(KT // 2):
                    dve.wait_ge(hT_up, idx * KT // 2 + kp + 1)
                    pair = slice(2 * kp, 2 * kp + 2)
                    src = lambda k: ps[:, 6 + kp % 2, (k % 2) * S:(k % 2 + 1) * S]
                    if idx < 2:
                        for k in (2 * kp, 2 * kp + 1):
                            v = dve.tensor_scalar(hT_lo_f[:, k, :], src(k), aff_a[:, k:k + 1], aff_b[:, k:k + 1],
                                                  ALU.mult, ALU.add)
                        link(v)
                        v = dve.tensor_tensor(hT_lo[:, pair, :], hT_lo_f[:, pair, :], hT_hi[:, pair, :].bitcast(F32),
                                              ALU.subtract)
                    else:
                        for k in (2 * kp, 2 * kp + 1):
                            v = dve.scalar_tensor_tensor(out=hT_lo[:, k, :], in0=src(k),
                                                         scalar=vec(f"norm_w{idx - 2}")[:, k:k + 1],
                                                         in1=hT_hi[:, k, :].bitcast(F32), op0=ALU.mult,
                                                         op1=ALU.subtract)
                    v.then_inc(xT_free[kp % 2], 1)
                    if kp >= 2:
                        split_chunk(name, 0, kp + 1)

            def ada_gemv0(t, us, first=False):
                for u in us:
                    for m in range(2):
                        q = 2 * u + m
                        dve.wait_ge(ada0_full[q], 16 * t + 16)
                        if u or not first:
                            dve.wait_ge(ada0_used, 4 * t + q - 1)
                        acc = ada_acc[:, m * D:(m + 1) * D]
                        dve.scalar_tensor_tensor(out=acc, in0=ada0_buf[:, q, :], scalar=cond[:, ds(2 * t + u, 1)],
                                                 in1=acc, op0=ALU.mult, op1=ALU.add).then_inc(ada0_used, 1)

            def ada_gemv(stage, t):
                T_, half = t + KT * stage, ADA_STAGES[stage][2]

                def step(j):
                    def run():
                        dve.wait_ge(ada_full[j], 16 * T_ + 16)
                        dve.wait_ge(ada_used, ADA_N * T_ + (j + 1))
                        acc = ada_acc[:, half * D + j * ADA_C:half * D + (j + 1) * ADA_C]
                        dve.scalar_tensor_tensor(out=acc, in0=ada_buf[:, j, :], scalar=cond[:, ds(t, 1)], in1=acc,
                                                 op0=ALU.mult, op1=ALU.add).then_inc(ada_used, 1)
                    return run
                return [step(j) for j in range(ADA_N)]

            dve.wait_ge(consts_in, 32)
            dve.wait_ge(cond_done, 1)
            dve.wait_ge(acc_init, 32)
            dve.wait_ge(acc_zero, 1)
            norm_x(0, EPS1)
            ada_gemv0(0, range(2), first=True)
            with dve.Fori(1, KT // 2) as t:
                ada_gemv0(t, range(2))

            def affine(layer):
                dve.wait_ge(cols_done, layer + 1)
                link(dve.tensor_copy(aff_b, ps[:, 4, 0:KT]))
                dve.scalar_tensor_tensor(out=aff_a, in0=ps[:, 4, KT:2 * KT], scalar=1.0, in1=vec(f"pre_g{layer}"),
                                         op0=ALU.add, op1=ALU.mult).then_inc(aff_ready, 1)
                dve.wait_ge(aff_ready, layer + 1)

            for j in range(LEAD):
                split_chunk("sgu_v", 0, j)
            affine(0)
            hT_copies(0, "sgu_v")

            dve.sem_inc(ada_used, CREDIT["ada_used"])
            dve.wait_ge(acc_init, 48)

            def v_blocks(i, first=False):
                for u in range(2):
                    t = 4 * i + 2 * u
                    splits("sgu_v", 2 * SCPB * i + SCPB * u, start=HT_NEXT if first and not u else LEAD,
                           between=ada_gemv(0, t) + ada_gemv(0, t + 1))
                    dve.wait_ge(proj_free, block_base["sgu_v"] + 2 * i + u + 1)
                    for tb in range(TB):
                        v = dve.bn_stats(bn_st[:, tb, ds(2 * i + u, 1), :],
                                         v_sb[:, tb, ds(i * 2 * NB + u * NB, NB)])
                    v.then_inc(vstat_done, 1)

            v_blocks(0, first=True)
            with dve.Fori(1, 4) as i:
                v_blocks(i)
            dve.wait_ge(vstat_done, 8)
            for tb in range(TB):
                link(dve.bn_aggr(bn_mv[:, 2 * tb:2 * tb + 2], bn_st[:, tb, :, :]))
            dve.tensor_scalar(rms[:, 0:TB], bn_mv.rearrange("p (t c) -> p t c", c=2)[:, :, 1], EPS1, None, ALU.add
                              ).then_inc(ms_done, 1)
            inverse_root()
            for tb in range(TB):
                v = dve.tensor_scalar(v_sb[:, tb, :], v_sb[:, tb, :], bn_mv[:, 2 * tb:2 * tb + 1],
                                      rstd[:, tb:tb + 1], ALU.subtract, ALU.mult)
            v.then_inc(v_norm, 1)

            def gate_gain(n0):
                dve.wait_ge(postg_in, 16 * (n0 // 4 + 1))
                for q in range(4):
                    dve.wait_ge(gate_rows, n0 + q + 1)
                    blk = gate_g[:, q * NB:(q + 1) * NB]
                    dve.tensor_tensor(blk, ps[:, 4 + q, :], blk, ALU.mult).then_inc(gate_read, 1)
                dve.wait_ge(gate_read, n0 + 4)

            gate_gain(0)

            def y_rest(n):
                dve.wait_ge(yt_done, n + 1)
                dve.wait_ge(yT_up, n + 1)
                for tb in range(TB):
                    tok = slice(tb * P, (tb + 1) * P)
                    v = None
                    for a in range(2):
                        v = dve.tensor_tensor(yT_lo[:, ds(n, 1), a, :, tok],
                                              ps[:, 6 + tb, a * S:(a + 1) * S].rearrange("p (n j s) -> p n j s", n=1, j=2),
                                              yT_hi[:, ds(4 * n + 2 * a, 2), tok].bitcast(F32)
                                              .rearrange("p (n j) s -> p n j s", n=1), ALU.subtract)
                v.then_inc(yT_done, 1)

            def uz(n, stage, first=False):
                c = 2 * SCPB * n
                t = 4 * n - KT * (stage - 1)
                g0, g1 = ada_gemv(stage, t) + ada_gemv(stage, t + 1), ada_gemv(stage, t + 2) + ada_gemv(stage, t + 3)
                dve.wait_ge(wcur_in, 16 * n + 16)
                dve.tensor_tensor(w_cur, w_cur,
                                  cst("mask_sgu").rearrange("p (g s) -> p g s", g=1).to_broadcast([P, GPB, P]),
                                  ALU.mult).then_inc(wcur_done, 1)
                link_at(n, 0, dve.tensor_copy(b_cur, vec("b_s")[:, ds(GPB * n, GPB)]))
                splits("sgu_uz", c, between=g0)
                if not first:
                    y_rest(n - 1)
                dve.wait_ge(mix_done, n + 1)
                dve.wait_ge(g_in, 16 * n + 16)
                if not first:
                    dve.wait_ge(yt_done, n)
                link_at(n, 1, dve.tensor_tensor(y_t, ps[:, 4:6, :],
                                                g_blk.rearrange("p (t n) -> p t n", t=1).to_broadcast([P, TB, NB]),
                                                ALU.mult))
                dve.wait_ge(proj_free, block_base["sgu_uz"] + 2 * n + 1)
                for g in range(GPB):
                    cols = slice(g * SGU_GD, (g + 1) * SGU_GD)
                    v = dve.scalar_tensor_tensor(out=y_t[:, :, cols], in0=y_t[:, :, cols], scalar=b_cur[:, g:g + 1],
                                                 in1=u_t[:, :, cols], op0=ALU.add, op1=ALU.mult)
                link_at(n, 2, v)
                splits("sgu_uz", c + SCPB, between=g1)
                dve.wait_ge(proj_free, block_base["sgu_uz"] + 2 * n + 2)
                dve.tensor_tensor(y_t, y_t, z_t, ALU.mult).then_inc(y_done, 1)

            uz_base = steps[0]

            def link_at(n, k, ins):
                ins.then_inc(dve_step, 1)
                dve.wait_ge(dve_step, uz_base + 3 * n + k + 1)

            dve.wait_ge(acc_init, 64)
            uz(0, 1, first=True)
            with dve.Fori(1, 4) as n:
                uz(n, 1)
            dve.wait_ge(acc_init, 80)
            with dve.Fori(4, 8) as n:
                uz(n, 2)
            steps[0] += 3 * 8
            y_rest(7)

            def copy_blocks(name, y):
                n = chunks_per[name]
                for b in range(4):
                    splits(name, n * b, n, more=b < 3 or more_after[name],
                           between=[f for t in range(4) for f in ada_gemv(3, 4 * b + t)] if name == "sgu_out" else ())
                    dve.wait_ge(w_used, block_done(name, b))
                    dve.wait_ge(ysq_done, TB * (copies[0] + 1))
                    copies[0] += 1
                    blk = slice(b * NB, (b + 1) * NB)
                    dve.tensor_tensor(y[:, :, blk], ps[:, 2 * (b % 2):2 * (b % 2) + 2, :],
                                      gate_g[:, blk].rearrange("p (t n) -> p t n", t=1).to_broadcast([P, TB, NB]),
                                      ALU.mult).then_inc(proj_free, 1)

            copies = [0]

            def post_norm(idx):
                x, y = (x_sb, y_sb) if idx else (x_sgu, y_sgu)
                dve.wait_ge(proj_free, block_base[("sgu_out", "mla_out")[idx]] + 4)
                link(dve.tensor_reduce(rms[:, 0:TB], ysq.rearrange("p (t b) -> p t b", t=TB), AX, ALU.add))
                dve.tensor_scalar(rms[:, 0:TB], rms[:, 0:TB], 1.0 / D, EPS1, ALU.mult, ALU.add).then_inc(ms_done, 1)
                inverse_root()
                if idx == 0:
                    dve.wait_ge(x_back, 16)
                for b in range(4):
                    for tb in range(TB):
                        blk = slice(b * NB, (b + 1) * NB)
                        v = dve.scalar_tensor_tensor(out=x_sb[:, tb, blk], in0=y[:, tb, blk], scalar=rstd[:, tb:tb + 1],
                                                     in1=x[:, tb, blk], op0=ALU.mult, op1=ALU.add)
                    v.then_inc(x_blk, 1)

            affine(1)
            dve.wait_ge(acc_init, 96)
            copy_blocks("sgu_out", y_sgu)
            post_norm(0)
            if stages > 1:
                norm_x(1, EPS1)
            if stages >= 2:
                hT_copies(1, "mla_in")
                splits("mla_in", 0, start=HT_NEXT)
                splits("mla_in", SCPB)
                splits("mla_in", 2 * SCPB)
                dve.wait_ge(c_ssq, 2 * TB)
                for m, n in enumerate((QL, KVL)):
                    v = dve.tensor_scalar(rms[:, m * TB:(m + 1) * TB], c_sq[:, m * TB:(m + 1) * TB], 1.0 / n, EPS1,
                                          ALU.mult, ALU.add)
                v.then_inc(ms_done, 1)
                inverse_root(rstd)
                for m, (lo, n) in enumerate(((0, QL), (QL, KVL))):
                    for tb in range(TB):
                        blk = craw[:, tb, lo:lo + n]
                        dve.tensor_scalar(blk, blk, rstd[:, m * TB + tb:m * TB + tb + 1], None, ALU.mult)

                def rope(x1, x2, cos, sin, temps, last_sem):
                    a, b, c, d = temps
                    dve.tensor_tensor(a, x1, cos, ALU.mult)
                    dve.tensor_tensor(b, x2, sin, ALU.mult)
                    dve.tensor_tensor(c, x1, sin, ALU.mult)
                    link(dve.tensor_tensor(d, x2, cos, ALU.mult))
                    dve.tensor_tensor(x1, a, b, ALU.subtract)
                    dve.tensor_tensor(x2, c, d, ALU.add).then_inc(last_sem, 1)

                cos = cst("cos").rearrange("p (t n) -> p t n", t=TB)
                sin = cst("sin").rearrange("p (t n) -> p t n", t=TB)
                kr = craw[:, :, QL + KVL:QL + KVL + ROPE]
                rope(kr[:, :, 0:32], kr[:, :, 32:64], cos, sin,
                     [t[:, 0:TB * 32].rearrange("p (t n) -> p t n", t=TB) for t in rope_t], c_normed)
                for b in range(3, 6):
                    splits("mla_in", SCPB * b, more=b < 5)
                gate_gain(4)
                dve.wait_ge(cT_turned, 1)
                for k in range(4):
                    dve.tensor_scalar(ckvT[:, k, :], ps[:, 4 + k // 2, (k % 2) * S:(k % 2 + 1) * S],
                                      vec("kv_g")[:, k:k + 1], None, ALU.mult)
                dve.tensor_copy(krT[0:ROPE, :], ps[0:ROPE, 2, 0:S]).then_inc(cT_dve, 1)

                b0 = block_base["mla_heads"]
                heads_base = [0]

                def step(p, k, ins):
                    ins.then_inc(dve_step, 1)
                    dve.wait_ge(dve_step, heads_base[0] + HEAD_STEPS * p + k + 1)

                HEAD_STEPS = 4

                def rope_q(p, par, k):
                    dve.wait_ge(proj_free, b0 + 2 * p + 1)
                    x = q_sb[par].rearrange("p t (h n) -> p t h n", h=HPP)
                    x1, x2 = x[:, :, :, NOPE:NOPE + 32], x[:, :, :, NOPE + 32:QKD]
                    a, b, c, d = (t.rearrange("p (t h n) -> p t h n", t=TB, h=HPP) for t in rope_t)
                    cs, sn = (t.rearrange("p t (h n) -> p t h n", h=1).to_broadcast([P, TB, HPP, 32])
                              for t in (cos, sin))
                    dve.tensor_tensor(a, x1, cs, ALU.mult)
                    dve.tensor_tensor(b, x2, sn, ALU.mult)
                    dve.tensor_tensor(c, x1, sn, ALU.mult)
                    v = dve.tensor_tensor(d, x2, cs, ALU.mult)
                    if k is None:
                        link(v)
                    else:
                        step(k[0], k[1], v)
                    dve.tensor_tensor(x1, a, b, ALU.subtract)
                    dve.tensor_tensor(x2, c, d, ALU.add).then_inc(q_roped, 1)

                def heads(i, par, last=False):
                    p = 2 * i + par
                    dve.wait_ge(turned_k, p + 1)
                    dve.tensor_copy(kT, ps[:, 7, :].rearrange("p (h s) -> p h s", h=HPP)).then_inc(kT_copied, 1)
                    for h in range(HPP):
                        dve.wait_ge(scores_done, 2 * p + h + 1)
                        dve.wait_ge(pt_done, CREDIT["pt_done"] + 2 * p + h - 1)
                        take_waits()
                        for tb in range(TB):
                            lo, hi = tb * P, tb * P + (tb + 1) * P
                            v = dve.tensor_tensor_reduce(prob[h][:, lo:hi], ps[:, 4 + h, lo:hi],
                                                         cst("mask_chunk")[:, lo:hi], MLA_SCALE, -3e38, ALU.add,
                                                         ALU.max, mx[:, h * TB + tb:h * TB + tb + 1])
                        step(p, h, v)
                        cols = slice(h * TB, (h + 1) * TB)
                        dve.tensor_scalar(nmx[:, cols], mx[:, cols], -1.0, None, ALU.mult).then_inc(max_done, 1)
                    dve.wait_ge(pt_done, CREDIT["pt_done"] + 2 * p + 2)
                    dve.wait_ge(pv_done, CREDIT["pv_done"] + p)
                    dve.tensor_copy(probT[1], ps[:, 7, 0:SCW]).then_inc(ptc_dve, 1)
                    dve.wait_ge(exp_done, 2 * p + 2)
                    step(p, 2, dve.reciprocal(rinv, sums))
                    if not last:
                        rope_q(p + 1, 1 - par, (p, 3))
                    else:
                        step(p, 3, dve.reciprocal(rinv, sums))
                    dve.wait_ge(pv_done, CREDIT["pv_done"] + p + 1)
                    dve.wait_ge(ogt_done, CREDIT["ogt_done"] + p)
                    for h in range(HPP):
                        for tb in range(TB):
                            n = h * TB + tb
                            v = dve.scalar_tensor_tensor(out=og[:, tb, h * VH:(h + 1) * VH],
                                                         in0=ps[:, 4, n * P:(n + 1) * P], scalar=rinv[:, n:n + 1],
                                                         in1=z_sb[:, tb, ds(p * HPP * VH + h * VH, VH)],
                                                         op0=ALU.mult, op1=ALU.mult)
                    v.then_inc(og_done, 1)
                    dve.wait_ge(ogc_up, p + 1)
                    heads_kt = ds(HPP * p, HPP)
                    dve.tensor_tensor(oT_mla[1][:, heads_kt, :], ps[:, 5, :].rearrange("p (h s) -> p h s", h=HPP),
                                      oT_mla[0][:, heads_kt, :].bitcast(F32), ALU.subtract).then_inc(ogc_done, 1)

                dve.sem_inc(ptc_dve, CREDIT["ptc_dve"])
                dve.sem_inc(og_done, CREDIT["og_done"])
                dve.sem_inc(ogc_done, CREDIT["ogc_done"])
                dve.sem_inc(pt_done, CREDIT["pt_done"])
                dve.sem_inc(ogt_done, CREDIT["ogt_done"])
                rope_q(0, 0, None)
                heads_base[0] = steps[0]
                with dve.Fori(0, 3) as i:
                    for par in range(2):
                        heads(i, par)
                heads(3, 0)
                for j in range(LEAD):
                    split_chunk("mla_out", 0, j)
                heads(3, 1, last=True)
                steps[0] += HEAD_STEPS * 8
                copy_blocks("mla_out", y_sb)
                post_norm(1)
                if stages > 2:
                    norm_x(2, EPS2)
            def rotation_angles():
                two_pi = 2 * np.pi
                parts, rest = [], two_pi
                for bits in (8, 8, 8):
                    scale = 2.0 ** (bits - 1 - np.floor(np.log2(rest)))
                    part = np.floor(rest * scale) / scale
                    parts.append(float(part))
                    rest -= part
                parts.append(float(rest))
                dve.wait_ge(pos_in, 16)
                link(dve.tensor_copy(pos_f, pos_i[:, :]))
                for tb in range(TB):
                    v = dve.tensor_scalar(ang[:, tb * RD:(tb + 1) * RD], cst("inv_freq"), pos_f[:, tb:tb + 1], None,
                                          ALU.mult)
                link(v)
                magic = 1.5 * 2.0 ** 23
                link(dve.tensor_scalar(turns, ang, 1 / two_pi, magic, ALU.mult, ALU.add))
                link(dve.tensor_scalar(turns, turns, -magic, None, ALU.add))
                for n, part in enumerate(parts):
                    link(dve.scalar_tensor_tensor(out=red, in0=turns, scalar=-part, in1=red if n else ang,
                                                  op0=ALU.mult, op1=ALU.add))
                link(dve.tensor_scalar(red, red, 3.141592, -3.141592, ALU.min, ALU.max))
                link(dve.scalar_tensor_tensor(out=turns, in0=red, scalar=-1.0, in1=red, op0=ALU.mult, op1=ALU.max))
                dve.tensor_scalar(turns, turns, -1.0, float(np.pi / 2), ALU.mult, ALU.add).then_inc(trig_in, 1)
                dve.wait_ge(trig_done, 1)

            def rotate(x, heads, after=None):
                x = x.rearrange("p t (h n) -> p t h n", h=heads)
                x1, x2 = x[:, :, :, 0:RD], x[:, :, :, RD:2 * RD]
                a, b, c, d = (t[:, 0:TB * heads * RD].rearrange("p (t h n) -> p t h n", t=TB, h=heads)
                              for t in rope2_t)
                cs, sn = (t.rearrange("p (t h n) -> p t h n", t=TB, h=1).to_broadcast([P, TB, heads, RD])
                          for t in (cos2, sin2))
                dve.tensor_tensor(a, x1, cs, ALU.mult)
                dve.tensor_tensor(b, x2, sn, ALU.mult)
                dve.tensor_tensor(c, x1, sn, ALU.mult)
                (after or link)(dve.tensor_tensor(d, x2, cs, ALU.mult))
                dve.tensor_tensor(x1, a, b, ALU.subtract)
                return dve.tensor_tensor(x2, d, c, ALU.add)

            def kvz(m):
                def keys(br):
                    src = raw[br + (m.branches == 2)]
                    dve.wait_ge(proj_free, block_base["a_kvz" if m.branches == 1 else "b_kv"] + br + m.branches)
                    link(rotate(src[:, :, 0:NKV * HD], NKV))
                    for tb in range(TB):
                        v = dve.tensor_copy(k_dup[br][:, tb, :].rearrange("p (g e n) -> p g e n", g=NKV, e=2),
                                            src[:, tb, 0:NKV * HD].rearrange("p (g e n) -> p g e n", g=NKV, e=1)
                                            .to_broadcast([P, NKV, 2, HD]))
                    v.then_inc(m.kdup, 1)

                z_name, z_at = ("a_kvz", 1) if m.branches == 1 else ("b_z", 0)
                if m.branches == 1:
                    splits("a_kvz", 0, start=HT_NEXT)
                    keys(0)
                else:
                    splits("b_kv", 0, start=HT_NEXT)
                    splits("b_kv", SCPB)
                    keys(0)
                    splits("b_kv", 2 * SCPB)
                    keys(1)
                    splits("b_kv", 3 * SCPB)
                for b in range(2):
                    splits(z_name, SCPB * (b + z_at))
                for br in range(m.branches):
                    dve.wait_ge(m.k_turned, br + 1)
                    dve.tensor_copy(kT_all[br][:, 2:4, :], ps[:, 5, :].rearrange("p (g s) -> p g s", g=2)
                                    ).then_inc(m.kT_dve, 1)
                for b in range(2, 4):
                    splits(z_name, SCPB * (b + z_at), more=b < 3)
                    if m.branches == 2:
                        unfold_blocks(b - 2)
                dve.wait_ge(w_used, block_done(z_name, 3 + z_at))
                for q in range(4):
                    k = slice(4 * q, 4 * q + 4)
                    dve.tensor_tensor(hT[:, k, :], hT_hi[:, k, :].bitcast(F32), hT_lo[:, k, :].bitcast(F32), ALU.add
                                      ).then_inc(hT_whole, 1)

            def unfold_blocks(c):
                pos = vec(("pos_k", "pos_v")[c])
                dve.wait_ge(c_copied, c + 1)
                for a in range(2):
                    for e in range(2):
                        half, k = slice(e * HD, (e + 1) * HD), slice(a * CS // 2, (a + 1) * CS // 2)
                        src = kcT[c][half].rearrange("p g (n k e) -> p g n k e", k=CS // 2, e=2)[:, :, a:a + NCMP, :, e]
                        v = dve.tensor_tensor(unfold[c][half, k], src.rearrange("p g n k -> p k g n"),
                                              pos[half, k].rearrange("p (k g n) -> p k g n", g=1, n=1)
                                              .to_broadcast([HD, CS // 2, NKV, NCMP]), ALU.add)
                v.then_inc(unfolded, 1)

            def compressed():
                dve.wait_ge(cmp_w2, 1)
                dve.tensor_copy(kcmp_all, ps[:, 4, 0:NKV * NCMP])
                dve.wait_ge(cmp_w2, 2)
                dve.tensor_copy(vcmp[0:NCMP, :], ps[0:NCMP, 5, 0:NKV * HD]).then_inc(cmp_kv, 1)
                dve.wait_ge(cmp_kv, 1)
                link(dve.memset(kcmp_grp, 0.0))

            def groups(m):
                name, NU = m.name + "_q", m.units
                is_b = m.branches == 2
                b0 = block_base[name]
                GROUP_STEPS = NU + (2 if not is_b else 13) + 2
                mask = cst("mask_causal" if is_b else "mask_window")
                base, k_at = [0], [0]

                def mark(g):
                    def step(ins):
                        k_at[0] += 1
                        ins.then_inc(dve_step, 1)
                        dve.wait_ge(dve_step, base[0] + GROUP_STEPS * g + k_at[0])
                    return step

                def softmax(g, u, step):
                    h = u % HG
                    dve.wait_ge(m.scores, 1 + NU * g + u + 1)
                    dve.wait_ge(m.pt_done, NU * g + u + 1)
                    take_waits()
                    for tb in range(TB):
                        n = tb * HG + h
                        lo, hi = tb * P, tb * P + (tb + 1) * P
                        v = dve.tensor_tensor_reduce(prob4[u % 4][:, lo:hi], ps[:, 2 + u % 2, lo:hi], mask[:, lo:hi],
                                                     SCALE2, -3e38 if is_b else sink_grp[:, h:h + 1], ALU.add,
                                                     ALU.max, mx2[:, n:n + 1])
                    step(v)
                    dve.tensor_scalar(t8(nmx2)[:, :, h], t8(mx2)[:, :, h], -1.0, None, ALU.mult
                                      ).then_inc(m.max_done, 1)

                def finish(g, read, step):
                    br = read - is_b
                    den = sums2[br]
                    if is_b and read == 0:
                        dve.wait_ge(cmp_pv, g + 1)
                        den = sums2[2]
                    else:
                        dve.wait_ge(m.exp_done, NU * g + HG * (br + 1))
                        dve.wait_ge(m.pv_done, 2 + NU * g + HG * (br + 1))
                    if not is_b:
                        dve.wait_ge(m.sink_exp, g + 1)
                        step(dve.tensor_tensor(den, den, sink_e, ALU.add))
                    step(dve.reciprocal(coef, den))
                    if is_b:
                        step(dve.tensor_tensor(t8(coef), t8(coef), gates[:, :, ds(32 * read + HG * g, HG)], ALU.mult))
                    dst = o_tmp if is_b and read else o_grp
                    v4 = lambda ap: ap.rearrange("p t (h n) -> p t h n", h=HG)
                    o = dve.tensor_tensor(v4(dst), v4(ps[:, 6:8, :]),
                                          coef.rearrange("p (t h n) -> p t h n", t=TB, n=1)
                                          .to_broadcast([P, TB, HG, HD]), ALU.mult)
                    o.then_inc(m.o_read, 1)
                    dve.wait_ge(m.o_read, m.reads * (g + 1) + read + 1)
                    if is_b and read:
                        step(dve.tensor_tensor(o_grp, o_grp, o_tmp, ALU.add))
                    if read == m.reads - 1:
                        dve.tensor_tensor(o_grp, o_grp, z_sb[:, :, ds(g * HW, HW)], ALU.mult).then_inc(m.og_done, 1)

                def rope_q(g, after):
                    dve.wait_ge(proj_free, b0 + g + 1)
                    rotate(q_grp, HG, after).then_inc(m.q_roped, 1)

                def group(g, last=False):
                    k_at[0] = 0
                    step = mark(g)
                    dve.wait_ge(m.scores, NU * g + 1)
                    for br in range(m.branches):
                        v = dve.tensor_copy(kT_grp[br].rearrange("p (g s) -> p g s", g=1), kT_all[br][:, ds(g, 1), :])
                    if is_b:
                        for e in range(2):
                            half = slice(e * HD, (e + 1) * HD)
                            v = dve.tensor_copy(kcmp_grp[half, e * NCMP:(e + 1) * NCMP],
                                                kcmp_all[half, ds(g * NCMP, NCMP)])
                    else:
                        v = dve.tensor_copy(sink_grp, sinks[:, ds(g * HG, HG)])
                    v.then_inc(m.k_ready, 1)
                    dve.wait_ge(m.k_ready, g + 1)
                    dve.wait_ge(m.turned, 2 * g + 2)
                    dve.tensor_copy(qT_grp[:, 2:4, :], ps[:, 5, :].rearrange("p (j s) -> p j s", j=2)
                                    ).then_inc(m.qT_dve, 1)
                    if is_b:
                        pc = p_cmp.rearrange("p (t h n) -> p t h n", t=TB, h=HG)
                        cm = sums2[2]
                        dve.wait_ge(cmp_scores, g + 1)
                        v = dve.tensor_tensor(pc, ps[:, 6, 0:TB * HG * NCMP].rearrange("p (t h n) -> p t h n", t=TB, h=HG),
                                              cst("mask_cmp").rearrange("p (t h n) -> p t h n", t=TB, h=1)
                                              .to_broadcast([P, TB, HG, NCMP]), ALU.add)
                        step(v)
                        step(dve.tensor_reduce(cm, p_cmp.rearrange("p (m n) -> p m n", n=NCMP), AX, ALU.max))
                        step(dve.tensor_scalar(cm, cm, NEG / 100, None, ALU.max))
                        dve.tensor_tensor(pc, pc, cm.rearrange("p (t h n) -> p t h n", t=TB, n=1)
                                          .to_broadcast([P, TB, HG, NCMP]), ALU.subtract).then_inc(cmp_shifted, 1)
                        dve.tensor_tensor(v_bd[0:HG * NCMP].rearrange("p (h n) -> p h n", h=HG),
                                          ps[0:HG * NCMP, 6, 256:256 + HD].rearrange("p (h n) -> p h n", h=1)
                                          .to_broadcast([HG * NCMP, HG, HD]),
                                          cst("mask_bd")[0:HG * NCMP].rearrange("p (h n) -> p h n", h=HG),
                                          ALU.mult).then_inc(vbd_done, 1)
                    softmax(g, 0, step)
                    softmax(g, 1, step)
                    if is_b:
                        dve.wait_ge(cmp_exp, g + 1)
                        step(dve.tensor_reduce(cm, p_cmp.rearrange("p (m n) -> p m n", n=NCMP), AX, ALU.add))
                        step(dve.tensor_scalar(cm, cm, 1e-30, None, ALU.max))
                        finish(g, 0, step)
                    for u in range(NU):
                        if u % 2:
                            dve.wait_ge(m.pt_done, 4 + NU * g + u + 1)
                            dve.wait_ge(m.pv_done, NU * g + u + 1)
                            dve.tensor_copy(probT2[1], ps[:, 5, 0:SCW]).then_inc(m.ptc_dve, 1)
                        if u + 2 < NU:
                            softmax(g, u + 2, step)
                        if is_b and u == HG:
                            finish(g, 1, step)
                    if not is_b:
                        dve.wait_ge(m.max_done, 2 + NU * (g + 1))
                        dve.tensor_tensor(t8(sink_e), t8(nmx2), sink_grp.rearrange("p (t h) -> p t h", t=1)
                                          .to_broadcast([P, TB, HG]), ALU.add).then_inc(m.sink_in, 1)
                    if not last:
                        rope_q(g + 1, step)
                    finish(g, m.reads - 1, step)
                    for bank in range(2):
                        dve.wait_ge(m.ogc_up, 2 * g + bank + 1)
                        k = ds(4 * g + 2 * bank, 2)
                        v = dve.tensor_tensor(oT_mix[1][:, k, :], ps[:, 4 + bank, :].rearrange("p (j s) -> p j s", j=2),
                                              oT_mix[0][:, k, :].bitcast(F32), ALU.subtract)
                    v.then_inc(m.ogc_done, 1)
                    while k_at[0] < GROUP_STEPS:
                        k_at[0] += 1
                        dve.sem_inc(dve_step, 1)

                for what, n in ((m.max_done, 2), (m.pt_done, 4), (m.pv_done, 2), (m.ptc_dve, 1), (m.scores, 1),
                                (m.ogc_done, 1), (m.o_read, m.reads), (m.og_done, 1)):
                    dve.sem_inc(what, n)
                rope_q(0, None)
                if is_b:
                    compressed()
                base[0] = steps[0]
                with dve.Fori(0, NKV - 1) as g:
                    group(g)
                for j in range(LEAD):
                    split_chunk(f"{m.name}_out", 0, j)
                group(NKV - 1, last=True)
                steps[0] += GROUP_STEPS * NKV

            def residual(m):
                name = f"{m.name}_out"
                for b in range(4):
                    splits(name, SCPB * b, more=b < 3 or more_after.get(name, False))
                    dve.wait_ge(w_used, block_done(name, b))
                    blk = x_sb[:, :, b * NB:(b + 1) * NB]
                    v = dve.tensor_tensor(blk, blk, ps[:, 2 * (b % 2):2 * (b % 2) + 2, :], ALU.add)
                    v.then_inc(proj_free, 1)

            for m, idx in ((ma, 2), (mb, 3)):
                if m is not None:
                    hT_copies(idx, ("a_kvz", "b_kv")[idx - 2])
                    if idx == 2:
                        rotation_angles()
                    kvz(m)
                    groups(m)
                    residual(m)
                    if stages > idx + 1:
                        norm_x(idx + 1, EPS2, final=(idx == 3))


INPUTS = ("x", "ada_w", "ada_b", "post_g", "sgu_w_in", "sgu_norm_g", "sgu_w_out", "mla_w_in", "mla_w_uq",
          "mla_w_ukv", "mla_w_out", "final_norm_w_2", "a_w_in_2", "a_sinks_2", "a_w_out_2",
          "b_w_in_2", "b_cmp_k_w1_2", "b_cmp_k_w2_2", "b_cmp_v_w1_2",
          "b_cmp_v_w2_2", "b_w_out_2")


def kernel(**inputs):
    import concourse.bacc as bacc
    from concourse.bass_utils import run_bass_kernel_spmd

    nc = bacc.Bacc("TRN2", target_bir_lowering=False, num_devices=1)
    arrays = {n: np.ascontiguousarray(inputs[n]) for n in INPUTS}
    a = {n: np.asarray(v) for n, v in inputs.items()}

    def columns(v, rows=P):
        out = np.zeros((P, v.size // rows), np.float32)
        out[:rows] = v.reshape(-1, rows).T
        return out

    def positions(v):
        return v.reshape(CL // 2, 2, HD).transpose(1, 2, 0).reshape(P, CL // 2)

    vecs = {"c": columns(a["c"][0]), "pre_g0": columns(a["pre_g"][0]), "pre_g1": columns(a["pre_g"][1]),
            "norm_w0": columns(a["norm_w_2"][0]), "norm_w1": columns(a["norm_w_2"][1]),
            "q_g": columns(a["mla_q_norm_g"][0], QL_P), "kv_g": columns(a["mla_kv_norm_g"][0]),
            "b_s": a["sgu_b_s"][0].T,
            "pos_k": positions(a["b_cmp_k_pos_2"][0]), "pos_v": positions(a["b_cmp_v_pos_2"][0])}
    arrays["vecs"] = np.ascontiguousarray(np.concatenate([vecs[n] for n in VEC_COLS], 1))
    arrays["w_s"] = np.ascontiguousarray(a["sgu_w_s"][0].transpose(2, 0, 1).reshape(P, -1))
    arrays["consts"] = shape_constants()
    arrays["pos"] = np.ascontiguousarray(a["positions_2"].reshape(TB, P).T)
    T = {n: nc.dram_tensor(n, v.shape, mybir.dt.from_np(v.dtype), kind="ExternalInput").ap()
         for n, v in arrays.items()}
    T["out"] = nc.dram_tensor("out", (1, S, D), F32, kind="ExternalOutput").ap()
    build(nc, T)
    r = run_bass_kernel_spmd(nc, [arrays], core_ids=[0])
    return r.results[0]["out"]
```
